# Optimizing a Trainium2 kernel written in Bass

```python
import jax
import jax.numpy as jnp
from jax import lax
import numpy as np

D_MODEL = 1024
BATCH = 1
SEQ = 1024
DEPTH = 1
DEC_BATCH = 8
DEC_SEQ = 1
PAST_LEN = 1024
PAGE_SIZE = 128

HEAD_DIM = 64
H_A = 8
KV_A = 2
G_A = H_A // KV_A
H_B = 8
WINDOW_A = 128
DILATIONS = ((128, 1), (512, 4), (2048, 16))
WINDOW_B = 2048
BLOCK = 128
BAND = 128
ROT_DIM = HEAD_DIM // 4
ROPE_THETA = 500000.0
Q_A = H_A * HEAD_DIM
K_A = KV_A * HEAD_DIM
Q_B = H_B * HEAD_DIM
D_MIX = Q_A + Q_B
D_IN = Q_A + 2 * K_A + 3 * Q_B
SPLITS = (Q_A, Q_A + K_A, Q_A + 2 * K_A, Q_A + 2 * K_A + Q_B, Q_A + 2 * K_A + 2 * Q_B)
PEER_HEADS = 8
PEER_QDIM = 256
N_KEYS = 128
N_EXPERTS = N_KEYS * N_KEYS
PEER_TOPK = 16
PEER_CHUNK = 128
EPS = 1e-6

kernel_name = 'hymba_swa_sink_dilated_peer_step'

def rms_norm(x, g):
    xf = x.astype(jnp.float32)
    r = xf * lax.rsqrt(jnp.mean(xf * xf, axis=-1, keepdims=True) + EPS)
    return (r * g.astype(jnp.float32)).astype(x.dtype)

def rope(x, pos):
    inv = ROPE_THETA ** (-jnp.arange(0, ROT_DIM, 2, dtype=jnp.float32) / ROT_DIM)
    ang = pos.astype(jnp.float32)[:, None] * inv[None, :]
    cos, sin = jnp.cos(ang)[:, None, :], jnp.sin(ang)[:, None, :]
    xr = x[..., :ROT_DIM].astype(jnp.float32)
    x1, x2 = xr[..., :ROT_DIM // 2], xr[..., ROT_DIM // 2:]
    rot = jnp.concatenate([x1 * cos - x2 * sin, x2 * cos + x1 * sin], axis=-1)
    return jnp.concatenate([rot.astype(x.dtype), x[..., ROT_DIM:]], axis=-1)

def project(x, pos, norm_g, w_in):
    B, T, _ = x.shape
    z = rms_norm(x, norm_g) @ w_in
    q_a, k_a, v_a, q_b, k_b, v_b = jnp.split(z, SPLITS, axis=-1)
    heads = lambda t, h: t.reshape(B, T, h, HEAD_DIM)
    q_a = rope(heads(q_a, H_A), pos).reshape(B, T, KV_A, G_A, HEAD_DIM)
    k_a = rope(heads(k_a, KV_A), pos)
    v_a = heads(v_a, KV_A)
    q_b = rope(heads(q_b, H_B), pos)
    k_b = rope(heads(k_b, H_B), pos)
    v_b = heads(v_b, H_B)
    return q_a, k_a, v_a, q_b, k_b, v_b

def banded_attention(q, k, v, sink):
    N, L, Hkv, G, D = q.shape
    nb = L // BLOCK
    qb = q.reshape(N, nb, BLOCK, Hkv, G, D)
    kb = k.reshape(N, nb, BLOCK, Hkv, D)
    vb = v.reshape(N, nb, BLOCK, Hkv, D)
    shift = lambda t: jnp.concatenate([jnp.zeros_like(t[:, :1]), t[:, :-1]], axis=1)
    kk = jnp.concatenate([shift(kb), kb], axis=2)
    vv = jnp.concatenate([shift(vb), vb], axis=2)
    s = jnp.einsum('nbqhgd,nbkhd->nbhgqk', qb, kk).astype(jnp.float32) * (D ** -0.5)
    qi = jnp.arange(BLOCK) + BLOCK
    ki = jnp.arange(2 * BLOCK)
    dist = qi[:, None] - ki[None, :]
    band = (dist >= 0) & (dist <= BAND)
    has_prev = (jnp.arange(nb)[:, None, None] > 0) | (ki[None, None, :] >= BLOCK)
    mask = band[None] & has_prev
    s = jnp.where(mask[None, :, None, None], s, -jnp.inf)
    lse = jax.nn.logsumexp(s, axis=-1)
    if sink is not None:
        lse = jnp.logaddexp(lse, sink.astype(jnp.float32)[:, :, None])
    p = jnp.exp(s - lse[..., None])
    o = jnp.einsum('nbhgqk,nbkhd->nbqhgd', p.astype(vv.dtype), vv)
    lse = lse.transpose(0, 1, 4, 2, 3).reshape(N, L, Hkv, G)
    return o.reshape(N, L, Hkv, G, D), lse

def dilated_branch_prompt(q, k, v, d):
    B, T, H, D = q.shape
    span = d * BLOCK
    Tp = -(-T // span) * span
    def sub(t):
        t = jnp.pad(t, ((0, 0), (0, Tp - T), (0, 0), (0, 0)))
        return t.reshape(B, Tp // d, d, H, D).transpose(0, 2, 1, 3, 4).reshape(B * d, Tp // d, H, D)
    o, lse = banded_attention(sub(q)[:, :, :, None], sub(k), sub(v), None)
    o = o[:, :, :, 0].reshape(B, d, Tp // d, H, D).transpose(0, 2, 1, 3, 4).reshape(B, Tp, H, D)[:, :T]
    lse = lse[..., 0].reshape(B, d, Tp // d, H).transpose(0, 2, 1, 3).reshape(B, Tp, H)[:, :T]
    return o, lse

def window_indices(L, S, w, d):
    n = w // d + 1
    idx = L + jnp.arange(S)[:, None] - d * jnp.arange(n)[None, :]
    return jnp.clip(idx, 0, None), idx >= 0

def gathered_attention(q, kv, idx, valid, sink):
    kv_g = kv[:, idx]
    s = jnp.einsum('nshgd,nskhd->nshgk', q, kv_g[:, :, :, 0]).astype(jnp.float32) * (HEAD_DIM ** -0.5)
    s = jnp.where(valid[None, :, None, None, :], s, -jnp.inf)
    lse = jax.nn.logsumexp(s, axis=-1)
    if sink is not None:
        lse = jnp.logaddexp(lse, sink.astype(jnp.float32))
    p = jnp.exp(s - lse[..., None])
    o = jnp.einsum('nshgk,nskhd->nshgd', p.astype(kv.dtype), kv_g[:, :, :, 1])
    return o, lse

def combine_dilations(branches):
    outs = jnp.stack([o for o, _ in branches])
    w = jax.nn.softmax(jnp.stack([s for _, s in branches]), axis=0)
    return jnp.sum(w[..., None].astype(outs.dtype) * outs, axis=0)

def mix_out(x, o_a, o_b, g_a, g_b, w_out):
    B, T = x.shape[:2]
    o = jnp.concatenate([rms_norm(o_a.reshape(B, T, Q_A), g_a), rms_norm(o_b.reshape(B, T, Q_B), g_b)], axis=-1)
    return x + o @ w_out

def peer_ffn(h, w_q, sub_keys, u, v):
    N = h.shape[0]
    nc = -(-N // PEER_CHUNK)
    hp = jnp.pad(h, ((0, nc * PEER_CHUNK - N), (0, 0))).reshape(nc, PEER_CHUNK, D_MODEL)
    def block(hc):
        q = (hc @ w_q).reshape(PEER_CHUNK, PEER_HEADS, 2, PEER_QDIM // 2)
        sc = jnp.einsum('chpd,hpkd->chpk', q, sub_keys).astype(jnp.float32)
        s1, i1 = lax.top_k(sc[:, :, 0], PEER_TOPK)
        s2, i2 = lax.top_k(sc[:, :, 1], PEER_TOPK)
        cand = (s1[..., :, None] + s2[..., None, :]).reshape(PEER_CHUNK, PEER_HEADS, PEER_TOPK * PEER_TOPK)
        cid = (i1[..., :, None] * N_KEYS + i2[..., None, :]).reshape(PEER_CHUNK, PEER_HEADS, PEER_TOPK * PEER_TOPK)
        top_s, pos = lax.top_k(cand, PEER_TOPK)
        eid = jnp.take_along_axis(cid, pos, axis=-1)
        gate = jax.nn.softmax(top_s, axis=-1)
        act = jax.nn.gelu(jnp.einsum('cd,chkd->chk', hc, u[eid]).astype(jnp.float32))
        return jnp.einsum('chk,chkd->cd', (gate * act).astype(v.dtype), v[eid])
    return lax.map(block, hp).reshape(nc * PEER_CHUNK, D_MODEL)[:N]

def setup_inputs(seed: int = 0) -> dict:
    key = jax.random.key(seed)
    ks = jax.random.split(key, 17)
    nrm = lambda k, shape, scale: scale * jax.random.normal(k, shape, jnp.float32)
    w_a_buf = min(WINDOW_A, PAST_LEN)
    w_b_buf = min(WINDOW_B, PAST_LEN)
    return {
        'x_prompt': nrm(ks[0], (BATCH, SEQ, D_MODEL), 1.0),
        'x_sample': nrm(ks[1], (DEC_BATCH, DEC_SEQ, D_MODEL), 1.0),
        'cache_swa_kv': nrm(ks[2], (DEPTH, DEC_BATCH, w_a_buf, 2, KV_A, HEAD_DIM), 1.0),
        'cache_dil_kv': nrm(ks[3], (DEPTH, DEC_BATCH, w_b_buf, 2, H_B, HEAD_DIM), 1.0),
        'attn_norm': 1.0 + nrm(ks[4], (DEPTH, D_MODEL), 0.02),
        'w_in': nrm(ks[5], (DEPTH, D_MODEL, D_IN), D_MODEL ** -0.5),
        'sinks': nrm(ks[6], (DEPTH, H_A), 0.5),
        'out_norm_a': 1.0 + nrm(ks[7], (DEPTH, Q_A), 0.02),
        'out_norm_b': 1.0 + nrm(ks[8], (DEPTH, Q_B), 0.02),
        'w_out': nrm(ks[9], (DEPTH, D_MIX, D_MODEL), D_MIX ** -0.5),
        'ffn_norm': 1.0 + nrm(ks[10], (DEPTH, D_MODEL), 0.02),
        'peer_w_q': nrm(ks[11], (DEPTH, D_MODEL, PEER_HEADS * PEER_QDIM), D_MODEL ** -0.5),
        'peer_sub_keys': nrm(ks[12], (DEPTH, PEER_HEADS, 2, N_KEYS, PEER_QDIM // 2), (PEER_QDIM // 2) ** -0.5),
        'peer_u': nrm(ks[13], (DEPTH, N_EXPERTS, D_MODEL), D_MODEL ** -0.5),
        'peer_v': nrm(ks[14], (DEPTH, N_EXPERTS, D_MODEL), PEER_HEADS ** -0.5),
        'final_norm': 1.0 + nrm(ks[15], (D_MODEL,), 0.02),
    }

def reference(x_prompt, x_sample, cache_swa_kv, cache_dil_kv, attn_norm, w_in, sinks, out_norm_a, out_norm_b,
              w_out, ffn_norm, peer_w_q, peer_sub_keys, peer_u, peer_v, final_norm):
    T = x_prompt.shape[1]
    S = x_sample.shape[1]
    L_A = cache_swa_kv.shape[2]
    L_B = cache_dil_kv.shape[2]
    pos_p = jnp.arange(T)
    pos_s = PAST_LEN + jnp.arange(S)
    xp, xs = x_prompt, x_sample
    swa_p, dil_p, swa_s, dil_s = [], [], [], []
    for l in range(DEPTH):
        sink_l = sinks[l].reshape(KV_A, G_A)
        q_a, k_a, v_a, q_b, k_b, v_b = project(xp, pos_p, attn_norm[l], w_in[l])
        o_a, _ = banded_attention(q_a, k_a, v_a, sink_l)
        o_b = combine_dilations([dilated_branch_prompt(q_b, k_b, v_b, d) for _, d in DILATIONS])
        xp = mix_out(xp, o_a, o_b, out_norm_a[l], out_norm_b[l], w_out[l])
        xp = xp + peer_ffn(rms_norm(xp, ffn_norm[l]).reshape(-1, D_MODEL), peer_w_q[l], peer_sub_keys[l],
                           peer_u[l], peer_v[l]).reshape(xp.shape)
        swa_p.append(jnp.stack([k_a, v_a], axis=2)[:, T - min(WINDOW_A, T):])
        dil_p.append(jnp.stack([k_b, v_b], axis=2)[:, T - min(WINDOW_B, T):])
        q_a, k_a, v_a, q_b, k_b, v_b = project(xs, pos_s, attn_norm[l], w_in[l])
        kv_a = jnp.concatenate([cache_swa_kv[l], jnp.stack([k_a, v_a], axis=2)], axis=1)
        idx_a, val_a = window_indices(L_A, S, WINDOW_A, 1)
        o_a, _ = gathered_attention(q_a, kv_a, idx_a, val_a, sink_l)
        kv_b = jnp.concatenate([cache_dil_kv[l], jnp.stack([k_b, v_b], axis=2)], axis=1)
        branches = []
        for w, d in DILATIONS:
            idx_b, val_b = window_indices(L_B, S, w, d)
            o, lse = gathered_attention(q_b[:, :, :, None], kv_b, idx_b, val_b, None)
            branches.append((o[:, :, :, 0], lse[..., 0]))
        o_b = combine_dilations(branches)
        xs = mix_out(xs, o_a, o_b, out_norm_a[l], out_norm_b[l], w_out[l])
        xs = xs + peer_ffn(rms_norm(xs, ffn_norm[l]).reshape(-1, D_MODEL), peer_w_q[l], peer_sub_keys[l],
                           peer_u[l], peer_v[l]).reshape(xs.shape)
        swa_s.append(kv_a[:, S:])
        dil_s.append(kv_b[:, S:])
    y_prompt = rms_norm(xp, final_norm)
    y_sample = rms_norm(xs, final_norm)
    return (y_prompt, y_sample, jnp.stack(swa_p), jnp.stack(dil_p), jnp.stack(swa_s), jnp.stack(dil_s))


_drawn_inputs = setup_inputs


def setup_inputs(seed=0):
    import zlib

    import numpy as np

    out = dict(_drawn_inputs(seed))
    spreads = {}
    factors = {'sinks': 6.324,
     'out_norm_a': 10.429,
     'out_norm_b': 10.375,
     'ffn_norm': 10.481,
     'final_norm': 8.112}
    for name, (base, spread) in spreads.items():
        noise = np.random.default_rng([zlib.crc32(name.encode()), seed]).standard_normal(out[name].shape)
        drawn = base * np.exp(spread * noise) if base else spread * noise
        out[name] = jnp.asarray(drawn.astype(out[name].dtype))
    for name, factor in factors.items():
        out[name] = (out[name] * factor).astype(out[name].dtype)
    return out
```

```python
from contextlib import ExitStack

import concourse.bass as bass
from concourse import mybir

F32 = mybir.dt.float32
BF16 = mybir.dt.bfloat16
U32 = mybir.dt.uint32
I32 = mybir.dt.int32
ALU = mybir.AluOpType
ACT = mybir.ActivationFunctionType
AX_X = mybir.AxisListType.X

P = 128
D = 1024
NT = 8
ROWS = (NT + 1) * P
NS = 8
KD = D // P
HD = 64
D_IN = 2304
HEADS = 8
KEYS = 128
TOPK = 16
N_EXP = KEYS * KEYS
EPS = 1e-6
NEG = -3.0e38
GELU_C = 0.7978845608028654
QA, KVA, QB, KB, VB_, END = 0, 512, 768, 1280, 1792, 2304
CHUNKS = ((QA, 512), (KVA, 256), (QB, 512), (KB, 512), (VB_, 512))
RING = 4
WO_SLOTS = 2
MAGIC = float(0x5F3759DF)


def build(nc, x_all, cache_swa, cache_dil, w_in, sinks, w_out, w_q, keys, peer_u, peer_v,
          ident, gain_cols, gain_rows, rope_cs, mask_b, mask_a, mask_sb, mask_sa, iota16, eye8, head_mask,
          y_p, y_s, swa_p, dil_p, swa_s, dil_s):
    ds = bass.ds
    with ExitStack() as ctx:
        def sb(name, shape, dt=F32):
            return ctx.enter_context(nc.sbuf_tensor(name, shape, dt))

        def pb(name, shape):
            return ctx.enter_context(nc.psum_tensor(name, shape, F32))

        producers, starts, names, kept = {}, {}, {}, []

        def sem(name, producer=None, start=1):
            s = ctx.enter_context(nc.semaphore(name))
            if producer:
                producers.setdefault(producer, []).append((s, start))
                starts[name] = start
                names[id(s)] = name
                kept.append(s)
            return s

        def after(s, n):
            return n + starts.get(names.get(id(s)), 0)

        def scratch(name, shape):
            return nc.dram_tensor(name, shape, F32, kind="Internal").ap()

        qT_scr = scratch("qT_scr", (8, P, ROWS))
        kTA_scr = scratch("kTA_scr", (P, ROWS))
        kvA_scr = scratch("kvA_scr", (ROWS, 256))
        zS_scr = scratch("zS_scr", (NS, D_IN))
        oS_scr = scratch("oS_scr", (NS, D))

        wbuf = sb("wbuf", [P, KD * D_IN])
        w_in_sb = wbuf[:, :].rearrange("p (k n) -> p k n", k=KD)
        wq_sb = wbuf[:, 0:KD * 2048].rearrange("p (k n) -> p k n", k=KD)
        keysT = wbuf[:, KD * 2048:].rearrange("p (h k) -> p h k", h=2 * HEADS)
        KTB = sb("KTB", [P, 4, D])
        VB = sb("VB", [P, NT, 512])
        ring = sb("ring", [P, 2 * RING, D])
        u_ring = [ring[:, i, :] for i in range(RING)]
        v_ring = [ring[:, RING + i, :] for i in range(RING)]
        hpair = sb("hpair", [P, 2, D])
        h_cur, h_next = hpair[:, 0, :], hpair[:, 1, :]
        x2 = sb("x2", [P, D])
        o_all = sb("o_all", [P, D])
        TT = sb("TT", [P, KD, P])
        S = sb("S", [P, D + 256])
        S_B, S_A = S[:, 0:D], S[:, D:D + 256]
        PT = sb("PT", [P, 10, P])
        maskB = sb("maskB", [P, D])
        maskA = sb("maskA", [P, 2, 256])
        wo_sb = sb("wo_sb", [P, WO_SLOTS, D])
        ybuf = sb("ybuf", [P, D])
        idn = sb("idn", [P, P])
        diag = sb("diag", [P, 4, P])
        qpad = sb("qpad", [P, 2, 2, P])
        kTA = sb("kTA", [P, 256])
        vA = sb("vA", [P, 2, P])
        gcol = sb("gcol", [P, 2, KD])
        grow = sb("grow", [KD, 2, P])
        rcs = sb("rcs", [P, NT + 1, 16])
        sink = sb("sink", [P, HEADS])
        iota = sb("iota", [P, TOPK])
        e8 = sb("e8", [P, 8, 8])
        pq = sb("pq", [P, 256])
        pqT = sb("pqT", [P, 2, P])
        sc = sb("sc", [P, 2, P])
        topv = sb("topv", [P, 2, 2, TOPK])
        topi = sb("topi", [P, 2, 2, TOPK], U32)
        topif = sb("topif", [P, 2, 2, TOPK])
        cand = sb("cand", [P, TOPK, TOPK])
        candv = sb("candv", [P, 2, TOPK])
        candp = sb("candp", [P, 2, TOPK], U32)
        candh = sb("candh", [P, 2, TOPK], U32)
        candf = sb("candf", [P, 2, TOPK])
        onehot = sb("onehot", [P, 2, TOPK, TOPK])
        sel = sb("sel", [P, 2, 2, TOPK])
        gexp = sb("gexp", [P, TOPK])
        idx_all = sb("idx_all", [P, P], U32)
        gates = sb("gates", [P, P])
        win_u = sb("win_u", [P, 2, TOPK], U32)
        win_v = sb("win_v", [P, 2, TOPK], U32)
        dots = sb("dots", [P, 2, TOPK])
        gl = sb("gl", [P, 3, TOPK])
        wv = sb("wv", [P, 2, TOPK])
        nw_x = sb("nw_x", [P, 2])
        nw_i = sb("nw_i", [P, 2], I32)
        nw_a = sb("nw_a", [P, 2])
        nw_b = sb("nw_b", [P, 2])
        nw_y = sb("nw_y", [P, 2])
        ssum = sb("ssum", [P, 2])
        amax = sb("amax", [P, 2])
        anm = sb("anm", [P, 2])
        aden = sb("aden", [P, 3])
        arden = sb("arden", [P, 2])
        gsm = sb("gsm", [P, 4])
        idxT = sb("idxT", [P, NS], U32)
        gateT = sb("gateT", [P, NS])
        dotsT = sb("dotsT", [P, NS])
        wz = sb("wz", [P, NS, 8])

        xin = ring[:, 0, :]
        xs = ring[:, 1, :]
        z = ring[:, 2:5, :].rearrange("p a n -> p (a n)")[:, 0:D_IN]
        rtmp = ring[:, 5, :]
        qTe = ring[:, 6, :].rearrange("p (b n) -> p b n", b=8)
        kTAe = ring[:, 7, 0:P]
        s_k = [ring[:, i, :].rearrange("p (s n) -> p s n", s=2) for i in range(2)]
        s_q = [ring[:, 2 + i, :] for i in range(2)]
        s_kA = [ring[:, 4, i * P:(i + 1) * P] for i in range(2)]
        s_v = [ring[:, 5 + i, :].rearrange("p (s n) -> p s n", s=2) for i in range(2)]
        s_vA = [ring[:, 7, i * P:(i + 1) * P] for i in range(2)]
        s_new = PT[:, :, :].rearrange("p a n -> p (a n)")
        s_prod = TT[:, :, :].rearrange("p a n -> p (a n)")
        s_sc = S[:, 0:192].rearrange("p (s n) -> p s n", s=3)
        s_scn = S[:, 192:320].rearrange("p (s n) -> p s n", s=2)
        s_pB, s_pA = S[:, 320:584], S[:, 584:720]
        s_pT = S[:, 720:912].rearrange("p (s n) -> p s n", s=3)
        s_pTn = S[:, 912:1040].rearrange("p (s n) -> p s n", s=2)
        s_mB, s_mA = maskB[0:64, 0:264], maskB[0:64, 264:400]
        s_hm = maskB[0:8, 512:1024]
        s_sink = gsm[0:64, 3:4]
        s_od = [ybuf[0:8, :], x2[0:8, :]]
        s_o = o_all[0:8, :]

        acc = pb("acc", [P, D])
        pS = pb("pS", [P, D])
        pA = pb("pA", [P, 512])
        pT = pb("pT", [P, D])
        pM = pb("pM", [P, 512])
        zbank = (pS[:, 0:512], pS[:, 512:768], pA[:, :], pT[:, 0:512], pT[:, 512:1024])

        c_in = sem("c_in")
        win_in = [sem(f"win_in{i}") for i in range(5)]
        x_in = sem("x_in")
        z_out = sem("z_out", "sp")
        q_out = sem("q_out", "sp")
        cache_out = sem("cache_out")
        wq_in = sem("wq_in")
        keys_in = sem("keys_in")
        snew_in = sem("snew_in")
        sconst_in = sem("sconst_in")
        sk_in = [sem(f"sk_in{i}") for i in range(2)]
        sv_in = [sem(f"sv_in{i}") for i in range(2)]
        so_out = sem("so_out")
        so_in = sem("so_in")
        newrow_out = sem("newrow_out")
        att_in = sem("att_in")
        qT_in = [sem(f"qT_in{i}") for i in range(2)]
        mx_in = sem("mx_in")
        wo_in = [sem(f"wo_in{i}") for i in range(WO_SLOTS)]
        y_out = sem("y_out", "sp")
        u_in = [sem(f"u_in{i}") for i in range(RING)]
        v_in = [sem(f"v_in{i}") for i in range(RING)]
        swa_out = sem("swa_out")

        a_xs = sem("a_xs", "dve")
        a_xT = sem("a_xT", "dve")
        a_rope = sem("a_rope", "dve")
        a_xt = sem("a_xt", "pe")
        a_z = sem("a_z", "pe")
        a_rt = sem("a_rt", "pe")
        a_ze = sem("a_ze", "act")
        a_te = sem("a_te", "act")
        a_vb = sem("a_vb", "pool")
        pads = sem("pads", "dve")
        k_t = sem("k_t", "pe")
        k_te = sem("k_te", "act")
        s_mul = sem("s_mul", "dve", 2)
        s_sT = sem("s_sT", "pe")
        s_max = sem("s_max", "dve")
        s_exp = sem("s_exp", "act")
        s_prob = sem("s_prob", "dve")
        s_bT = sem("s_bT", "pe")
        s_bTe = sem("s_bTe", "act")
        s_pv = sem("s_pv", "pe")
        s_dg = sem("s_dg", "dve")
        s_fold = sem("s_fold", "pe")
        s_done = sem("s_done", "dve")
        att_s = sem("att_s", "pe", 2)
        att_max = sem("att_max", "dve")
        att_exp = sem("att_exp", "act")
        att_t = sem("att_t", "pe")
        att_te = sem("att_te", "act")
        att_pv = sem("att_pv", "pe")
        att_o = sem("att_o", "dve")
        mx_on = sem("mx_on", "dve")
        mx_t = sem("mx_t", "pe")
        mx_onT = sem("mx_onT", "dve")
        wo_used = sem("wo_used", "pe", WO_SLOTS)
        mx_mm = sem("mx_mm", "pe")
        mx_h = sem("mx_h", "dve")
        mx_ht = sem("mx_ht", "pe")
        mx_hT = sem("mx_hT", "act")
        pr_q = sem("pr_q", "pe")
        pr_qe = sem("pr_qe", "act")
        pr_t = sem("pr_t", "pe")
        pr_te = sem("pr_te", "act")
        pr_s = sem("pr_s", "pe")
        pr_se = sem("pr_se", "act")
        pr_top = sem("pr_top", "dve")
        pr_exp = sem("pr_exp", "act")
        pr_idx = sem("pr_idx", "dve")
        win_set = sem("win_set", "pool")
        win_cp = sem("win_cp", "pool")
        gl_in = sem("gl_in", "dve")
        gl_th = sem("gl_th", "act")
        w_set = sem("w_set", "dve")
        diag_set = sem("diag_set", "act")
        u_used = sem("u_used", "dve", RING)
        v_used = sem("v_used", "pe", RING)
        acc_init = sem("acc_init", "pe")
        fin_g = sem("fin_g", "pe")
        fin_y = sem("fin_y", "dve")
        fin_free = sem("fin_free", "dve")
        gs_t = sem("gs_t", "pe")
        gs_idx = sem("gs_idx", "dve")
        gs_h = sem("gs_h", "pe")
        gs_in = sem("gs_in", "dve")
        gs_th = sem("gs_th", "act")
        gs_w = sem("gs_w", "dve")
        gs_acc = sem("gs_acc", "pe")

        steps = {who: ctx.enter_context(nc.semaphore(f"{who}_step")) for who in ("sp", "pool", "dve")}

        def hold(eng, who, s, n):
            eng.wait_ge(s, after(s, n))
            eng.sem_inc(steps[who], 1)

        def set_starts(eng, who):
            for s, start in producers[who]:
                eng.sem_inc(s, start)

        def repeat(eng, start, end):
            return eng.Fori(start, end)

        block = ctx.enter_context(nc.Block())

        @block.sync
        def _(sp):
            set_starts(sp, "sp")
            sp.dma_start(xin, x_all[0:P, :]).then_inc(x_in, 16)
            consts = [(idn[:, :], ident), (gcol[:, :, :], gain_cols), (grow[:, :, :], gain_rows),
                      (rcs[:, :, :], rope_cs.rearrange("(t p) c -> p t c", p=P)), (maskA[:, :, :], mask_a),
                      (sink[:, :], sinks.broadcast_to([P, HEADS])), (iota[:, :], iota16), (e8[:, :, :], eye8)]
            for dst, src in consts:
                sp.dma_start(dst, src).then_inc(c_in, 16)
            w_in_v = w_in.rearrange("(k p) n -> p k n", p=P)
            for n, (c0, w) in enumerate(CHUNKS):
                sp.dma_start(w_in_sb[:, :, c0:c0 + w], w_in_v[:, :, c0:c0 + w]).then_inc(win_in[n], 16)

            def cache_copy(r):
                n = 1023 * D
                src = cache_dil[ds(r, 1)].rearrange("r s n -> r (s n)")[:, D:D + n]
                dst = dil_s[ds(r, 1)].rearrange("r s n -> r (s n)")[:, 0:n]
                sp.dma_start(dst.rearrange("r (a b) -> (r a) b", a=176),
                             src.rearrange("r (a b) -> (r a) b", a=176)).then_inc(cache_out, 16)

            with repeat(sp, 0, NT) as t:
                hold(sp, "sp", a_xs, t + 1)
                sp.dma_start(xin, x_all[ds((t + 1) * P, P), :]).then_inc(x_in, 16)
                cache_copy(t)
                hold(sp, "sp", a_ze, 5 * t + 5)
                hold(sp, "sp", a_rope, 2 * t + 2)
                sp.dma_start(dil_p[ds(t * P, P), :], z[:, KB:END]).then_inc(z_out, 16)
                sp.dma_start(kvA_scr[ds(t * P, P), :], z[:, KVA:QB]).then_inc(z_out, 16)
                hold(sp, "sp", a_te, 4 * t + 4)
                sp.dma_start(qT_scr[:, :, ds(t * P, P)].rearrange("b p n -> p b n"), qTe).then_inc(q_out, 16)
                sp.dma_start(kTA_scr[:, ds(t * P, P)], kTAe).then_inc(q_out, 16)
            sp.dma_start(swa_s[:, 0:127 * 256].rearrange("r (a b) -> r a b", a=16),
                         cache_swa[:, 256:].rearrange("r (a b) -> r a b", a=16)).then_inc(cache_out, 16)
            hold(sp, "sp", a_ze, 5 * NT + 5)
            hold(sp, "sp", a_rope, 2 * NT + 2)
            sp.dma_start(zS_scr, z[0:NS, :]).then_inc(z_out, 16)
            sp.dma_start(dil_s[:, 1023, :], z[0:NS, KB:END]).then_inc(newrow_out, 16)
            sp.dma_start(swa_s[:, 127 * 256:], z[0:NS, KVA:QB]).then_inc(newrow_out, 16)
            hold(sp, "sp", a_z, 5 * NT + 5)
            hold(sp, "sp", a_vb, NT)
            sp.dma_start(hpair[:, :, :].rearrange("p a n -> p (a n)").rearrange("p (h d) -> p h d", d=P),
                         keys.rearrange("h k d -> k h d")).then_inc(keys_in, 16)

            sp.dma_start(s_mB, mask_sb).then_inc(sconst_in, 16)
            sp.dma_start(s_mA, mask_sa).then_inc(sconst_in, 16)
            sp.dma_start(s_hm, head_mask).then_inc(sconst_in, 16)
            for r in range(NS):
                sp.dma_start(gsm[r * 8:r * 8 + 8, 3:4], sinks.rearrange("a h -> h a")).then_inc(sconst_in, 16)
            hold(sp, "sp", z_out, 32 * NT + 16)
            hold(sp, "sp", q_out, 32 * NT)
            sp.wait_ge(newrow_out, 32)
            sp.dma_start(s_new[0:8, 0:256], zS_scr[:, KVA:QB]).then_inc(snew_in, 16)
            sp.dma_start(s_new[0:8, 256:1280], zS_scr[:, KB:END]).then_inc(snew_in, 16)

            def cache_rows(dst, r, k_or_v):
                c = cache_dil[ds(r, 1), :, k_or_v * 512:k_or_v * 512 + 512].rearrange("r s n -> (r s) n")
                yield dst[:, 0, :], c[896:1024, :]
                yield dst[0:96, 1, :], c[512:896:4, :]
                yield dst[96:128, 1, :], c[0:512:16, :]

            with repeat(sp, 0, NS // 2) as i:
                for b in range(2):
                    r = 2 * i + b
                    hold(sp, "sp", s_mul, r - 1)
                    for dst, src in cache_rows(s_k[b], r, 0):
                        sp.dma_start(dst, src).then_inc(sk_in[b], 16)
                    sp.dma_start(s_kA[b], cache_swa[ds(r, 1), :].rearrange("r (s n) -> (r s) n", n=256)[:, 0:P])\
                      .then_inc(sk_in[b], 16)
                    sp.dma_start(s_q[b][:, 0:512], zS_scr[ds(r, 1), QA:KVA].broadcast_to([P, 512]))\
                      .then_inc(sk_in[b], 16)
                    sp.dma_start(s_q[b][:, 512:1024], zS_scr[ds(r, 1), QB:KB].broadcast_to([P, 512]))\
                      .then_inc(sk_in[b], 16)
            sp.dma_start(wq_sb[:, :, :], w_q.rearrange("(k p) n -> p k n", p=P)).then_inc(wq_in, 16)
            for r in range(NS):
                b = r % 2
                if r >= 2:
                    hold(sp, "sp", s_pv, r - 1)
                for dst, src in cache_rows(s_v[b], r, 1):
                    sp.dma_start(dst, src).then_inc(sv_in[b], 16)
                sp.dma_start(s_vA[b], cache_swa[r, :].rearrange("(s n) -> s n", n=256)[:, P:256])\
                  .then_inc(sv_in[b], 16)
            hold(sp, "sp", s_done, 1)
            sp.dma_start(oS_scr, s_o).then_inc(so_out, 16)
            sp.dma_start(swa_p, kvA_scr[(NT - 1) * P:NT * P, :]).then_inc(swa_out, 16)
            sp.wait_ge(so_out, 16)

            def att_tile(t):
                first = isinstance(t, int) and t == 0
                if not first:
                    hold(sp, "sp", att_s, 8 * t)
                    hold(sp, "sp", att_max, 8 * t)
                    hold(sp, "sp", att_pv, 8 * t)
                sp.dma_start(maskB[:, :], mask_b[:, ds((NT - 1 - t) * P, D)]).then_inc(att_in, 16)
                if first:
                    sp.dma_start(kTA[:, P:256], kTA_scr[:, 0:P]).then_inc(att_in, 16)
                    sp.dma_start(vA[:, 1, :], kvA_scr[0:P, P:256]).then_inc(att_in, 16)
                else:
                    sp.dma_start(kTA[:, :], kTA_scr[:, ds((t - 1) * P, 256)]).then_inc(att_in, 16)
                    sp.dma_start(vA[:, :, :], kvA_scr[ds((t - 1) * P, 256), P:256].rearrange(
                        "(b p) n -> p b n", p=P)).then_inc(att_in, 16)

            def att_q(t, p, par):
                hold(sp, "sp", att_s, 8 * t + 2 * p + par - 1)
                rows = slice(64 * par, 64 * par + 64)
                src = qT_scr.rearrange("(m b) r n -> b r m n", m=2)[ds(p, 1), rows, :, ds(t * P, P)]
                sp.dma_start(qpad[rows, par, :, :], src.rearrange("b r m n -> (b r) m n")).then_inc(qT_in[par], 16)

            def mix_loads(t):
                first = isinstance(t, int) and t == 0
                if not first:
                    hold(sp, "sp", acc_init, t)
                sp.dma_start(x2[:, :], x_all[ds(t * P, P), :]).then_inc(mx_in, 16)
                wo_v = w_out.rearrange("(k p) n -> k p n", p=P)
                for k in range(KD):
                    hold(sp, "sp", wo_used, KD * t + k + 1 - WO_SLOTS)
                    sp.dma_start(wo_sb[:, k % WO_SLOTS, :], wo_v[k]).then_inc(wo_in[k % WO_SLOTS], 16)

            def store_y(t):
                hold(sp, "sp", fin_y, t + 1)
                sp.dma_start(y_p[ds(t * P, P), :], ybuf[:, :]).then_inc(y_out, 16)

            hold(sp, "sp", pads, 1)
            att_tile(0)
            att_q(0, 0, 0)
            att_q(0, 0, 1)
            with repeat(sp, 1, 4) as p:
                att_q(0, p, 0)
                att_q(0, p, 1)
            mix_loads(0)
            att_tile(1)
            with repeat(sp, 0, 4) as p:
                att_q(1, p, 0)
                att_q(1, p, 1)
            with repeat(sp, 0, NT - 2) as t:
                mix_loads(t + 1)
                att_tile(t + 2)
                with repeat(sp, 0, 4) as p:
                    att_q(t + 2, p, 0)
                    att_q(t + 2, p, 1)
                store_y(t)
            mix_loads(NT - 1)
            hold(sp, "sp", mx_on, NT)
            sp.dma_start(o_all[0:NS, :], oS_scr).then_inc(so_in, 16)
            store_y(NT - 2)
            mix_loads(NT)
            store_y(NT - 1)
            hold(sp, "sp", fin_y, NT + 1)
            sp.dma_start(y_s, ybuf[0:NS, :]).then_inc(y_out, 16)
            hold(sp, "sp", y_out, 16 * (NT + 1))
            sp.wait_ge(cache_out, 16 * (NT + 1))
            sp.wait_ge(swa_out, 16)

        @block.gpsimd
        def _(pool):
            set_starts(pool, "pool")
            with repeat(pool, 0, NT) as t:
                hold(pool, "pool", a_ze, 5 * t + 5)
                pool.tensor_copy(VB[:, ds(t, 1), :].rearrange("p t n -> p (t n)"), z[:, VB_:END]).then_inc(a_vb, 1)

            def fetch(buf, table, win, landed):
                pool.indirect_dma_start(buf, None, table, bass.IndirectOffsetOnAxis(win, 0)).then_inc(landed, 16)

            def section(t, p, par, last=False):
                head = 2 * p + par
                s = 8 * t + head
                nxt = s + 1
                pool.tensor_copy(win_v[:, par, :], win_u[:, par, :]).then_inc(win_cp, 1)
                if not last:
                    hold(pool, "pool", pr_idx, 4 * t + p + 1 + par)
                    col = 0 if isinstance(p, int) and p == 3 and par == 1 else (head + 1) * TOPK
                    pool.tensor_copy(win_u[:, 1 - par, :], idx_all[:, ds(col, TOPK)]).then_inc(win_set, 1)
                    hold(pool, "pool", win_set, nxt + 1)
                hold(pool, "pool", win_cp, s + 1)
                for j in range(TOPK):
                    if not last:
                        hold(pool, "pool", u_used, TOPK * nxt + j - RING + 1)
                        fetch(u_ring[j % RING], peer_u, win_u[:, 1 - par, j:j + 1], u_in[j % RING])
                    hold(pool, "pool", v_used, TOPK * s + j - RING + 1)
                    fetch(v_ring[j % RING], peer_v, win_v[:, par, j:j + 1], v_in[j % RING])

            hold(pool, "pool", pr_idx, 1)
            pool.tensor_copy(win_u[:, 0, :], idx_all[:, 0:TOPK]).then_inc(win_set, 1)
            hold(pool, "pool", win_set, 1)
            for j in range(TOPK):
                hold(pool, "pool", u_used, j - RING + 1)
                fetch(u_ring[j % RING], peer_u, win_u[:, 0, j:j + 1], u_in[j % RING])
            with repeat(pool, 0, NT - 1) as t:
                with repeat(pool, 0, 3) as p:
                    section(t, p, 0)
                    section(t, p, 1)
                section(t, 3, 0)
                section(t, 3, 1)
            with repeat(pool, 0, 3) as p:
                section(NT - 1, p, 0)
                section(NT - 1, p, 1)
            section(NT - 1, 3, 0)
            section(NT - 1, 3, 1, last=True)
            hold(pool, "pool", gs_idx, 1)
            for r in range(NS):
                n = TOPK * HEADS * NT + r
                hold(pool, "pool", u_used, n - RING + 1)
                fetch(u_ring[r % RING], peer_u, idxT[:, r:r + 1], u_in[r % RING])
            for r in range(NS):
                n = TOPK * HEADS * NT + r
                hold(pool, "pool", v_used, n - RING + 1)
                fetch(v_ring[r % RING], peer_v, idxT[:, r:r + 1], v_in[r % RING])

        @block.tensor
        def _(pe):
            set_starts(pe, "pe")

            def x_transposes(t):
                pe.wait_ge(a_xs, after(a_xs, t + 1))
                for k in range(KD):
                    m = pe.transpose(acc[:, k * P:(k + 1) * P], xs[:, k * P:(k + 1) * P], idn[:, :])
                m.then_inc(a_xt, 1)

            def z_chunk(t, c, first=False):
                c0, w = CHUNKS[c]
                if first:
                    pe.wait_ge(win_in[c], 16)
                if c == 0:
                    pe.wait_ge(a_xT, after(a_xT, t + 1))
                    pe.wait_ge(a_ze, after(a_ze, 5 * t))
                if c == 1:
                    pe.wait_ge(a_te, after(a_te, 4 * t))
                for k in range(KD):
                    m = pe.matmul(zbank[c][:, 0:w], TT[:, k, :], w_in_sb[:, k, c0:c0 + w],
                                  start=(k == 0), stop=(k == KD - 1))
                m.then_inc(a_z, 1)

            def qk_transposes(t):
                pe.wait_ge(a_rope, after(a_rope, 2 * t + 2))
                pe.wait_ge(a_ze, after(a_ze, 5 * t + 4))
                for b in range(4):
                    m = pe.transpose(pS[:, 512 + b * P:512 + (b + 1) * P], z[:, b * P:(b + 1) * P], idn[:, :])
                m.then_inc(a_rt, 1)
                for b in range(4):
                    m = pe.transpose(pA[:, b * P:(b + 1) * P], z[:, QB + b * P:QB + (b + 1) * P], idn[:, :])
                m.then_inc(a_rt, 1)
                for b in range(4):
                    m = pe.transpose(pM[:, b * P:(b + 1) * P], z[:, KB + b * P:KB + (b + 1) * P], idn[:, :])
                m.then_inc(a_rt, 1)
                pe.transpose(pT[:, 0:P], z[:, KVA:KVA + P], idn[:, :]).then_inc(a_rt, 1)

            def project(t, first=False, last=False):
                z_chunk(t, 0, first)
                z_chunk(t, 1, first)
                if not last:
                    x_transposes(t + 1)
                for c in (2, 3, 4):
                    z_chunk(t, c, first)
                if not last:
                    qk_transposes(t)

            pe.wait_ge(c_in, 16 * 8)
            x_transposes(0)
            project(0, first=True)
            with repeat(pe, 1, NT) as t:
                project(t)
            project(NT, last=True)

            pe.wait_ge(keys_in, 16)
            pe.wait_ge(a_ze, after(a_ze, 5 * NT + 5))
            pe.wait_ge(a_te, after(a_te, 4 * NT))
            for b in range(2):
                if b:
                    pe.wait_ge(k_te, after(k_te, 1))
                for k in range(8):
                    m = pe.transpose(pT[:, k * P:(k + 1) * P], hpair[:, b, k * P:(k + 1) * P], idn[:, :])
                m.then_inc(k_t, 1)

            pe.wait_ge(s_mul, after(s_mul, NS))
            pe.transpose(pS[0:64, 0:P], s_sc[:, 0, :], idn[:, :])
            pe.transpose(pS[0:64, P:2 * P], s_sc[:, 1, :], idn[:, :])
            pe.transpose(pS[0:64, 256:264], s_scn[0:8, 0, :], idn[0:8, 0:8])
            pe.transpose(pS[0:64, 512:640], s_sc[:, 2, :], idn[:, :])
            pe.transpose(pS[0:64, 640:648], s_scn[0:8, 1, :], idn[0:8, 0:8]).then_inc(s_sT, 1)
            pe.wait_ge(s_prob, after(s_prob, 1))
            pe.wait_ge(k_te, after(k_te, 2))
            i64 = idn[0:64, 0:64]
            pe.transpose(pT[:, 0:64], s_pB[0:64, 0:P], i64)
            pe.transpose(pT[:, 64:128], s_pB[0:64, P:2 * P], i64)
            pe.transpose(pT[:, 128:192], s_pA[0:64, 0:P], i64)
            pe.transpose(pT[0:8, 192:256], s_pB[0:64, 256:264], i64)
            pe.transpose(pT[0:8, 256:320], s_pA[0:64, P:136], i64).then_inc(s_bT, 1)

            def sample_pv(r):
                b, bank = r % 2, (pS, pT)[r % 2]
                if r == 0:
                    pe.wait_ge(s_bTe, after(s_bTe, 1))
                if r >= 2:
                    pe.wait_ge(s_dg, after(s_dg, r - 1))
                pe.wait_ge(sv_in[b], 64 * (r // 2 + 1))
                c = slice(8 * r, 8 * r + 8)
                pe.matmul(bank[0:8, 0:512], s_pT[:, 0, c], s_v[b][:, 0, :], start=True, stop=False)
                pe.matmul(bank[0:8, 0:512], s_pT[:, 1, c], s_v[b][:, 1, :], start=False, stop=False)
                pe.matmul(bank[0:8, 0:512], s_pTn[0:8, 0, c], s_new[0:8, 768:1280], start=False, stop=True)
                pe.matmul(bank[0:8, 512:640], s_pT[:, 2, c], s_vA[b], start=True, stop=False)
                pe.matmul(bank[0:8, 512:640], s_pTn[0:8, 1, c], s_new[0:8, P:256],
                          start=False, stop=True).then_inc(s_pv, 1)

            def sample_fold(r):
                pe.wait_ge(s_dg, after(s_dg, r + 1))
                for half in range(2):
                    m = pe.matmul(acc[0:8, half * 512:(half + 1) * 512], e8[0:8, r, :],
                                  s_od[r % 2][:, half * 512:(half + 1) * 512], start=(r == 0), stop=(r == NS - 1))
                m.then_inc(s_fold, 1)

            sample_pv(0)
            for r in range(NS):
                if r + 1 < NS:
                    sample_pv(r + 1)
                sample_fold(r)

            def att_scores(t, p, par):
                a = 8 * t + 2 * p + par
                if par == 0 and (isinstance(p, int) and p == 0 or not isinstance(p, int)):
                    pe.wait_ge(att_in, 48 * (t + 1))
                pe.wait_ge(qT_in[par], 16 * (4 * t + p + 1))
                pe.wait_ge(att_max, after(att_max, a))
                pe.wait_ge(att_te, after(att_te, 3 * a))
                pe.wait_ge(mx_hT, after(mx_hT, t))
                for half in range(2):
                    pe.matmul(pS[:, half * 512:(half + 1) * 512], qpad[:, par, 1, :],
                              KTB[:, ds(p, 1), half * 512:(half + 1) * 512], start=True, stop=True)
                pe.matmul(pA[:, 0:256], qpad[:, par, 0, :], kTA[:, :], start=True, stop=True).then_inc(att_s, 1)

            def att_transposes(t, p, par):
                a = 8 * t + 2 * p + par
                pe.wait_ge(att_exp, after(att_exp, a + 1))
                for half in range(2):
                    for k in range(4 * half, 4 * half + 4):
                        m = pe.transpose(pT[:, k * P:(k + 1) * P], S_B[:, k * P:(k + 1) * P], idn[:, :])
                    m.then_inc(att_t, 1)
                for k in range(2):
                    m = pe.transpose(pA[:, 256 + k * P:256 + (k + 1) * P], S_A[:, k * P:(k + 1) * P], idn[:, :])
                m.then_inc(att_t, 1)

            def att_values(t, p, par, pair_of_peer):
                a = 8 * t + 2 * p + par
                pe.wait_ge(att_te, after(att_te, 3 * a + 3))
                if pair_of_peer is not None:
                    pe.wait_ge(pr_qe, after(pr_qe, pair_of_peer))
                for k in range(NT):
                    pe.matmul(pM[:, 256:320], PT[:, k, :],
                              VB[:, k, ds(p * P + par * HD, HD)], start=(k == 0), stop=(k == NT - 1))
                for k in range(2):
                    m = pe.matmul(pM[:, 320:384], PT[:, 8 + k, :], vA[:, k, par * HD:(par + 1) * HD],
                                  start=(k == 0), stop=(k == 1))
                m.then_inc(att_pv, 1)

            def gain_to_psum(which):
                for k in range(KD):
                    m = pe.matmul(pT[:, k * P:(k + 1) * P], idn[0:KD, k:k + 1].broadcast_to([KD, P]),
                                  grow[0:KD, which, :], start=True, stop=True)
                return m

            def mix(t):
                pe.wait_ge(mx_on, after(mx_on, t + 1))
                for k in range(KD):
                    m = pe.transpose(pT[:, k * P:(k + 1) * P], S[:, k * P:(k + 1) * P], idn[:, :])
                m.then_inc(mx_t, 1)
                pe.wait_ge(mx_onT, after(mx_onT, t + 1))
                for k in range(KD):
                    pe.wait_ge(wo_in[k % WO_SLOTS], 16 * ((KD // WO_SLOTS) * t + k // WO_SLOTS + 1))
                    for half in range(2):
                        m = pe.matmul(pS[:, half * 512:(half + 1) * 512], TT[:, k, :],
                                      wo_sb[:, k % WO_SLOTS, half * 512:(half + 1) * 512],
                                      start=(k == 0), stop=(k == KD - 1))
                    m.then_inc(wo_used, 1)
                gain_to_psum(0).then_inc(mx_mm, 1)
                pe.wait_ge(mx_h, after(mx_h, t + 1))
                for k in range(KD):
                    m = pe.transpose(pS[:, k * P:(k + 1) * P], h_next[:, k * P:(k + 1) * P], idn[:, :])
                m.then_inc(mx_ht, 1)

            def peer_query(t, p, par, att):
                b = 8 * t + 2 * p + par
                pe.wait_ge(mx_hT, after(mx_hT, t + 1))
                pe.wait_ge(pr_se, after(pr_se, b))
                if att is not None:
                    pe.wait_ge(att_o, after(att_o, att))
                for k in range(KD):
                    m = pe.matmul(pM[:, 0:256], TT[:, k, :], wq_sb[:, k, ds(p * 512 + par * 256, 256)],
                                  start=(k == 0), stop=(k == KD - 1))
                m.then_inc(pr_q, 1)

            def peer_transposes(t, p, par, att):
                b = 8 * t + 2 * p + par
                pe.wait_ge(pr_qe, after(pr_qe, b + 1))
                if att is not None:
                    pe.wait_ge(att_te, after(att_te, 3 * att + 3))
                for k in range(2):
                    m = pe.transpose(pA[:, k * P:(k + 1) * P], pq[:, k * P:(k + 1) * P], idn[:, :])
                m.then_inc(pr_t, 1)

            def peer_scores(t, p, par, att):
                b = 8 * t + 2 * p + par
                pe.wait_ge(pr_te, after(pr_te, b + 1))
                if att is not None:
                    pe.wait_ge(att_o, after(att_o, att + 1))
                for k in range(2):
                    m = pe.matmul(pM[:, k * P:(k + 1) * P], pqT[:, k, :],
                                  keysT[:, ds(4 * p + 2 * par + k, 1), :], start=True, stop=True)
                m.then_inc(pr_s, 1)

            def weigh(s, j):
                n = TOPK * s + j
                pe.wait_ge(diag_set, after(diag_set, n + 1))
                pe.wait_ge(v_in[j % RING], 16 * (4 * s + j // RING + 1))
                for half in range(2):
                    m = pe.matmul(acc[:, half * 512:(half + 1) * 512], diag[:, j % 4, :],
                                  v_ring[j % RING][:, half * 512:(half + 1) * 512],
                                  start=False, stop=False, skip_group_check=True)
                m.then_inc(v_used, 1)

            def acc_start(t, rows=P):
                pe.wait_ge(mx_mm, after(mx_mm, t + 1))
                pe.wait_ge(mx_h, after(mx_h, t + 1))
                if not (isinstance(t, int) and t == 0):
                    pe.wait_ge(fin_free, after(fin_free, t))
                for half in range(2):
                    m = pe.matmul(acc[0:rows, half * 512:(half + 1) * 512], idn[:, 0:rows],
                                  x2[:, half * 512:(half + 1) * 512], start=True, stop=False,
                                  skip_group_check=True)
                m.then_inc(acc_init, 1)

            def final_gain(t):
                pe.wait_ge(att_te, after(att_te, min(3 * 8 * (t + 3), 3 * 8 * NT) if isinstance(t, int) else
                                         3 * 8 * (t + 3)))
                gain_to_psum(1).then_inc(fin_g, 1)

            def section(p, par, tg=None, tp=None, ta=None):
                h = 2 * p + par
                att = None if ta is None else 8 * ta + h
                done = NT * 8 if ta is None else att
                for j in range(TOPK):
                    if ta is not None and j == 0:
                        att_scores(ta, p, par)
                    if tp is not None and j == 2:
                        peer_query(tp, p, par, done)
                    if ta is not None and j == 5:
                        att_transposes(ta, p, par)
                    if ta is not None and j == 8:
                        att_values(ta, p, par, None if tp is None else 8 * tp + h + 1)
                    if tp is not None and j == 9:
                        peer_transposes(tp, p, par, att)
                    if tp is not None and j == 12:
                        peer_scores(tp, p, par, att)
                    if tg is not None:
                        weigh(8 * tg + h, j)

            with repeat(pe, 0, 4) as p:
                section(p, 0, ta=0)
                section(p, 1, ta=0)
            mix(0)
            with repeat(pe, 0, 4) as p:
                section(p, 0, tp=0, ta=1)
                section(p, 1, tp=0, ta=1)
            acc_start(0)
            with repeat(pe, 0, NT - 2) as t:
                mix(t + 1)
                with repeat(pe, 0, 4) as p:
                    section(p, 0, tg=t, tp=t + 1, ta=t + 2)
                    section(p, 1, tg=t, tp=t + 1, ta=t + 2)
                final_gain(t)
                acc_start(t + 1)
            for t in (NT - 2, NT - 1):
                mix(t + 1)
                with repeat(pe, 0, 4) as p:
                    section(p, 0, tg=t, tp=t + 1)
                    section(p, 1, tg=t, tp=t + 1)
                final_gain(t)
                if t == NT - 1:
                    pe.wait_ge(gs_in, after(gs_in, 1))
                    pe.transpose(pA[:, 0:8], S[0:8, 0:P], idn[0:8, 0:8])
                    pe.transpose(pA[:, 8:16], gates[0:8, :], idn[0:8, 0:8]).then_inc(gs_t, 1)
                acc_start(t + 1, P if t < NT - 1 else NS)
            for r in range(NS):
                bank = (pS, pT)[r % 2]
                if r == 1:
                    pe.wait_ge(fin_y, after(fin_y, NT))
                if r >= 2:
                    pe.wait_ge(u_used, after(u_used, TOPK * 8 * NT + r - 1))
                for half in range(2):
                    m = pe.matmul(bank[:, half * 512:(half + 1) * 512], idn[:, r:r + 1].broadcast_to([P, P]),
                                  h_next[:, half * 512:(half + 1) * 512], start=True, stop=True)
                m.then_inc(gs_h, 1)
            pe.wait_ge(gs_w, after(gs_w, 1))
            for r in range(NS):
                pe.wait_ge(v_in[r % RING], 16 * (4 * 8 * NT + r // RING + 1))
                for half in range(2):
                    m = pe.matmul(acc[0:NS, half * 512:(half + 1) * 512], wz[:, r, :],
                                  v_ring[r % RING][:, half * 512:(half + 1) * 512],
                                  start=False, stop=False, skip_group_check=True)
                m.then_inc(v_used, 1)
            gain_to_psum(1).then_inc(fin_g, 1)

        @block.scalar
        def _(act):
            set_starts(act, "act")

            def copy(out, in_):
                return act.activation(out, in_, ACT.Copy)

            def z_copies(t):
                for c, (c0, w) in enumerate(CHUNKS):
                    act.wait_ge(a_z, after(a_z, 5 * t + c + 1))
                    if c == 0:
                        act.wait_ge(z_out, after(z_out, 32 * t))
                        act.wait_ge(a_vb, after(a_vb, t))
                        act.wait_ge(a_rt, after(a_rt, 4 * t))
                    if c == 0:
                        copy(z[:, 0:512].rearrange("p (b a d) -> p a b d", a=2, b=4),
                             zbank[0].rearrange("p (a b d) -> p a b d", a=2, b=4)).then_inc(a_ze, 1)
                    else:
                        copy(z[:, c0:c0 + w], zbank[c][:, 0:w]).then_inc(a_ze, 1)

            with repeat(act, 0, NT) as t:
                z_copies(t)
                act.wait_ge(q_out, after(q_out, 32 * t))
                act.wait_ge(a_rt, after(a_rt, 4 * t + 1))
                copy(qTe[:, 0:4, :], pS[:, 512:1024].rearrange("p (b n) -> p b n", b=4)).then_inc(a_te, 1)
                act.wait_ge(a_rt, after(a_rt, 4 * t + 2))
                copy(qTe[:, 4:8, :], pA[:, :].rearrange("p (b n) -> p b n", b=4)).then_inc(a_te, 1)
                act.wait_ge(a_rt, after(a_rt, 4 * t + 3))
                copy(KTB[:, :, ds(t * P, P)], pM[:, :].rearrange("p (b n) -> p b n", b=4)).then_inc(a_te, 1)
                act.wait_ge(a_rt, after(a_rt, 4 * t + 4))
                copy(kTAe, pT[:, 0:P]).then_inc(a_te, 1)
            z_copies(NT)
            for b in range(2):
                act.wait_ge(k_t, after(k_t, b + 1))
                copy(keysT[:, 8 * b:8 * b + 8, :], pT[:, :].rearrange("p (h k) -> p h k", h=8)).then_inc(k_te, 1)

            act.wait_ge(s_max, after(s_max, 1))
            act.activation(s_pB[0:64, :], s_pB[0:64, :], ACT.Exp, bias=anm[0:64, 0:1], accum_out=aden[0:64, 0:1])
            act.activation(s_pA[0:64, :], s_pA[0:64, :], ACT.Exp, bias=anm[0:64, 1:2], accum_out=aden[0:64, 1:2])
            act.activation(aden[0:64, 2:3], s_sink, ACT.Exp, bias=anm[0:64, 1:2]).then_inc(s_exp, 1)
            act.wait_ge(s_bT, after(s_bT, 1))
            copy(s_pT, pT[:, 0:192].rearrange("p (s n) -> p s n", s=3))
            copy(s_pTn[0:8, :, :], pT[0:8, 192:320].rearrange("p (s n) -> p s n", s=2)).then_inc(s_bTe, 1)

            def att_softmax(t, p, par):
                a = 8 * t + 2 * p + par
                act.wait_ge(att_max, after(att_max, a + 1))
                act.activation(S_B, S_B, ACT.Exp, bias=anm[:, 0:1], accum_out=aden[:, 0:1])
                act.activation(S_A, S_A, ACT.Exp, bias=anm[:, 1:2], accum_out=aden[:, 1:2])
                act.activation(aden[:, 2:3], sink[:, ds(p + 4 * par, 1)], ACT.Exp,
                               bias=anm[:, 1:2]).then_inc(att_exp, 1)

            def att_copies(t, p, par):
                a = 8 * t + 2 * p + par
                act.wait_ge(att_pv, after(att_pv, a))
                for k in range(2):
                    act.wait_ge(att_t, after(att_t, 3 * a + k + 1))
                    copy(PT[:, 4 * k:4 * k + 4, :],
                         pT[:, 512 * k:512 * k + 512].rearrange("p (b n) -> p b n", b=4)).then_inc(att_te, 1)
                act.wait_ge(att_t, after(att_t, 3 * a + 3))
                copy(PT[:, 8:10, :], pA[:, 256:512].rearrange("p (b n) -> p b n", b=2)).then_inc(att_te, 1)

            def mix(t):
                act.wait_ge(mx_ht, after(mx_ht, t + 1))
                copy(TT[:, 0:4, :], pS[:, 0:512].rearrange("p (b n) -> p b n", b=4))
                copy(TT[:, 4:8, :], pS[:, 512:1024].rearrange("p (b n) -> p b n", b=4)).then_inc(mx_hT, 1)

            def tanh(s, par):
                act.wait_ge(gl_in, after(gl_in, s + 1))
                act.activation(gl[:, 1, :], gl[:, 0, :], ACT.Tanh, scale=GELU_C).then_inc(gl_th, 1)

            def section(p, par, tg=None, tp=None, ta=None):
                h = 2 * p + par
                if tg is not None:
                    tanh(8 * tg + h, par)
                    act.wait_ge(w_set, after(w_set, 8 * tg + h + 1))
                for j in range(TOPK):
                    if tg is not None:
                        n = TOPK * (8 * tg + h) + j
                        act.wait_ge(v_used, after(v_used, n - 3))
                        act.activation(diag[:, j % 4, :], idn[:, :], ACT.Copy,
                                       scale=wv[:, par, j:j + 1]).then_inc(diag_set, 1)
                    if ta is not None and j == 3:
                        att_softmax(ta, p, par)
                    if tp is not None and j == 4:
                        act.wait_ge(pr_q, after(pr_q, 8 * tp + h + 1))
                        act.wait_ge(pr_t, after(pr_t, 8 * tp + h))
                        copy(pq[:, :], pM[:, 0:256]).then_inc(pr_qe, 1)
                    if ta is not None and j == 7:
                        att_copies(ta, p, par)
                    if tp is not None and j == 10:
                        act.wait_ge(pr_t, after(pr_t, 8 * tp + h + 1))
                        copy(pqT[:, :, :], pA[:, 0:256].rearrange("p (b n) -> p b n", b=2)).then_inc(pr_te, 1)
                    if tp is not None and j == 13:
                        act.wait_ge(pr_s, after(pr_s, 8 * tp + h + 1))
                        act.wait_ge(pr_top, after(pr_top, 8 * tp + h))
                        copy(sc[:, :, :], pM[:, 0:256].rearrange("p (b n) -> p b n", b=2)).then_inc(pr_se, 1)
                if tp is not None:
                    act.wait_ge(pr_top, after(pr_top, 8 * tp + h + 1))
                    act.activation(gexp[:, :], candv[:, par, :], ACT.Exp, bias=gsm[:, 0:1],
                                   accum_out=gsm[:, 1:2]).then_inc(pr_exp, 1)

            with repeat(act, 0, 4) as p:
                section(p, 0, ta=0)
                section(p, 1, ta=0)
            mix(0)
            with repeat(act, 0, 4) as p:
                section(p, 0, tp=0, ta=1)
                section(p, 1, tp=0, ta=1)
            with repeat(act, 0, NT - 2) as t:
                mix(t + 1)
                with repeat(act, 0, 4) as p:
                    section(p, 0, tg=t, tp=t + 1, ta=t + 2)
                    section(p, 1, tg=t, tp=t + 1, ta=t + 2)
            with repeat(act, NT - 2, NT) as t:
                mix(t + 1)
                with repeat(act, 0, 4) as p:
                    section(p, 0, tg=t, tp=t + 1)
                    section(p, 1, tg=t, tp=t + 1)
            act.wait_ge(gs_in, after(gs_in, 2))
            act.activation(gl[:, 1, 0:NS], gl[:, 0, 0:NS], ACT.Tanh, scale=GELU_C).then_inc(gs_th, 1)

        @block.vector
        def _(dve):
            set_starts(dve, "dve")
            D_ = dve.drain

            dve.memset(qpad[:, :, :, :], 0.0)
            dve.memset(kTA[:, 0:P], 0.0)
            dve.memset(vA[:, 0, :], 0.0).then_inc(pads, 1)

            def sum_squares(x, n, out, junk, rows=P):
                dve.tensor_tensor_reduce(junk, x, x, 1.0, 0.0, ALU.mult, ALU.add, out)

            def rsqrt(rows, cols, count):
                r, c = slice(0, rows), slice(0, cols)
                D_()
                dve.tensor_scalar(nw_x[r, c], ssum[r, c], 1.0 / count, EPS, ALU.mult, ALU.add)
                D_()
                dve.tensor_scalar(nw_i[r, c], nw_x[r, c].bitcast(I32), 1, None, ALU.arith_shift_right)
                D_()
                dve.tensor_scalar(nw_i[r, c], nw_i[r, c], -1.0, MAGIC, ALU.mult, ALU.add)
                y = nw_i[r, c].bitcast(F32)
                for _ in range(3):
                    D_()
                    dve.tensor_tensor(nw_a[r, c], y, y, ALU.mult)
                    D_()
                    dve.scalar_tensor_tensor(nw_b[r, c], nw_a[r, c], -0.5, nw_x[r, c], ALU.mult, ALU.mult)
                    D_()
                    dve.scalar_tensor_tensor(nw_y[r, c], nw_b[r, c], 1.5, y, ALU.add, ALU.mult)
                    y = nw_y[r, c]
                D_()

            def with_gain(which, psum, done):
                for half in range(2):
                    g = gcol[:, which, 4 * half:4 * half + 4].unsqueeze(2).broadcast_to([P, 4, P])
                    i = dve.tensor_tensor(TT[:, 4 * half:4 * half + 4, :],
                                          psum[:, 512 * half:512 * half + 512].rearrange("p (b n) -> p b n", b=4),
                                          g, ALU.mult)
                i.then_inc(done, 1)

            def scale_x(t):
                dve.wait_ge(x_in, 16 * (t + 1))
                sum_squares(xin, D, ssum[:, 0:1], xs)
                rsqrt(P, 1, D)
                dve.tensor_scalar(xs, xin, nw_y[:, 0:1], None, ALU.mult).then_inc(a_xs, 1)

            def x_gain(t):
                dve.wait_ge(a_xt, after(a_xt, t + 1))
                dve.wait_ge(a_z, after(a_z, 5 * t))
                with_gain(0, acc, a_xT)

            def rope(t, c0, heads):
                zr = z[:, c0:c0 + heads * HD].rearrange("p (h d) -> p h d", d=HD)[:, :, 0:16]
                lo, hi = zr[:, :, 0:8], zr[:, :, 8:16]
                cos = rcs[:, ds(t, 1), 0:8].broadcast_to([P, heads, 8])
                sin = rcs[:, ds(t, 1), 8:16].broadcast_to([P, heads, 8])
                tmp = rtmp[:, 0:4 * heads * 8].rearrange("p (a h d) -> p a h d", a=4, h=heads)
                dve.tensor_tensor(tmp[:, 0, :, :], lo, cos, ALU.mult)
                dve.tensor_tensor(tmp[:, 1, :, :], hi, sin, ALU.mult)
                dve.tensor_tensor(tmp[:, 2, :, :], hi, cos, ALU.mult)
                dve.tensor_tensor(tmp[:, 3, :, :], lo, sin, ALU.mult)
                D_()
                dve.tensor_tensor(lo, tmp[:, 0, :, :], tmp[:, 1, :, :], ALU.subtract)
                dve.tensor_tensor(hi, tmp[:, 2, :, :], tmp[:, 3, :, :], ALU.add).then_inc(a_rope, 1)

            def rope_tile(t):
                dve.wait_ge(a_ze, after(a_ze, 5 * t + 2))
                rope(t, QA, 10)
                D_()
                dve.wait_ge(a_ze, after(a_ze, 5 * t + 4))
                rope(t, QB, 16)

            dve.wait_ge(c_in, 16 * 8)
            scale_x(0)
            x_gain(0)
            with repeat(dve, 0, NT) as t:
                scale_x(t + 1)
                rope_tile(t)
                x_gain(t + 1)
            rope_tile(NT)

            dve.wait_ge(snew_in, 32)
            dve.wait_ge(a_z, after(a_z, 5 * NT + 5))
            dve.wait_ge(a_rt, after(a_rt, 4 * NT))

            def dot_heads(out, k, q, n, rows, groups):
                prod = s_prod[0:rows, 0:n]
                D_()
                dve.tensor_tensor(prod.rearrange("p (a b c) -> p a b c", a=groups[0], b=groups[1]), k, q, ALU.mult)
                D_()
                return dve.tensor_reduce(out, prod.rearrange("p (a b d) -> p a b d", d=HD, a=groups[2]),
                                         AX_X, ALU.add)

            with repeat(dve, 0, NS // 2) as i:
                for b in range(2):
                    r = 2 * i + b
                    cols = ds(r * 8, 8)
                    hold(dve, "dve", sk_in[b], 96 * (i + 1))
                    qA, qB = s_q[b][:, 0:512], s_q[b][:, 512:1024]
                    dot_heads(s_sc[:, 0:2, cols], s_k[b].unsqueeze(2),
                              qB.unsqueeze(1).unsqueeze(1).broadcast_to([P, 2, 1, 512]), 1024, P, (2, 1, 2))
                    dot_heads(s_sc[:, 2:3, cols], s_kA[b].rearrange("p (a d) -> p a d", a=2)
                              .unsqueeze(2).broadcast_to([P, 2, 4, HD]),
                              qA.rearrange("p (b a d) -> p a b d", a=2, b=4), 512, P, (2, 4, 1))
                    dot_heads(s_scn[0:8, 0:1, cols], s_new[0:8, 256:768].unsqueeze(1).unsqueeze(1),
                              qB[0:8, :].unsqueeze(1).unsqueeze(1), 512, 8, (1, 1, 1))
                    dot_heads(s_scn[0:8, 1:2, cols], s_new[0:8, 0:P].rearrange("p (a d) -> p a d", a=2)
                              .unsqueeze(2).broadcast_to([8, 2, 4, HD]),
                              qA[0:8, :].rearrange("p (b a d) -> p a b d", a=2, b=4), 512, 8, (2, 4, 1))\
                        .then_inc(s_mul, 1)
            dve.wait_ge(s_sT, after(s_sT, 1))
            dve.wait_ge(sconst_in, 16 * (3 + NS))
            R = slice(0, 64)
            dve.tensor_tensor_reduce(s_pB[R, :], pS[R, 0:264], s_mB, 0.125, NEG, ALU.add, ALU.max, amax[R, 0:1])
            dve.tensor_tensor_reduce(s_pA[R, :], pS[R, 512:648], s_mA, 0.125, NEG, ALU.add, ALU.max, amax[R, 1:2])
            D_()
            dve.tensor_tensor(amax[R, 1:2], amax[R, 1:2], s_sink, ALU.max)
            D_()
            dve.tensor_scalar(anm[R, :], amax[R, :], -1.0, None, ALU.mult).then_inc(s_max, 1)
            dve.wait_ge(s_exp, after(s_exp, 1))
            dve.tensor_tensor(aden[R, 1:2], aden[R, 1:2], aden[R, 2:3], ALU.add)
            D_()
            dve.reciprocal(arden[R, :], aden[R, 0:2])
            D_()
            dve.tensor_scalar(s_pB[R, :], s_pB[R, :], arden[R, 0:1], None, ALU.mult)
            dve.tensor_scalar(s_pA[R, :], s_pA[R, :], arden[R, 1:2], None, ALU.mult).then_inc(s_prob, 1)
            for r in range(NS):
                bank = (pS, pT)[r % 2]
                dve.wait_ge(s_pv, after(s_pv, r + 1))
                if r >= 2:
                    dve.wait_ge(s_fold, after(s_fold, r - 1))
                dve.tensor_tensor(s_od[r % 2][:, 0:512].rearrange("p (a b d) -> p a b d", a=2, b=4),
                                  bank[0:8, 512:640].rearrange("p (a d) -> p a d", a=2).unsqueeze(2)
                                  .broadcast_to([8, 2, 4, HD]),
                                  s_hm.rearrange("p (a b d) -> p a b d", a=2, b=4), ALU.mult)
                dve.tensor_tensor(s_od[r % 2][:, 512:1024], bank[0:8, 0:512], s_hm, ALU.mult).then_inc(s_dg, 1)
            dve.wait_ge(s_fold, after(s_fold, NS))
            dve.tensor_copy(s_o, acc[0:8, :]).then_inc(s_done, 1)

            def att_maxima(t, p, par, first):
                a = 8 * t + 2 * p + par
                dve.wait_ge(att_s, after(att_s, a + 1))
                hold(dve, "dve", att_t, 3 * a)
                dve.tensor_tensor_reduce(S_B, pS[:, :], maskB[:, :], 0.125, NEG, ALU.add, ALU.max, amax[:, 0:1])
                dve.tensor_tensor_reduce(S_A, pA[:, 0:256], maskA[:, 0 if first else 1, :], 0.125, NEG,
                                         ALU.add, ALU.max, amax[:, 1:2])
                D_()
                dve.tensor_tensor(amax[:, 1:2], amax[:, 1:2], sink[:, ds(p + 4 * par, 1)], ALU.max)
                D_()
                dve.tensor_scalar(anm[:, :], amax[:, :], -1.0, None, ALU.mult).then_inc(att_max, 1)

            def att_output(t, p, par):
                a = 8 * t + 2 * p + par
                dve.wait_ge(att_exp, after(att_exp, a + 1))
                dve.tensor_tensor(aden[:, 1:2], aden[:, 1:2], aden[:, 2:3], ALU.add)
                D_()
                dve.reciprocal(arden[:, :], aden[:, 0:2])
                D_()
                dve.wait_ge(att_pv, after(att_pv, a + 1))
                dve.tensor_scalar(o_all[:, ds(512 + p * P + par * HD, HD)], pM[:, 256:320], arden[:, 0:1],
                                  None, ALU.mult)
                dve.tensor_scalar(o_all[:, ds(p * HD + par * 256, HD)], pM[:, 320:384], arden[:, 1:2],
                                  None, ALU.mult).then_inc(att_o, 1)

            def mix(t):
                if isinstance(t, int) and t == NT:
                    hold(dve, "dve", so_in, 16)
                D_()
                for half in range(2):
                    c = slice(512 * half, 512 * half + 512)
                    sum_squares(o_all[:, c], 512, ssum[:, half:half + 1], S[:, c])
                rsqrt(P, 2, 512)
                for half in range(2):
                    c = slice(512 * half, 512 * half + 512)
                    i = dve.tensor_scalar(S[:, c], o_all[:, c], nw_y[:, half:half + 1], None, ALU.mult)
                i.then_inc(mx_on, 1)
                dve.wait_ge(mx_t, after(mx_t, t + 1))
                if not (isinstance(t, int) and t == 0):
                    dve.wait_ge(pr_q, after(pr_q, 8 * t))
                with_gain(1, pT, mx_onT)
                dve.wait_ge(mx_mm, after(mx_mm, t + 1))
                dve.wait_ge(mx_in, 16 * (t + 1))
                dve.tensor_tensor(x2[:, :], x2[:, :], pS[:, :], ALU.add)
                D_()
                sum_squares(x2[:, :], D, ssum[:, 0:1], S_B)
                rsqrt(P, 1, D)
                dve.scalar_tensor_tensor(h_next, x2[:, :], nw_y[:, 0:1], pT[:, :], ALU.mult,
                                         ALU.mult).then_inc(mx_h, 1)

            def top16(values, places, scores, width):
                D_()
                dve.max(values[:, 0:8], scores)
                D_()
                dve.max_index(places[:, 0:8], values[:, 0:8], scores)
                D_()
                dve.match_replace(scores, values[:, 0:8], scores, NEG)
                D_()
                dve.max(values[:, 8:16], scores)
                D_()
                dve.max_index(places[:, 8:16], values[:, 8:16], scores)

            def rank(t, p, par):
                b = 8 * t + 2 * p + par
                hold(dve, "dve", pr_se, b + 1)
                for half in range(2):
                    top16(topv[:, par, half, :], topi[:, par, half, :], sc[:, half, :], KEYS)
                D_()
                dve.tensor_tensor(cand[:, :, :], topv[:, par, 0, :].unsqueeze(2).broadcast_to([P, TOPK, TOPK]),
                                  topv[:, par, 1, :].unsqueeze(1).broadcast_to([P, TOPK, TOPK]), ALU.add)
                top16(candv[:, par, :], candp[:, par, :], cand[:, :, :].rearrange("p a b -> p (a b)"), TOPK * TOPK)
                dve.tensor_scalar(gsm[:, 0:1], candv[:, par, 0:1], -1.0, None, ALU.mult).then_inc(pr_top, 1)

            def gate(t, p, par):
                b = 8 * t + 2 * p + par
                dve.wait_ge(pr_exp, after(pr_exp, b + 1))
                dve.reciprocal(gsm[:, 2:3], gsm[:, 1:2])
                D_()
                dve.tensor_scalar(gates[:, ds(p * 32 + par * TOPK, TOPK)], gexp[:, :], gsm[:, 2:3], None, ALU.mult)

            def numbers(t, p, gathered):
                D_()
                dve.tensor_copy(topif[:, :, :, :], topi[:, :, :, :])
                for half in range(2):
                    if half == 0:
                        dve.tensor_scalar(candh[:, :, :], candp[:, :, :], 4, None, ALU.logical_shift_right)
                    else:
                        dve.tensor_scalar(candh[:, :, :], candp[:, :, :], 15, None, ALU.bitwise_and)
                    D_()
                    dve.tensor_copy(candf[:, :, :], candh[:, :, :])
                    D_()
                    full = [P, 2, TOPK, TOPK]
                    dve.tensor_tensor(onehot[:, :, :, :], candf[:, :, :].unsqueeze(3).broadcast_to(full),
                                      iota[:, :].unsqueeze(1).unsqueeze(1).broadcast_to(full), ALU.is_equal)
                    D_()
                    dve.tensor_tensor(onehot[:, :, :, :], onehot[:, :, :, :],
                                      topif[:, :, half, :].unsqueeze(2).broadcast_to(full), ALU.mult)
                    D_()
                    dve.tensor_reduce(sel[:, half, :, :], onehot[:, :, :, :], AX_X, ALU.add)
                D_()
                if gathered is not None:
                    dve.wait_ge(win_set, after(win_set, gathered))
                dve.scalar_tensor_tensor(
                    idx_all[:, ds(p * 32, 32)], sel[:, 0, :, :].rearrange("p a b -> p (a b)"), float(KEYS),
                    sel[:, 1, :, :].rearrange("p a b -> p (a b)"), ALU.mult, ALU.add).then_inc(pr_idx, 1)

            def dot(us, j, par):
                dve.wait_ge(u_in[j % RING], 16 * (4 * us + j // RING + 1))
                dve.tensor_tensor_reduce(u_ring[j % RING], u_ring[j % RING], h_cur, 1.0, 0.0, ALU.mult, ALU.add,
                                         dots[:, par, j:j + 1]).then_inc(u_used, 1)

            def gelu_arg(x, n):
                D_()
                dve.tensor_tensor(gl[:, 0, 0:n], x, x, ALU.mult)
                D_()
                dve.tensor_scalar(gl[:, 0, 0:n], gl[:, 0, 0:n], 0.044715, 1.0, ALU.mult, ALU.add)
                D_()
                return dve.tensor_tensor(gl[:, 0, 0:n], gl[:, 0, 0:n], x, ALU.mult)

            def gelu_gate(out, x, g, n):
                dve.scalar_tensor_tensor(gl[:, 2, 0:n], gl[:, 1, 0:n], 1.0, x, ALU.add, ALU.mult)
                D_()
                return dve.scalar_tensor_tensor(out, gl[:, 2, 0:n], 0.5, g, ALU.mult, ALU.mult)

            def section(p, par, tg=None, tp=None, ta=None, first=False, last=False):
                h = 2 * p + par
                s = None if tg is None else 8 * tg + h
                ends = isinstance(p, int) and p == 3 and par == 1
                if tg is not None:
                    gelu_arg(dots[:, par, :], TOPK).then_inc(gl_in, 1)
                    if ends:
                        dve.tensor_copy(h_cur, h_next)
                        D_()
                for j in range(TOPK):
                    if tg is not None and not (last and ends):
                        dot(s + 1, j, 1 - par)
                    if tg is not None and j == 0:
                        dve.wait_ge(gl_th, after(gl_th, s + 1))
                        gelu_gate(wv[:, par, :], dots[:, par, :], gates[:, ds(h * TOPK, TOPK)], TOPK)\
                            .then_inc(w_set, 1)
                    if ta is not None and j == 1:
                        att_maxima(ta, p, par, first)
                    if ta is not None and j == 9:
                        att_output(ta, p, par)
                    if tp is not None and j == 14:
                        rank(tp, p, par)
                if tp is not None:
                    gate(tp, p, par)
                    if par == 1:
                        numbers(tp, p, None if tg is None else s + 1)

            def final(t, rows=P):
                r = slice(0, rows)
                n = TOPK * 8 * (t + 1) if rows == P else TOPK * 8 * NT + NS
                dve.wait_ge(v_used, after(v_used, n))
                dve.wait_ge(y_out, after(y_out, 16 * t))
                dve.tensor_copy(ybuf[r, :], acc[r, :]).then_inc(fin_free, 1)
                D_()
                sum_squares(ybuf[r, :], D, ssum[r, 0:1], S[r, 0:D])
                rsqrt(rows, 1, D)
                dve.wait_ge(fin_g, after(fin_g, t + 1))
                dve.scalar_tensor_tensor(ybuf[r, :], ybuf[r, :], nw_y[r, 0:1], pT[r, :], ALU.mult, ALU.mult)\
                    .then_inc(fin_y, 1)

            with repeat(dve, 0, 4) as p:
                section(p, 0, ta=0, first=True)
                section(p, 1, ta=0, first=True)
            mix(0)
            with repeat(dve, 0, 4) as p:
                section(p, 0, tp=0, ta=1)
                section(p, 1, tp=0, ta=1)
            dve.tensor_copy(h_cur, h_next)
            D_()
            for j in range(TOPK):
                dot(0, j, 0)
            with repeat(dve, 0, NT - 2) as t:
                mix(t + 1)
                with repeat(dve, 0, 3) as p:
                    section(p, 0, tg=t, tp=t + 1, ta=t + 2)
                    section(p, 1, tg=t, tp=t + 1, ta=t + 2)
                section(3, 0, tg=t, tp=t + 1, ta=t + 2)
                section(3, 1, tg=t, tp=t + 1, ta=t + 2)
                final(t)
            for t in (NT - 2, NT - 1):
                mix(t + 1)
                with repeat(dve, 0, 3) as p:
                    section(p, 0, tg=t, tp=t + 1)
                    section(p, 1, tg=t, tp=t + 1)
                section(3, 0, tg=t, tp=t + 1)
                section(3, 1, tg=t, tp=t + 1, last=(t == NT - 1))
                if t == NT - 1:
                    D_()
                    dve.tensor_copy(S[0:8, 0:P], idx_all[0:8, :]).then_inc(gs_in, 1)
                    dve.wait_ge(gs_t, after(gs_t, 1))
                    dve.tensor_copy(gateT[:, :], pA[:, 8:16])
                    dve.tensor_copy(idxT[:, :], pA[:, 0:8]).then_inc(gs_idx, 1)
                final(t)
            for r in range(NS):
                dve.wait_ge(u_in[r % RING], 16 * (4 * 8 * NT + r // RING + 1))
                dve.wait_ge(gs_h, after(gs_h, r + 1))
                dve.tensor_tensor_reduce(u_ring[r % RING], u_ring[r % RING], (pS, pT)[r % 2][:, :], 1.0, 0.0,
                                         ALU.mult, ALU.add, dotsT[:, r:r + 1]).then_inc(u_used, 1)
            gelu_arg(dotsT[:, :], NS).then_inc(gs_in, 1)
            dve.wait_ge(gs_th, after(gs_th, 1))
            gelu_gate(gl[:, 0, NS:2 * NS], dotsT[:, :], gateT[:, :], NS)
            D_()
            dve.tensor_tensor(wz[:, :, :], gl[:, 0, NS:2 * NS].unsqueeze(2).broadcast_to([P, NS, 8]),
                              e8[:, :, :], ALU.mult).then_inc(gs_w, 1)
            final(NT, NS)


def tables(np):
    pos = np.concatenate([np.arange(NT * P), np.full(P, NT * P)]).astype(np.float32)
    inv = (np.float32(500000.0) ** (-np.arange(0, 16, 2, dtype=np.float32) / np.float32(16))).astype(np.float32)
    ang = (pos[:, None] * inv[None, :]).astype(np.float32)
    rope_cs = np.concatenate([np.cos(ang), np.sin(ang)], axis=1).astype(np.float32)

    def log_count(dist, branches):
        c = sum(((dist >= 0) & (dist <= w) & (dist % d == 0)).astype(np.int64) for w, d in branches)
        return np.where(c > 0, 8 * np.log(np.maximum(c, 1)), -1e30).astype(np.float32)

    dil = ((128, 1), (512, 4), (2048, 16))
    win = ((128, 1),)
    q = np.arange(P)[:, None]
    mask_b = log_count(q + (NT - 1) * P - np.arange((2 * NT - 1) * P)[None, :], dil)
    both = log_count(q + P - np.arange(2 * P)[None, :], win)
    own = np.where(np.arange(2 * P)[None, :] < P, np.float32(-1e30), both)
    mask_a = np.stack([own, both], axis=1).astype(np.float32)
    rows = np.concatenate([np.arange(896, 1024), np.arange(512, 896, 4), np.arange(0, 512, 16)])
    new = np.repeat(np.where(np.eye(NS) > 0, 8 * np.log(3.0), -1e30), HEADS, axis=0)
    mask_sb = np.concatenate([np.repeat(log_count(1024 - rows[None, :], dil), 64, axis=0), new], axis=1)
    new = np.repeat(np.where(np.eye(NS) > 0, 0.0, -1e30), HEADS, axis=0)
    mask_sa = np.concatenate([np.zeros((64, P)), new], axis=1)
    return {
        "ident": np.eye(P, dtype=np.float32), "rope_cs": rope_cs, "mask_b": mask_b, "mask_a": mask_a,
        "mask_sb": mask_sb.astype(np.float32), "mask_sa": mask_sa.astype(np.float32),
        "iota16": np.tile(np.arange(16, dtype=np.float32), (P, 1)),
        "eye8": np.tile(np.eye(8, dtype=np.float32)[None], (P, 1, 1)),
        "head_mask": np.repeat(np.eye(8, dtype=np.float32), HD, axis=1),
    }


_INS = ("x_all", "cache_swa", "cache_dil", "w_in", "sinks", "w_out", "w_q", "keys", "peer_u", "peer_v", "ident",
        "gain_cols", "gain_rows", "rope_cs", "mask_b", "mask_a", "mask_sb", "mask_sa", "iota16", "eye8", "head_mask")
_OUTS = (("y_p", (1024, 1024)), ("y_s", (8, 1024)), ("swa_p", (128, 256)), ("dil_p", (1024, 1024)),
         ("swa_s", (8, 128 * 256)), ("dil_s", (8, 1024, 1024)))


def kernel(x_prompt, x_sample, cache_swa_kv, cache_dil_kv, attn_norm, w_in, sinks, out_norm_a, out_norm_b,
           w_out, ffn_norm, peer_w_q, peer_sub_keys, peer_u, peer_v, final_norm):
    import numpy as np
    import concourse.bacc as bacc
    from concourse.bass_utils import run_bass_kernel_spmd

    def cols(g):
        return np.asarray(g).reshape(KD, P).T

    x_all = np.concatenate([np.asarray(x_prompt).reshape(NT * P, D), np.asarray(x_sample).reshape(NS, D),
                            np.zeros((P - NS, D), np.float32)])
    out_gain = np.concatenate([np.asarray(out_norm_a)[0], np.asarray(out_norm_b)[0]])
    arrays = {
        "x_all": x_all,
        "cache_swa": np.asarray(cache_swa_kv).reshape(NS, 128 * 256),
        "cache_dil": np.asarray(cache_dil_kv).reshape(NS, 1024, 1024),
        "w_in": np.asarray(w_in)[0], "sinks": np.asarray(sinks).reshape(1, HEADS), "w_out": np.asarray(w_out)[0],
        "w_q": np.asarray(peer_w_q)[0], "keys": np.asarray(peer_sub_keys).reshape(2 * HEADS, KEYS, P),
        "peer_u": np.asarray(peer_u)[0], "peer_v": np.asarray(peer_v)[0],
        "gain_cols": np.stack([cols(np.asarray(attn_norm)[0]), cols(out_gain)], axis=1),
        "gain_rows": np.stack([np.asarray(ffn_norm)[0].reshape(KD, P), np.asarray(final_norm).reshape(KD, P)],
                              axis=1),
        **tables(np),
    }
    nc = bacc.Bacc("TRN2", target_bir_lowering=False, num_devices=1)
    feeds, args = {}, []
    for name in _INS:
        a = np.ascontiguousarray(arrays[name])
        feeds[f"in_{name}"] = a
        args.append(nc.dram_tensor(f"in_{name}", a.shape, mybir.dt.from_np(a.dtype), kind="ExternalInput").ap())
    for name, shape in _OUTS:
        args.append(nc.dram_tensor(f"out_{name}", shape, F32, kind="ExternalOutput").ap())
    build(nc, *args)
    r = run_bass_kernel_spmd(nc, [feeds], core_ids=[0]).results[0]
    got = [np.asarray(r[f"out_{name}"]) for name, _ in _OUTS]
    return (got[0].reshape(1, 1024, 1024), got[1].reshape(8, 1, 1024), got[2].reshape(1, 1, 128, 2, 2, 64),
            got[3].reshape(1, 1, 1024, 2, 8, 64), got[4].reshape(1, 8, 128, 2, 2, 64),
            got[5].reshape(1, 8, 1024, 2, 8, 64))
```

```python
from contextlib import ExitStack

import concourse.bass as bass
from concourse import mybir

F32 = mybir.dt.float32
U32 = mybir.dt.uint32
I32 = mybir.dt.int32
ALU = mybir.AluOpType
ACT = mybir.ActivationFunctionType
AX_X = mybir.AxisListType.X

P = 128
D = 1024
NT = 8
ROWS = (NT + 1) * P
NS = 8
KD = D // P
HD = 64
D_IN = 2304
HEADS = 8
KEYS = 128
TOPK = 16
EPS = 1e-6
NEG = -3.0e38
GELU_C = 0.7978845608028654
QA, KVA, QB, KB, VB_, END = 0, 512, 768, 1280, 1792, 2304
CHUNKS = ((QA, 512), (KVA, 256), (QB, 512), (KB, 512), (VB_, 512))
RING = 4
WO_SLOTS = 2
MAGIC = float(0x5F3759DF)


def build(nc, x_all, cache_swa, cache_dil, w_in, sinks, w_out, w_q, keys, peer_u, peer_v,
          ident, gain_cols, gain_rows, final_gain, rope_cs, mask_b, mask_a, mask_sb, mask_sa, iota16, eye8, head_mask,
          y_p, y_s, swa_p, dil_p, swa_s, dil_s):
    ds = bass.ds
    with ExitStack() as ctx:
        def sb(name, shape, dt=F32):
            return ctx.enter_context(nc.sbuf_tensor(name, shape, dt))

        def pb(name, shape):
            return ctx.enter_context(nc.psum_tensor(name, shape, F32))

        producers, starts, names, kept = {}, {}, {}, []

        def sem(name, producer=None, start=1):
            s = ctx.enter_context(nc.semaphore(name))
            if producer:
                producers.setdefault(producer, []).append((s, start))
                starts[name] = start
                names[id(s)] = name
                kept.append(s)
            return s

        def after(s, n):
            return n + starts.get(names.get(id(s)), 0)

        def scratch(name, shape):
            return nc.dram_tensor(name, shape, F32, kind="Internal").ap()

        qT_scr = scratch("qT_scr", (8, P, ROWS))
        kTA_scr = scratch("kTA_scr", (P, ROWS))
        kvA_scr = scratch("kvA_scr", (ROWS, 256))
        zS_scr = scratch("zS_scr", (NS, D_IN))
        oS_scr = scratch("oS_scr", (NS, D))

        wbuf = sb("wbuf", [P, KD * D_IN])
        w_in_sb = wbuf[:, :].rearrange("p (k n) -> p k n", k=KD)
        wq_sb = wbuf[:, 0:KD * 2048].rearrange("p (k n) -> p k n", k=KD)
        keysT = wbuf[:, KD * 2048:].rearrange("p (h k) -> p h k", h=2 * HEADS)
        KTB = sb("KTB", [P, 4, D])
        VB = sb("VB", [P, NT, 512])
        ring = sb("ring", [P, 2 * RING, D])
        u_ring = [ring[:, i, :] for i in range(RING)]
        v_ring = [ring[:, RING + i, :] for i in range(RING)]
        hpair = sb("hpair", [P, 2, D])
        h_cur, h_next = hpair[:, 0, :], hpair[:, 1, :]
        x2 = sb("x2", [P, D])
        o_all = sb("o_all", [P, D])
        TT = sb("TT", [P, KD, P])
        S = sb("S", [P, D + 256])
        S_B, S_A = S[:, 0:D], S[:, D:D + 256]
        PT = sb("PT", [P, 10, P])
        maskB = sb("maskB", [P, D])
        maskA = sb("maskA", [P, 2, 256])
        wo_sb = sb("wo_sb", [P, WO_SLOTS, D])
        ybuf = sb("ybuf", [P, D])
        fgain = sb("fgain", [P, D])
        idn = sb("idn", [P, P])
        diag = sb("diag", [P, 4, P])
        qpad = sb("qpad", [P, 2, 2, P])
        kTA = sb("kTA", [P, 256])
        vA = sb("vA", [P, 2, P])
        gcol = sb("gcol", [P, 2, KD])
        grow = sb("grow", [KD, P])
        rcs = sb("rcs", [P, NT + 1, 16])
        sink = sb("sink", [P, HEADS])
        iota = sb("iota", [P, TOPK])
        e8 = sb("e8", [P, 8, 8])
        pq = sb("pq", [P, 256])
        pqT = sb("pqT", [P, 2, P])
        sc = sb("sc", [P, 2, P])
        topv = sb("topv", [P, 2, 2, TOPK])
        topi = sb("topi", [P, 2, 2, TOPK], U32)
        topif = sb("topif", [P, 2, 2, TOPK])
        cand = sb("cand", [P, TOPK, TOPK])
        candv = sb("candv", [P, 2, TOPK])
        candp = sb("candp", [P, 2, TOPK], U32)
        candh = sb("candh", [P, 2, TOPK], U32)
        candf = sb("candf", [P, 2, TOPK])
        onehot = sb("onehot", [P, 2, TOPK, TOPK])
        sel = sb("sel", [P, 2, 2, TOPK])
        gexp = sb("gexp", [P, TOPK])
        idx_all = sb("idx_all", [P, P], U32)
        gates = sb("gates", [P, P])
        win_u = sb("win_u", [P, 2, TOPK], U32)
        win_v = sb("win_v", [P, 2, TOPK], U32)
        dots = sb("dots", [P, 2, TOPK])
        gl = sb("gl", [P, 3, TOPK])
        wv = sb("wv", [P, 2, TOPK])
        nw_x = sb("nw_x", [P, 2])
        nw_i = sb("nw_i", [P, 2], I32)
        nw_a = sb("nw_a", [P, 2])
        nw_b = sb("nw_b", [P, 2])
        nw_y = sb("nw_y", [P, 2])
        ssum = sb("ssum", [P, 2])
        amax = sb("amax", [P, 2])
        anm = sb("anm", [P, 2])
        aden = sb("aden", [P, 3])
        arden = sb("arden", [P, 2])
        gsm = sb("gsm", [P, 4])
        idxT = sb("idxT", [P, NS], U32)
        gateT = sb("gateT", [P, NS])
        dotsT = sb("dotsT", [P, NS])
        wz = sb("wz", [P, NS, 8])

        xin = ring[:, 0, :]
        xs = ring[:, 1, :]
        z = ring[:, 2:5, :].rearrange("p a n -> p (a n)")[:, 0:D_IN]
        rtmp = ring[:, 5, :]
        qTe = ring[:, 6, :].rearrange("p (b n) -> p b n", b=8)
        kTAe = ring[:, 7, 0:P]
        s_k = [ring[:, i, :].rearrange("p (s n) -> p s n", s=2) for i in range(2)]
        s_q = [ring[:, 2 + i, :] for i in range(2)]
        s_kA = [ring[:, 4, i * P:(i + 1) * P] for i in range(2)]
        s_v = [ring[:, 5 + i, :].rearrange("p (s n) -> p s n", s=2) for i in range(2)]
        s_vA = [ring[:, 7, i * P:(i + 1) * P] for i in range(2)]
        s_new = PT[:, :, :].rearrange("p a n -> p (a n)")
        s_prod = TT[:, :, :].rearrange("p a n -> p (a n)")
        s_sc = S[:, 0:192].rearrange("p (s n) -> p s n", s=3)
        s_scn = S[:, 192:320].rearrange("p (s n) -> p s n", s=2)
        s_pB, s_pA = S[:, 320:584], S[:, 584:720]
        s_pT = S[:, 720:912].rearrange("p (s n) -> p s n", s=3)
        s_pTn = S[:, 912:1040].rearrange("p (s n) -> p s n", s=2)
        s_mB, s_mA = maskB[0:64, 0:264], maskB[0:64, 264:400]
        s_hm = maskB[0:8, 512:1024]
        s_sink = gsm[0:64, 3:4]
        s_od = [ybuf[0:8, :], x2[0:8, :]]
        s_o = o_all[0:8, :]

        acc = pb("acc", [P, D])
        pS = pb("pS", [P, D])
        pA = pb("pA", [P, 512])
        pT = pb("pT", [P, D])
        pM = pb("pM", [P, 512])
        zbank = (pS[:, 0:512], pS[:, 512:768], pA[:, :], pT[:, 0:512], pT[:, 512:1024])

        c_in = sem("c_in")
        win_in = [sem(f"win_in{i}") for i in range(5)]
        x_in = sem("x_in")
        z_out = sem("z_out", "sp")
        q_out = sem("q_out", "sp")
        cache_out = sem("cache_out")
        wq_in = sem("wq_in")
        keys_in = sem("keys_in")
        snew_in = sem("snew_in")
        sconst_in = sem("sconst_in")
        sk_in = [sem(f"sk_in{i}") for i in range(2)]
        sv_in = [sem(f"sv_in{i}") for i in range(2)]
        so_out = sem("so_out")
        so_in = sem("so_in")
        newrow_out = sem("newrow_out")
        att_in = sem("att_in")
        qT_in = [sem(f"qT_in{i}") for i in range(2)]
        mx_in = sem("mx_in")
        wo_in = [sem(f"wo_in{i}") for i in range(WO_SLOTS)]
        y_out = sem("y_out", "sp")
        u_in = [sem(f"u_in{i}") for i in range(RING)]
        v_in = [sem(f"v_in{i}") for i in range(RING)]
        swa_out = sem("swa_out")

        a_xs = sem("a_xs", "dve")
        a_xT = sem("a_xT", "dve")
        a_rope = sem("a_rope", "dve")
        a_xt = sem("a_xt", "pe")
        a_z = sem("a_z", "pe")
        a_rt = sem("a_rt", "pe")
        a_ze = sem("a_ze", "act")
        a_te = sem("a_te", "act")
        a_vb = sem("a_vb", "pool")
        pads = sem("pads", "dve")
        k_t = sem("k_t", "pe")
        k_te = sem("k_te", "act")
        s_mul = sem("s_mul", "dve", 2)
        s_sT = sem("s_sT", "pe")
        s_max = sem("s_max", "dve")
        s_exp = sem("s_exp", "act")
        s_prob = sem("s_prob", "dve")
        s_bT = sem("s_bT", "pe")
        s_bTe = sem("s_bTe", "act")
        s_pv = sem("s_pv", "pe")
        s_dg = sem("s_dg", "dve")
        s_fold = sem("s_fold", "pe")
        s_done = sem("s_done", "dve")
        att_s = sem("att_s", "pe", 2)
        att_max = sem("att_max", "dve")
        att_exp = sem("att_exp", "act")
        att_t = sem("att_t", "pe")
        att_te = sem("att_te", "act")
        att_pv = sem("att_pv", "pe")
        att_o = sem("att_o", "dve")
        mx_on = sem("mx_on", "dve")
        mx_t = sem("mx_t", "pe")
        mx_onT = sem("mx_onT", "dve")
        wo_used = sem("wo_used", "pe", WO_SLOTS)
        mx_mm = sem("mx_mm", "pe")
        mx_x2 = sem("mx_x2", "dve")
        mx_h = sem("mx_h", "dve")
        mx_ht = sem("mx_ht", "pe")
        mx_hT = sem("mx_hT", "act")
        pr_q = sem("pr_q", "pe")
        pr_qe = sem("pr_qe", "act")
        pr_t = sem("pr_t", "pe")
        pr_te = sem("pr_te", "act")
        pr_s = sem("pr_s", "pe")
        pr_se = sem("pr_se", "act")
        pr_read = sem("pr_read", "dve")
        pr_top = sem("pr_top", "dve")
        pr_exp = sem("pr_exp", "act")
        pr_idx = sem("pr_idx", "dve")
        win_set = sem("win_set", "pool")
        win_cp = sem("win_cp", "pool")
        gl_in = sem("gl_in", "dve")
        gl_th = sem("gl_th", "act")
        w_set = sem("w_set", "dve")
        diag_set = sem("diag_set", "act")
        u_used = sem("u_used", "dve", RING)
        v_used = sem("v_used", "pe", RING)
        acc_init = sem("acc_init", "pe")
        fin_y = sem("fin_y", "dve")
        fin_free = sem("fin_free", "act")
        gs_t = sem("gs_t", "pe")
        gs_idx = sem("gs_idx", "dve")
        gs_h = sem("gs_h", "pe")
        gs_in = sem("gs_in", "dve")
        gs_th = sem("gs_th", "act")
        gs_w = sem("gs_w", "dve")

        steps = {who: ctx.enter_context(nc.semaphore(f"{who}_step")) for who in ("sp", "pool", "dve")}

        def hold(eng, who, s, n):
            eng.wait_ge(s, after(s, n))
            eng.sem_inc(steps[who], 1)

        def set_starts(eng, who):
            for s, start in producers[who]:
                eng.sem_inc(s, start)

        def repeat(eng, start, end):
            return eng.Fori(start, end)

        def tiles_of(t):
            if not isinstance(t, int):
                return t, t + 1, t + 2
            return (t if 0 <= t < NT else None, t + 1 if 0 <= t + 1 <= NT else None,
                    t + 2 if t + 2 < NT else None)

        def place(p, par):
            return 2 * p + par if isinstance(p, int) else None

        def back(p, par, n):
            half = (par - n) % 2
            pair = p + (par - n - half) // 2
            return (pair % 4 if isinstance(p, int) else pair), half

        def has_next(t):
            return not isinstance(t, int) or t + 2 <= NT

        def begun(t):
            return not isinstance(t, int) or t >= 0

        def exists(t, p, par, n):
            if not isinstance(t, int) or t >= -1 and not isinstance(p, int):
                return True
            return t >= -1 and 0 <= 8 * (t + 1) + 2 * p + par - n < 8 * (NT + 1)

        def iteration(eng, section, t):
            section(t, 0, 0)
            section(t, 0, 1)
            with repeat(eng, 1, 3) as p:
                section(t, p, 0)
                section(t, p, 1)
            section(t, 3, 0)
            section(t, 3, 1)

        def iterations(eng, section):
            iteration(eng, section, -2)
            iteration(eng, section, -1)
            iteration(eng, section, 0)
            with repeat(eng, 1, NT - 2) as t:
                iteration(eng, section, t)
            iteration(eng, section, NT - 2)
            iteration(eng, section, NT - 1)

        block = ctx.enter_context(nc.Block())

        @block.sync
        def _(sp):
            set_starts(sp, "sp")
            sp.dma_start(xin, x_all[0:P, :]).then_inc(x_in, 16)
            consts = [(idn[:, :], ident), (gcol[:, :, :], gain_cols), (grow[:, :], gain_rows), (fgain[:, :], final_gain.broadcast_to([P, D])),
                      (rcs[:, :, :], rope_cs.rearrange("(t p) c -> p t c", p=P)), (maskA[:, :, :], mask_a),
                      (sink[:, :], sinks.broadcast_to([P, HEADS])), (iota[:, :], iota16), (e8[:, :, :], eye8)]
            for dst, src in consts:
                sp.dma_start(dst, src).then_inc(c_in, 16)
            w_in_v = w_in.rearrange("(k p) n -> p k n", p=P)
            for n, (c0, w) in enumerate(CHUNKS):
                sp.dma_start(w_in_sb[:, :, c0:c0 + w], w_in_v[:, :, c0:c0 + w]).then_inc(win_in[n], 16)

            def cache_copy(r):
                n = 1023 * D
                src = cache_dil[ds(r, 1)].rearrange("r s n -> r (s n)")[:, D:D + n]
                dst = dil_s[ds(r, 1)].rearrange("r s n -> r (s n)")[:, 0:n]
                sp.dma_start(dst.rearrange("r (a b) -> (r a) b", a=176),
                             src.rearrange("r (a b) -> (r a) b", a=176)).then_inc(cache_out, 16)

            with repeat(sp, 0, NT) as t:
                hold(sp, "sp", a_xs, t + 1)
                sp.dma_start(xin, x_all[ds((t + 1) * P, P), :]).then_inc(x_in, 16)
                cache_copy(t)
                hold(sp, "sp", a_ze, 5 * t + 5)
                hold(sp, "sp", a_rope, 2 * t + 2)
                sp.dma_start(dil_p[ds(t * P, P), :], z[:, KB:END]).then_inc(z_out, 16)
                sp.dma_start(kvA_scr[ds(t * P, P), :], z[:, KVA:QB]).then_inc(z_out, 16)
                hold(sp, "sp", a_te, 4 * t + 4)
                sp.dma_start(qT_scr[:, :, ds(t * P, P)].rearrange("b p n -> p b n"), qTe).then_inc(q_out, 16)
                sp.dma_start(kTA_scr[:, ds(t * P, P)], kTAe).then_inc(q_out, 16)
            sp.dma_start(swa_s[:, 0:127 * 256].rearrange("r (a b) -> r a b", a=16),
                         cache_swa[:, 256:].rearrange("r (a b) -> r a b", a=16)).then_inc(cache_out, 16)
            hold(sp, "sp", a_ze, 5 * NT + 5)
            hold(sp, "sp", a_rope, 2 * NT + 2)
            sp.dma_start(zS_scr, z[0:NS, :]).then_inc(z_out, 16)
            sp.dma_start(dil_s[:, 1023, :], z[0:NS, KB:END]).then_inc(newrow_out, 16)
            sp.dma_start(swa_s[:, 127 * 256:], z[0:NS, KVA:QB]).then_inc(newrow_out, 16)
            hold(sp, "sp", a_z, 5 * NT + 5)
            hold(sp, "sp", a_vb, NT)
            sp.dma_start(hpair[:, :, :].rearrange("p a n -> p (a n)").rearrange("p (h d) -> p h d", d=P),
                         keys.rearrange("h k d -> k h d")).then_inc(keys_in, 16)

            sp.dma_start(s_mB, mask_sb).then_inc(sconst_in, 16)
            sp.dma_start(s_mA, mask_sa).then_inc(sconst_in, 16)
            sp.dma_start(s_hm, head_mask).then_inc(sconst_in, 16)
            for r in range(NS):
                sp.dma_start(gsm[r * 8:r * 8 + 8, 3:4], sinks.rearrange("a h -> h a")).then_inc(sconst_in, 16)
            hold(sp, "sp", z_out, 32 * NT + 16)
            hold(sp, "sp", q_out, 32 * NT)
            sp.wait_ge(newrow_out, 32)
            sp.dma_start(s_new[0:8, 0:256], zS_scr[:, KVA:QB]).then_inc(snew_in, 16)
            sp.dma_start(s_new[0:8, 256:1280], zS_scr[:, KB:END]).then_inc(snew_in, 16)

            def cache_rows(dst, r, k_or_v):
                c = cache_dil[ds(r, 1), :, k_or_v * 512:k_or_v * 512 + 512].rearrange("r s n -> (r s) n")
                yield dst[:, 0, :], c[896:1024, :]
                yield dst[0:96, 1, :], c[512:896:4, :]
                yield dst[96:128, 1, :], c[0:512:16, :]

            with repeat(sp, 0, NS // 2) as i:
                for b in range(2):
                    r = 2 * i + b
                    hold(sp, "sp", s_mul, r - 1)
                    for dst, src in cache_rows(s_k[b], r, 0):
                        sp.dma_start(dst, src).then_inc(sk_in[b], 16)
                    sp.dma_start(s_kA[b], cache_swa[ds(r, 1), :].rearrange("r (s n) -> (r s) n", n=256)[:, 0:P])\
                      .then_inc(sk_in[b], 16)
                    sp.dma_start(s_q[b][:, 0:512], zS_scr[ds(r, 1), QA:KVA].broadcast_to([P, 512]))\
                      .then_inc(sk_in[b], 16)
                    sp.dma_start(s_q[b][:, 512:1024], zS_scr[ds(r, 1), QB:KB].broadcast_to([P, 512]))\
                      .then_inc(sk_in[b], 16)
            sp.dma_start(wq_sb[:, :, :], w_q.rearrange("(k p) n -> p k n", p=P)).then_inc(wq_in, 16)
            for r in range(NS):
                b = r % 2
                if r >= 2:
                    hold(sp, "sp", s_pv, r - 1)
                for dst, src in cache_rows(s_v[b], r, 1):
                    sp.dma_start(dst, src).then_inc(sv_in[b], 16)
                sp.dma_start(s_vA[b], cache_swa[r, :].rearrange("(s n) -> s n", n=256)[:, P:256])\
                  .then_inc(sv_in[b], 16)
            hold(sp, "sp", s_done, 1)
            sp.dma_start(oS_scr, s_o).then_inc(so_out, 16)
            sp.dma_start(swa_p, kvA_scr[(NT - 1) * P:NT * P, :]).then_inc(swa_out, 16)
            sp.wait_ge(so_out, 16)

            def att_tile(t):
                first = isinstance(t, int) and t == 0
                if not first:
                    hold(sp, "sp", att_s, 8 * t)
                    hold(sp, "sp", att_max, 8 * t)
                    hold(sp, "sp", att_pv, 8 * t)
                sp.dma_start(maskB[:, :], mask_b[:, ds((NT - 1 - t) * P, D)]).then_inc(att_in, 16)
                if first:
                    sp.dma_start(kTA[:, P:256], kTA_scr[:, 0:P]).then_inc(att_in, 16)
                    sp.dma_start(vA[:, 1, :], kvA_scr[0:P, P:256]).then_inc(att_in, 16)
                else:
                    sp.dma_start(kTA[:, :], kTA_scr[:, ds((t - 1) * P, 256)]).then_inc(att_in, 16)
                    sp.dma_start(vA[:, :, :], kvA_scr[ds((t - 1) * P, 256), P:256].rearrange(
                        "(b p) n -> p b n", p=P)).then_inc(att_in, 16)

            def att_q(t, p, par):
                hold(sp, "sp", att_s, 8 * t + 2 * p + par - 1)
                rows = slice(64 * par, 64 * par + 64)
                src = qT_scr.rearrange("(m b) r n -> b r m n", m=2)[ds(p, 1), rows, :, ds(t * P, P)]
                sp.dma_start(qpad[rows, par, :, :], src.rearrange("b r m n -> (b r) m n")).then_inc(qT_in[par], 16)

            wo_v = w_out.rearrange("(k p) n -> k p n", p=P)

            def w_out_chunks(t, chunks):
                for k in chunks:
                    hold(sp, "sp", wo_used, KD * t + k + 1 - WO_SLOTS)
                    sp.dma_start(wo_sb[:, k % WO_SLOTS, :], wo_v[k]).then_inc(wo_in[k % WO_SLOTS], 16)

            def loads(t):
                _, tp, ta = tiles_of(t)
                if ta is not None:
                    att_tile(ta)
                    att_q(ta, 0, 0)
                    att_q(ta, 0, 1)
                if tp is not None:
                    if begun(t):
                        hold(sp, "sp", acc_init, tp)
                    sp.dma_start(x2[:, :], x_all[ds(tp * P, P), :]).then_inc(mx_in, 16)
                    w_out_chunks(tp, range(WO_SLOTS, KD))
                if not (isinstance(t, int) and t == NT - 1):
                    w_out_chunks(t + 2, range(WO_SLOTS))
                if not isinstance(t, int) or t >= 1:
                    store_y(t - 1)
                if ta is not None:
                    with repeat(sp, 1, 4) as p:
                        att_q(ta, p, 0)
                        att_q(ta, p, 1)

            def store_y(t):
                hold(sp, "sp", fin_y, t + 1)
                sp.dma_start(y_p[ds(t * P, P), :], ybuf[:, :]).then_inc(y_out, 16)

            hold(sp, "sp", pads, 1)
            loads(-2)
            loads(-1)
            loads(0)
            with repeat(sp, 1, NT - 2) as t:
                loads(t)
            hold(sp, "sp", mx_on, NT)
            sp.dma_start(o_all[0:NS, :], oS_scr).then_inc(so_in, 16)
            loads(NT - 2)
            loads(NT - 1)
            store_y(NT - 1)
            hold(sp, "sp", fin_y, NT + 1)
            sp.dma_start(y_s, ybuf[0:NS, :]).then_inc(y_out, 16)
            hold(sp, "sp", y_out, 16 * (NT + 1))
            sp.wait_ge(cache_out, 16 * (NT + 1))
            sp.wait_ge(swa_out, 16)

        @block.gpsimd
        def _(pool):
            set_starts(pool, "pool")
            with repeat(pool, 0, NT) as t:
                hold(pool, "pool", a_ze, 5 * t + 5)
                pool.tensor_copy(VB[:, ds(t, 1), :].rearrange("p t n -> p (t n)"), z[:, VB_:END]).then_inc(a_vb, 1)

            def fetch(buf, table, win, landed):
                pool.indirect_dma_start(buf, None, table, bass.IndirectOffsetOnAxis(win, 0)).then_inc(landed, 16)

            def section(t, p, par, last=False):
                head = 2 * p + par
                s = 8 * t + head
                nxt = s + 1
                pool.tensor_copy(win_v[:, par, :], win_u[:, par, :]).then_inc(win_cp, 1)
                if not last:
                    hold(pool, "pool", pr_idx, 4 * t + p + 1 + par)
                    col = 0 if isinstance(p, int) and p == 3 and par == 1 else (head + 1) * TOPK
                    pool.tensor_copy(win_u[:, 1 - par, :], idx_all[:, ds(col, TOPK)]).then_inc(win_set, 1)
                    hold(pool, "pool", win_set, nxt + 1)
                hold(pool, "pool", win_cp, s + 1)
                for j in range(TOPK):
                    if not last:
                        hold(pool, "pool", u_used, TOPK * nxt + j - RING + 1)
                        fetch(u_ring[j % RING], peer_u, win_u[:, 1 - par, j:j + 1], u_in[j % RING])
                    hold(pool, "pool", v_used, TOPK * s + j - RING + 1)
                    fetch(v_ring[j % RING], peer_v, win_v[:, par, j:j + 1], v_in[j % RING])

            hold(pool, "pool", pr_idx, 1)
            pool.tensor_copy(win_u[:, 0, :], idx_all[:, 0:TOPK]).then_inc(win_set, 1)
            hold(pool, "pool", win_set, 1)
            for j in range(TOPK):
                hold(pool, "pool", u_used, j - RING + 1)
                fetch(u_ring[j % RING], peer_u, win_u[:, 0, j:j + 1], u_in[j % RING])
            with repeat(pool, 0, NT - 1) as t:
                with repeat(pool, 0, 3) as p:
                    section(t, p, 0)
                    section(t, p, 1)
                section(t, 3, 0)
                section(t, 3, 1)
            with repeat(pool, 0, 3) as p:
                section(NT - 1, p, 0)
                section(NT - 1, p, 1)
            section(NT - 1, 3, 0)
            section(NT - 1, 3, 1, last=True)
            hold(pool, "pool", gs_idx, 1)
            for r in range(NS):
                n = TOPK * HEADS * NT + r
                hold(pool, "pool", u_used, n - RING + 1)
                fetch(u_ring[r % RING], peer_u, idxT[:, r:r + 1], u_in[r % RING])
            for r in range(NS):
                n = TOPK * HEADS * NT + r
                hold(pool, "pool", v_used, n - RING + 1)
                fetch(v_ring[r % RING], peer_v, idxT[:, r:r + 1], v_in[r % RING])

        @block.tensor
        def _(pe):
            set_starts(pe, "pe")

            def x_transposes(t):
                pe.wait_ge(a_xs, after(a_xs, t + 1))
                for k in range(KD):
                    m = pe.transpose(acc[:, k * P:(k + 1) * P], xs[:, k * P:(k + 1) * P], idn[:, :])
                m.then_inc(a_xt, 1)

            def z_chunk(t, c, first=False):
                c0, w = CHUNKS[c]
                if first:
                    pe.wait_ge(win_in[c], 16)
                if c == 0:
                    pe.wait_ge(a_xT, after(a_xT, t + 1))
                    pe.wait_ge(a_ze, after(a_ze, 5 * t))
                if c == 1:
                    pe.wait_ge(a_te, after(a_te, 4 * t))
                for k in range(KD):
                    m = pe.matmul(zbank[c][:, 0:w], TT[:, k, :], w_in_sb[:, k, c0:c0 + w],
                                  start=(k == 0), stop=(k == KD - 1))
                m.then_inc(a_z, 1)

            def qk_transposes(t):
                pe.wait_ge(a_rope, after(a_rope, 2 * t + 2))
                pe.wait_ge(a_ze, after(a_ze, 5 * t + 4))
                for b in range(4):
                    m = pe.transpose(pS[:, 512 + b * P:512 + (b + 1) * P], z[:, b * P:(b + 1) * P], idn[:, :])
                m.then_inc(a_rt, 1)
                for b in range(4):
                    m = pe.transpose(pA[:, b * P:(b + 1) * P], z[:, QB + b * P:QB + (b + 1) * P], idn[:, :])
                m.then_inc(a_rt, 1)
                for b in range(4):
                    m = pe.transpose(pM[:, b * P:(b + 1) * P], z[:, KB + b * P:KB + (b + 1) * P], idn[:, :])
                m.then_inc(a_rt, 1)
                pe.transpose(pT[:, 0:P], z[:, KVA:KVA + P], idn[:, :]).then_inc(a_rt, 1)

            def project(t, first=False, last=False):
                z_chunk(t, 0, first)
                z_chunk(t, 1, first)
                if not last:
                    x_transposes(t + 1)
                for c in (2, 3, 4):
                    z_chunk(t, c, first)
                if not last:
                    qk_transposes(t)

            pe.wait_ge(c_in, 16 * 9)
            x_transposes(0)
            project(0, first=True)
            with repeat(pe, 1, NT) as t:
                project(t)
            project(NT, last=True)

            pe.wait_ge(keys_in, 16)
            pe.wait_ge(a_ze, after(a_ze, 5 * NT + 5))
            pe.wait_ge(a_te, after(a_te, 4 * NT))
            for b in range(2):
                if b:
                    pe.wait_ge(k_te, after(k_te, 1))
                for k in range(8):
                    m = pe.transpose(pT[:, k * P:(k + 1) * P], hpair[:, b, k * P:(k + 1) * P], idn[:, :])
                m.then_inc(k_t, 1)

            pe.wait_ge(s_mul, after(s_mul, NS))
            pe.transpose(pS[0:64, 0:P], s_sc[:, 0, :], idn[:, :])
            pe.transpose(pS[0:64, P:2 * P], s_sc[:, 1, :], idn[:, :])
            pe.transpose(pS[0:64, 256:264], s_scn[0:8, 0, :], idn[0:8, 0:8])
            pe.transpose(pS[0:64, 512:640], s_sc[:, 2, :], idn[:, :])
            pe.transpose(pS[0:64, 640:648], s_scn[0:8, 1, :], idn[0:8, 0:8]).then_inc(s_sT, 1)
            pe.wait_ge(s_prob, after(s_prob, 1))
            pe.wait_ge(k_te, after(k_te, 2))
            i64 = idn[0:64, 0:64]
            pe.transpose(pT[:, 0:64], s_pB[0:64, 0:P], i64)
            pe.transpose(pT[:, 64:128], s_pB[0:64, P:2 * P], i64)
            pe.transpose(pT[:, 128:192], s_pA[0:64, 0:P], i64)
            pe.transpose(pT[0:8, 192:256], s_pB[0:64, 256:264], i64)
            pe.transpose(pT[0:8, 256:320], s_pA[0:64, P:136], i64).then_inc(s_bT, 1)

            def sample_pv(r):
                b, bank = r % 2, (pS, pT)[r % 2]
                if r == 0:
                    pe.wait_ge(s_bTe, after(s_bTe, 1))
                if r >= 2:
                    pe.wait_ge(s_dg, after(s_dg, r - 1))
                pe.wait_ge(sv_in[b], 64 * (r // 2 + 1))
                c = slice(8 * r, 8 * r + 8)
                pe.matmul(bank[0:8, 0:512], s_pT[:, 0, c], s_v[b][:, 0, :], start=True, stop=False)
                pe.matmul(bank[0:8, 0:512], s_pT[:, 1, c], s_v[b][:, 1, :], start=False, stop=False)
                pe.matmul(bank[0:8, 0:512], s_pTn[0:8, 0, c], s_new[0:8, 768:1280], start=False, stop=True)
                pe.matmul(bank[0:8, 512:640], s_pT[:, 2, c], s_vA[b], start=True, stop=False)
                pe.matmul(bank[0:8, 512:640], s_pTn[0:8, 1, c], s_new[0:8, P:256],
                          start=False, stop=True).then_inc(s_pv, 1)

            def sample_fold(r):
                pe.wait_ge(s_dg, after(s_dg, r + 1))
                for half in range(2):
                    m = pe.matmul(acc[0:8, half * 512:(half + 1) * 512], e8[0:8, r, :],
                                  s_od[r % 2][:, half * 512:(half + 1) * 512], start=(r == 0), stop=(r == NS - 1))
                m.then_inc(s_fold, 1)

            sample_pv(0)
            for r in range(NS):
                if r + 1 < NS:
                    sample_pv(r + 1)
                sample_fold(r)

            def att_scores(t, p, par):
                a = 8 * t + 2 * p + par
                if place(p, par) == 0:
                    pe.wait_ge(att_in, 48 * (t + 1))
                    if begun(t - 1):
                        pe.wait_ge(mx_x2, after(mx_x2, t))
                pe.wait_ge(qT_in[par], 16 * (4 * t + p + 1))
                pe.wait_ge(att_max, after(att_max, a))
                pe.wait_ge(att_te, after(att_te, 3 * a))
                for half in range(2):
                    pe.matmul(pS[:, half * 512:(half + 1) * 512], qpad[:, par, 1, :],
                              KTB[:, ds(p, 1), half * 512:(half + 1) * 512], start=True, stop=True)
                pe.matmul(pA[:, 0:256], qpad[:, par, 0, :], kTA[:, :], start=True, stop=True).then_inc(att_s, 1)

            def att_transposes(t, p, par):
                a = 8 * t + 2 * p + par
                pe.wait_ge(att_exp, after(att_exp, a + 1))
                if place(p, par) == 0 and begun(t - 1):
                    pe.wait_ge(mx_hT, after(mx_hT, t))
                for half in range(2):
                    for k in range(4 * half, 4 * half + 4):
                        m = pe.transpose(pT[:, k * P:(k + 1) * P], S_B[:, k * P:(k + 1) * P], idn[:, :])
                    m.then_inc(att_t, 1)
                for k in range(2):
                    m = pe.transpose(pA[:, 256 + k * P:256 + (k + 1) * P], S_A[:, k * P:(k + 1) * P], idn[:, :])
                m.then_inc(att_t, 1)

            def att_values(t, p, par):
                a = 8 * t + 2 * p + par
                pe.wait_ge(att_te, after(att_te, 3 * a + 3))
                if place(p, par) == 0:
                    if exists(t - 2, p, par, 1):
                        pe.wait_ge(pr_se, after(pr_se, 8 * (t - 1)))
                elif exists(t - 2, p, par, 1):
                    pe.wait_ge(pr_qe, after(pr_qe, a - 8))
                for k in range(NT):
                    pe.matmul(pM[:, 256:320], PT[:, k, :],
                              VB[:, k, ds(p * P + par * HD, HD)], start=(k == 0), stop=(k == NT - 1))
                for k in range(2):
                    m = pe.matmul(pM[:, 320:384], PT[:, 8 + k, :], vA[:, k, par * HD:(par + 1) * HD],
                                  start=(k == 0), stop=(k == 1))
                m.then_inc(att_pv, 1)

            def out_transposes(t):
                pe.wait_ge(mx_on, after(mx_on, t + 1))
                for k in range(KD):
                    m = pe.transpose(pT[:, k * P:(k + 1) * P], S[:, k * P:(k + 1) * P], idn[:, :])
                m.then_inc(mx_t, 1)

            def out_projection(t, k):
                if k == 0:
                    pe.wait_ge(mx_onT, after(mx_onT, t + 1))
                pe.wait_ge(wo_in[k % WO_SLOTS], 16 * ((KD // WO_SLOTS) * t + k // WO_SLOTS + 1))
                for half in range(2):
                    m = pe.matmul(pS[:, half * 512:(half + 1) * 512], PT[:, k, :],
                                  wo_sb[:, k % WO_SLOTS, half * 512:(half + 1) * 512],
                                  start=(k == 0), stop=(k == KD - 1))
                m.then_inc(wo_used, 1)

            def h_gain():
                for k in range(KD):
                    m = pe.matmul(pT[:, k * P:(k + 1) * P], idn[0:KD, k:k + 1].broadcast_to([KD, P]),
                                  grow[0:KD, :], start=True, stop=True)
                m.then_inc(mx_mm, 1)

            def h_transposes(t):
                pe.wait_ge(mx_h, after(mx_h, t + 1))
                for k in range(KD):
                    m = pe.transpose(pT[:, k * P:(k + 1) * P], h_next[:, k * P:(k + 1) * P], idn[:, :])
                m.then_inc(mx_ht, 1)

            def peer_query(t, b, p, par, att):
                pe.wait_ge(mx_hT, after(mx_hT, t + 1))
                pe.wait_ge(pr_se, after(pr_se, b))
                pe.wait_ge(att_o, after(att_o, att))
                for k in range(KD):
                    m = pe.matmul(pM[:, 0:256], TT[:, k, :], wq_sb[:, k, ds(p * 512 + par * 256, 256)],
                                  start=(k == 0), stop=(k == KD - 1))
                m.then_inc(pr_q, 1)

            def peer_transposes(b, att):
                pe.wait_ge(pr_qe, after(pr_qe, b + 1))
                pe.wait_ge(att_te, after(att_te, 3 * att))
                for k in range(2):
                    m = pe.transpose(pA[:, k * P:(k + 1) * P], pq[:, k * P:(k + 1) * P], idn[:, :])
                m.then_inc(pr_t, 1)

            def peer_scores(b, p, par, att):
                pe.wait_ge(pr_te, after(pr_te, b + 1))
                pe.wait_ge(att_o, after(att_o, att))
                for k in range(2):
                    m = pe.matmul(pM[:, k * P:(k + 1) * P], pqT[:, k, :],
                                  keysT[:, ds(4 * p + 2 * par + k, 1), :], start=True, stop=True)
                m.then_inc(pr_s, 1)

            def weigh(s, j):
                n = TOPK * s + j
                pe.wait_ge(diag_set, after(diag_set, n + 1))
                pe.wait_ge(v_in[j % RING], 16 * (4 * s + j // RING + 1))
                for half in range(2):
                    m = pe.matmul(acc[:, half * 512:(half + 1) * 512], diag[:, j % 4, :],
                                  v_ring[j % RING][:, half * 512:(half + 1) * 512],
                                  start=False, stop=False, skip_group_check=True)
                m.then_inc(v_used, 1)

            def acc_start(t, rows=P):
                pe.wait_ge(mx_h, after(mx_h, t + 1))
                if not (isinstance(t, int) and t == 0):
                    pe.wait_ge(fin_free, after(fin_free, t))
                for half in range(2):
                    m = pe.matmul(acc[0:rows, half * 512:(half + 1) * 512], idn[:, 0:rows],
                                  x2[:, half * 512:(half + 1) * 512], start=True, stop=False,
                                  skip_group_check=True)
                m.then_inc(acc_init, 1)

            def section(t, p, par):
                tg, tp, ta = tiles_of(t)
                h = place(p, par)
                b = 8 * (t + 1) + 2 * p + par - 1
                peer = exists(t, p, par, 1)
                of_peer = t if h == 0 else t + 1
                before = NT * 8 if ta is None else 8 * ta + 2 * p + par
                att = before if ta is None or h == 0 else before + 1
                out = t + 2 if h == 7 and has_next(t) else None
                s_, t_, v_ = (9, 13, 15) if h == 0 else (0, 5, 8)
                q_, qt_, qs_ = (0, 3, 5) if h == 0 else (2, 9, 12)
                if h == 0 and tg is not None:
                    acc_start(tg)
                for j in range(TOPK):
                    if peer and j == q_:
                        peer_query(of_peer, b, *back(p, par, 1), before)
                    if ta is not None and j == s_:
                        att_scores(ta, p, par)
                    if ta is not None and j == t_:
                        att_transposes(ta, p, par)
                    if ta is not None and j == v_:
                        att_values(ta, p, par)
                    if peer and j == qt_:
                        peer_transposes(b, att)
                    if peer and j == qs_:
                        peer_scores(b, *back(p, par, 1), att)
                    if out is not None and j == 13:
                        out_transposes(out)
                    if out is not None and j >= 14:
                        out_projection(out, j - 14)
                    if h == 0 and tp is not None:
                        if 1 <= j <= 6:
                            out_projection(tp, j + 1)
                        if j == 6:
                            h_gain()
                        if j == 10:
                            h_transposes(tp)
                    if tg is not None:
                        weigh(8 * tg + 2 * p + par, j)

            iterations(pe, section)
            section(NT, 0, 0)
            pe.wait_ge(gs_in, after(gs_in, 1))
            pe.transpose(pA[:, 0:8], S[0:8, 0:P], idn[0:8, 0:8])
            pe.transpose(pA[:, 8:16], gates[0:8, :], idn[0:8, 0:8]).then_inc(gs_t, 1)
            acc_start(NT, NS)
            for r in range(NS):
                bank = (pS, pT)[r % 2]
                if r >= 2:
                    pe.wait_ge(u_used, after(u_used, TOPK * 8 * NT + r - 1))
                for half in range(2):
                    m = pe.matmul(bank[:, half * 512:(half + 1) * 512], idn[:, r:r + 1].broadcast_to([P, P]),
                                  h_next[:, half * 512:(half + 1) * 512], start=True, stop=True)
                m.then_inc(gs_h, 1)
            pe.wait_ge(gs_w, after(gs_w, 1))
            for r in range(NS):
                pe.wait_ge(v_in[r % RING], 16 * (4 * 8 * NT + r // RING + 1))
                for half in range(2):
                    m = pe.matmul(acc[0:NS, half * 512:(half + 1) * 512], wz[:, r, :],
                                  v_ring[r % RING][:, half * 512:(half + 1) * 512],
                                  start=False, stop=False, skip_group_check=True)
                m.then_inc(v_used, 1)

        @block.scalar
        def _(act):
            set_starts(act, "act")

            def copy(out, in_):
                return act.activation(out, in_, ACT.Copy)

            def z_copies(t):
                for c, (c0, w) in enumerate(CHUNKS):
                    act.wait_ge(a_z, after(a_z, 5 * t + c + 1))
                    if c == 0:
                        act.wait_ge(z_out, after(z_out, 32 * t))
                        act.wait_ge(a_vb, after(a_vb, t))
                        act.wait_ge(a_rt, after(a_rt, 4 * t))
                    if c == 0:
                        copy(z[:, 0:512].rearrange("p (b a d) -> p a b d", a=2, b=4),
                             zbank[0].rearrange("p (a b d) -> p a b d", a=2, b=4)).then_inc(a_ze, 1)
                    else:
                        copy(z[:, c0:c0 + w], zbank[c][:, 0:w]).then_inc(a_ze, 1)

            with repeat(act, 0, NT) as t:
                z_copies(t)
                act.wait_ge(q_out, after(q_out, 32 * t))
                act.wait_ge(a_rt, after(a_rt, 4 * t + 1))
                copy(qTe[:, 0:4, :], pS[:, 512:1024].rearrange("p (b n) -> p b n", b=4)).then_inc(a_te, 1)
                act.wait_ge(a_rt, after(a_rt, 4 * t + 2))
                copy(qTe[:, 4:8, :], pA[:, :].rearrange("p (b n) -> p b n", b=4)).then_inc(a_te, 1)
                act.wait_ge(a_rt, after(a_rt, 4 * t + 3))
                copy(KTB[:, :, ds(t * P, P)], pM[:, :].rearrange("p (b n) -> p b n", b=4)).then_inc(a_te, 1)
                act.wait_ge(a_rt, after(a_rt, 4 * t + 4))
                copy(kTAe, pT[:, 0:P]).then_inc(a_te, 1)
            z_copies(NT)
            for b in range(2):
                act.wait_ge(k_t, after(k_t, b + 1))
                copy(keysT[:, 8 * b:8 * b + 8, :], pT[:, :].rearrange("p (h k) -> p h k", h=8)).then_inc(k_te, 1)

            act.wait_ge(s_max, after(s_max, 1))
            act.activation(s_pB[0:64, :], s_pB[0:64, :], ACT.Exp, bias=anm[0:64, 0:1], accum_out=aden[0:64, 0:1])
            act.activation(s_pA[0:64, :], s_pA[0:64, :], ACT.Exp, bias=anm[0:64, 1:2], accum_out=aden[0:64, 1:2])
            act.activation(aden[0:64, 2:3], s_sink, ACT.Exp, bias=anm[0:64, 1:2]).then_inc(s_exp, 1)
            act.wait_ge(s_bT, after(s_bT, 1))
            copy(s_pT, pT[:, 0:192].rearrange("p (s n) -> p s n", s=3))
            copy(s_pTn[0:8, :, :], pT[0:8, 192:320].rearrange("p (s n) -> p s n", s=2)).then_inc(s_bTe, 1)

            def att_softmax(t, p, par):
                a = 8 * t + 2 * p + par
                act.wait_ge(att_max, after(att_max, a + 1))
                act.activation(S_B, S_B, ACT.Exp, bias=anm[:, 0:1], accum_out=aden[:, 0:1])
                act.activation(S_A, S_A, ACT.Exp, bias=anm[:, 1:2], accum_out=aden[:, 1:2])
                act.activation(aden[:, 2:3], sink[:, ds(p + 4 * par, 1)], ACT.Exp,
                               bias=anm[:, 1:2]).then_inc(att_exp, 1)

            def att_copies(t, p, par):
                a = 8 * t + 2 * p + par
                act.wait_ge(att_pv, after(att_pv, a))
                if place(p, par) == 0 and begun(t - 1):
                    act.wait_ge(mx_mm, after(mx_mm, t))
                for k in range(2):
                    act.wait_ge(att_t, after(att_t, 3 * a + k + 1))
                    copy(PT[:, 4 * k:4 * k + 4, :],
                         pT[:, 512 * k:512 * k + 512].rearrange("p (b n) -> p b n", b=4)).then_inc(att_te, 1)
                act.wait_ge(att_t, after(att_t, 3 * a + 3))
                copy(PT[:, 8:10, :], pA[:, 256:512].rearrange("p (b n) -> p b n", b=2)).then_inc(att_te, 1)

            def h_copies(t):
                act.wait_ge(mx_ht, after(mx_ht, t + 1))
                copy(TT[:, 0:4, :], pT[:, 0:512].rearrange("p (b n) -> p b n", b=4))
                copy(TT[:, 4:8, :], pT[:, 512:1024].rearrange("p (b n) -> p b n", b=4)).then_inc(mx_hT, 1)

            def tanh(s, par):
                act.wait_ge(gl_in, after(gl_in, s + 1))
                act.activation(gl[:, 1, :], gl[:, 0, :], ACT.Tanh, scale=GELU_C).then_inc(gl_th, 1)

            def take_tile(t, rows=P):
                act.wait_ge(v_used, after(v_used, TOPK * 8 * (t + 1) if rows == P else TOPK * 8 * NT + NS))
                act.wait_ge(y_out, after(y_out, 16 * t))
                copy(ybuf[0:rows, :], acc[0:rows, :]).then_inc(fin_free, 1)

            def section(t, p, par):
                tg, tp, ta = tiles_of(t)
                h = place(p, par)
                b = 8 * (t + 1) + 2 * p + par - 1
                peer = exists(t, p, par, 1)
                rank = exists(t, p, par, 2)
                if h == 0 and (not isinstance(t, int) or t >= 1):
                    take_tile(t - 1)
                if tg is not None:
                    s = 8 * tg + 2 * p + par
                    tanh(s, par)
                    act.wait_ge(w_set, after(w_set, s + 1))
                for j in range(TOPK):
                    if tg is not None:
                        n = TOPK * s + j
                        act.wait_ge(v_used, after(v_used, n - 3))
                        act.activation(diag[:, j % 4, :], idn[:, :], ACT.Copy,
                                       scale=wv[:, par, j:j + 1]).then_inc(diag_set, 1)
                    if ta is not None and j == (12 if h == 0 else 3):
                        att_softmax(ta, p, par)
                    if peer and j == (1 if h == 0 else 4):
                        act.wait_ge(pr_q, after(pr_q, b + 1))
                        act.wait_ge(pr_t, after(pr_t, b))
                        copy(pq[:, :], pM[:, 0:256]).then_inc(pr_qe, 1)
                    if ta is not None and j == (14 if h == 0 else 7):
                        att_copies(ta, p, par)
                    if peer and j == (4 if h == 0 else 10):
                        act.wait_ge(pr_t, after(pr_t, b + 1))
                        copy(pqT[:, :, :], pA[:, 0:256].rearrange("p (b n) -> p b n", b=2)).then_inc(pr_te, 1)
                    if peer and j == (6 if h == 0 else 13):
                        act.wait_ge(pr_s, after(pr_s, b + 1))
                        act.wait_ge(pr_read, after(pr_read, b))
                        copy(sc[:, :, :], pM[:, 0:256].rearrange("p (b n) -> p b n", b=2)).then_inc(pr_se, 1)
                    if rank and j == 8:
                        act.wait_ge(pr_top, after(pr_top, b))
                        act.activation(gexp[:, :], candv[:, par, :], ACT.Exp, bias=gsm[:, 0:1],
                                       accum_out=gsm[:, 1:2]).then_inc(pr_exp, 1)
                    if h == 0 and tp is not None and j == 11:
                        h_copies(tp)

            iterations(act, section)
            section(NT, 0, 0)
            section(NT, 0, 1)
            act.wait_ge(gs_in, after(gs_in, 2))
            act.activation(gl[:, 1, 0:NS], gl[:, 0, 0:NS], ACT.Tanh, scale=GELU_C).then_inc(gs_th, 1)
            take_tile(NT, NS)

        @block.vector
        def _(dve):
            set_starts(dve, "dve")
            D_ = dve.drain

            dve.memset(qpad[:, :, :, :], 0.0)
            dve.memset(kTA[:, 0:P], 0.0)
            dve.memset(vA[:, 0, :], 0.0).then_inc(pads, 1)

            def sum_squares(x, n, out, junk, rows=P):
                dve.tensor_tensor_reduce(junk, x, x, 1.0, 0.0, ALU.mult, ALU.add, out)

            def rsqrt(rows, cols, count):
                r, c = slice(0, rows), slice(0, cols)
                D_()
                dve.tensor_scalar(nw_x[r, c], ssum[r, c], 1.0 / count, EPS, ALU.mult, ALU.add)
                D_()
                dve.tensor_scalar(nw_i[r, c], nw_x[r, c].bitcast(I32), 1, None, ALU.arith_shift_right)
                D_()
                dve.tensor_scalar(nw_i[r, c], nw_i[r, c], -1.0, MAGIC, ALU.mult, ALU.add)
                y = nw_i[r, c].bitcast(F32)
                for _ in range(3):
                    D_()
                    dve.tensor_tensor(nw_a[r, c], y, y, ALU.mult)
                    D_()
                    dve.scalar_tensor_tensor(nw_b[r, c], nw_a[r, c], -0.5, nw_x[r, c], ALU.mult, ALU.mult)
                    D_()
                    dve.scalar_tensor_tensor(nw_y[r, c], nw_b[r, c], 1.5, y, ALU.add, ALU.mult)
                    y = nw_y[r, c]
                D_()

            def with_gain(which, out, psum, done):
                for half in range(2):
                    g = gcol[:, which, 4 * half:4 * half + 4].unsqueeze(2).broadcast_to([P, 4, P])
                    i = dve.tensor_tensor(out[:, 4 * half:4 * half + 4, :],
                                          psum[:, 512 * half:512 * half + 512].rearrange("p (b n) -> p b n", b=4),
                                          g, ALU.mult)
                i.then_inc(done, 1)

            def scale_x(t):
                dve.wait_ge(x_in, 16 * (t + 1))
                sum_squares(xin, D, ssum[:, 0:1], xs)
                rsqrt(P, 1, D)
                dve.tensor_scalar(xs, xin, nw_y[:, 0:1], None, ALU.mult).then_inc(a_xs, 1)

            def x_gain(t):
                dve.wait_ge(a_xt, after(a_xt, t + 1))
                dve.wait_ge(a_z, after(a_z, 5 * t))
                with_gain(0, TT, acc, a_xT)

            def rope(t, c0, heads):
                zr = z[:, c0:c0 + heads * HD].rearrange("p (h d) -> p h d", d=HD)[:, :, 0:16]
                lo, hi = zr[:, :, 0:8], zr[:, :, 8:16]
                cos = rcs[:, ds(t, 1), 0:8].broadcast_to([P, heads, 8])
                sin = rcs[:, ds(t, 1), 8:16].broadcast_to([P, heads, 8])
                tmp = rtmp[:, 0:4 * heads * 8].rearrange("p (a h d) -> p a h d", a=4, h=heads)
                dve.tensor_tensor(tmp[:, 0, :, :], lo, cos, ALU.mult)
                dve.tensor_tensor(tmp[:, 1, :, :], hi, sin, ALU.mult)
                dve.tensor_tensor(tmp[:, 2, :, :], hi, cos, ALU.mult)
                dve.tensor_tensor(tmp[:, 3, :, :], lo, sin, ALU.mult)
                D_()
                dve.tensor_tensor(lo, tmp[:, 0, :, :], tmp[:, 1, :, :], ALU.subtract)
                dve.tensor_tensor(hi, tmp[:, 2, :, :], tmp[:, 3, :, :], ALU.add).then_inc(a_rope, 1)

            def rope_tile(t):
                dve.wait_ge(a_ze, after(a_ze, 5 * t + 2))
                rope(t, QA, 10)
                D_()
                dve.wait_ge(a_ze, after(a_ze, 5 * t + 4))
                rope(t, QB, 16)

            dve.wait_ge(c_in, 16 * 9)
            scale_x(0)
            x_gain(0)
            with repeat(dve, 0, NT) as t:
                scale_x(t + 1)
                rope_tile(t)
                x_gain(t + 1)
            rope_tile(NT)

            dve.wait_ge(snew_in, 32)
            dve.wait_ge(a_z, after(a_z, 5 * NT + 5))
            dve.wait_ge(a_rt, after(a_rt, 4 * NT))

            def dot_heads(out, k, q, n, rows, groups):
                prod = s_prod[0:rows, 0:n]
                D_()
                dve.tensor_tensor(prod.rearrange("p (a b c) -> p a b c", a=groups[0], b=groups[1]), k, q, ALU.mult)
                D_()
                return dve.tensor_reduce(out, prod.rearrange("p (a b d) -> p a b d", d=HD, a=groups[2]),
                                         AX_X, ALU.add)

            with repeat(dve, 0, NS // 2) as i:
                for b in range(2):
                    r = 2 * i + b
                    cols = ds(r * 8, 8)
                    hold(dve, "dve", sk_in[b], 96 * (i + 1))
                    qA, qB = s_q[b][:, 0:512], s_q[b][:, 512:1024]
                    dot_heads(s_sc[:, 0:2, cols], s_k[b].unsqueeze(2),
                              qB.unsqueeze(1).unsqueeze(1).broadcast_to([P, 2, 1, 512]), 1024, P, (2, 1, 2))
                    dot_heads(s_sc[:, 2:3, cols], s_kA[b].rearrange("p (a d) -> p a d", a=2)
                              .unsqueeze(2).broadcast_to([P, 2, 4, HD]),
                              qA.rearrange("p (b a d) -> p a b d", a=2, b=4), 512, P, (2, 4, 1))
                    dot_heads(s_scn[0:8, 0:1, cols], s_new[0:8, 256:768].unsqueeze(1).unsqueeze(1),
                              qB[0:8, :].unsqueeze(1).unsqueeze(1), 512, 8, (1, 1, 1))
                    dot_heads(s_scn[0:8, 1:2, cols], s_new[0:8, 0:P].rearrange("p (a d) -> p a d", a=2)
                              .unsqueeze(2).broadcast_to([8, 2, 4, HD]),
                              qA[0:8, :].rearrange("p (b a d) -> p a b d", a=2, b=4), 512, 8, (2, 4, 1))\
                        .then_inc(s_mul, 1)
            dve.wait_ge(s_sT, after(s_sT, 1))
            dve.wait_ge(sconst_in, 16 * (3 + NS))
            R = slice(0, 64)
            dve.tensor_tensor_reduce(s_pB[R, :], pS[R, 0:264], s_mB, 0.125, NEG, ALU.add, ALU.max, amax[R, 0:1])
            dve.tensor_tensor_reduce(s_pA[R, :], pS[R, 512:648], s_mA, 0.125, NEG, ALU.add, ALU.max, amax[R, 1:2])
            D_()
            dve.tensor_tensor(amax[R, 1:2], amax[R, 1:2], s_sink, ALU.max)
            D_()
            dve.tensor_scalar(anm[R, :], amax[R, :], -1.0, None, ALU.mult).then_inc(s_max, 1)
            dve.wait_ge(s_exp, after(s_exp, 1))
            dve.tensor_tensor(aden[R, 1:2], aden[R, 1:2], aden[R, 2:3], ALU.add)
            D_()
            dve.reciprocal(arden[R, :], aden[R, 0:2])
            D_()
            dve.tensor_scalar(s_pB[R, :], s_pB[R, :], arden[R, 0:1], None, ALU.mult)
            dve.tensor_scalar(s_pA[R, :], s_pA[R, :], arden[R, 1:2], None, ALU.mult).then_inc(s_prob, 1)
            for r in range(NS):
                bank = (pS, pT)[r % 2]
                dve.wait_ge(s_pv, after(s_pv, r + 1))
                if r >= 2:
                    dve.wait_ge(s_fold, after(s_fold, r - 1))
                dve.tensor_tensor(s_od[r % 2][:, 0:512].rearrange("p (a b d) -> p a b d", a=2, b=4),
                                  bank[0:8, 512:640].rearrange("p (a d) -> p a d", a=2).unsqueeze(2)
                                  .broadcast_to([8, 2, 4, HD]),
                                  s_hm.rearrange("p (a b d) -> p a b d", a=2, b=4), ALU.mult)
                dve.tensor_tensor(s_od[r % 2][:, 512:1024], bank[0:8, 0:512], s_hm, ALU.mult).then_inc(s_dg, 1)
            dve.wait_ge(s_fold, after(s_fold, NS))
            dve.tensor_copy(s_o, acc[0:8, :]).then_inc(s_done, 1)

            def att_maxima(t, p, par, first):
                a = 8 * t + 2 * p + par
                dve.wait_ge(att_s, after(att_s, a + 1))
                hold(dve, "dve", att_t, 3 * a)
                dve.tensor_tensor_reduce(S_B, pS[:, :], maskB[:, :], 0.125, NEG, ALU.add, ALU.max, amax[:, 0:1])
                dve.tensor_tensor_reduce(S_A, pA[:, 0:256], maskA[:, 0 if first else 1, :], 0.125, NEG,
                                         ALU.add, ALU.max, amax[:, 1:2])
                D_()
                dve.tensor_tensor(amax[:, 1:2], amax[:, 1:2], sink[:, ds(p + 4 * par, 1)], ALU.max)
                D_()
                dve.tensor_scalar(anm[:, :], amax[:, :], -1.0, None, ALU.mult).then_inc(att_max, 1)

            def att_output(t, p, par):
                a = 8 * t + 2 * p + par
                dve.wait_ge(att_exp, after(att_exp, a + 1))
                dve.tensor_tensor(aden[:, 1:2], aden[:, 1:2], aden[:, 2:3], ALU.add)
                D_()
                dve.reciprocal(arden[:, :], aden[:, 0:2])
                D_()
                dve.wait_ge(att_pv, after(att_pv, a + 1))
                dve.tensor_scalar(o_all[:, ds(512 + p * P + par * HD, HD)], pM[:, 256:320], arden[:, 0:1],
                                  None, ALU.mult)
                dve.tensor_scalar(o_all[:, ds(p * HD + par * 256, HD)], pM[:, 320:384], arden[:, 1:2],
                                  None, ALU.mult).then_inc(att_o, 1)

            def out_squares(t):
                if isinstance(t, int) and t == NT:
                    hold(dve, "dve", so_in, 16)
                D_()
                for half in range(2):
                    c = slice(512 * half, 512 * half + 512)
                    sum_squares(o_all[:, c], 512, ssum[:, half:half + 1], S[:, c])

            def out_norm(t):
                rsqrt(P, 2, 512)
                for half in range(2):
                    c = slice(512 * half, 512 * half + 512)
                    i = dve.tensor_scalar(S[:, c], o_all[:, c], nw_y[:, half:half + 1], None, ALU.mult)
                i.then_inc(mx_on, 1)

            def out_gain(t):
                dve.wait_ge(mx_t, after(mx_t, t + 1))
                with_gain(1, PT, pT, mx_onT)

            def residual(t):
                dve.wait_ge(mx_mm, after(mx_mm, t + 1))
                dve.wait_ge(mx_in, 16 * (t + 1))
                dve.tensor_tensor(x2[:, :], x2[:, :], pS[:, :], ALU.add).then_inc(mx_x2, 1)
                D_()
                sum_squares(x2[:, :], D, ssum[:, 0:1], S_B)

            def norm_h(t):
                rsqrt(P, 1, D)
                dve.scalar_tensor_tensor(h_next, x2[:, :], nw_y[:, 0:1], pT[:, :], ALU.mult,
                                         ALU.mult).then_inc(mx_h, 1)

            def top8(values, places, scores):
                D_()
                dve.max(values, scores)
                D_()
                return dve.max_index(places, values, scores)

            def rank_half(b, par, half):
                if half == 0:
                    hold(dve, "dve", pr_se, b + 1)
                values, places, x = topv[:, par, half, :], topi[:, par, half, :], sc[:, half, :]
                top8(values[:, 0:8], places[:, 0:8], x)
                D_()
                dve.match_replace(x, values[:, 0:8], x, NEG)
                i = top8(values[:, 8:16], places[:, 8:16], x)
                if half == 1:
                    i.then_inc(pr_read, 1)

            sums = cand[:, :, :].rearrange("p a b -> p (a b)")

            def rank_sums(par):
                D_()
                dve.tensor_tensor(cand[:, :, :], topv[:, par, 0, :].unsqueeze(2).broadcast_to([P, TOPK, TOPK]),
                                  topv[:, par, 1, :].unsqueeze(1).broadcast_to([P, TOPK, TOPK]), ALU.add)
                top8(candv[:, par, 0:8], candp[:, par, 0:8], sums)

            def rank_rest(par):
                D_()
                dve.match_replace(sums, candv[:, par, 0:8], sums, NEG)
                top8(candv[:, par, 8:16], candp[:, par, 8:16], sums)
                dve.tensor_scalar(gsm[:, 0:1], candv[:, par, 0:1], -1.0, None, ALU.mult).then_inc(pr_top, 1)

            def gate(b, p, par):
                dve.wait_ge(pr_exp, after(pr_exp, b + 1))
                dve.reciprocal(gsm[:, 2:3], gsm[:, 1:2])
                D_()
                dve.tensor_scalar(gates[:, ds(p * 32 + par * TOPK, TOPK)], gexp[:, :], gsm[:, 2:3], None, ALU.mult)

            def numbers_half(half):
                D_()
                if half == 0:
                    dve.tensor_copy(topif[:, :, :, :], topi[:, :, :, :])
                    dve.tensor_scalar(candh[:, :, :], candp[:, :, :], 4, None, ALU.logical_shift_right)
                else:
                    dve.tensor_scalar(candh[:, :, :], candp[:, :, :], 15, None, ALU.bitwise_and)
                D_()
                dve.tensor_copy(candf[:, :, :], candh[:, :, :])
                D_()
                full = [P, 2, TOPK, TOPK]
                dve.tensor_tensor(onehot[:, :, :, :], candf[:, :, :].unsqueeze(3).broadcast_to(full),
                                  iota[:, :].unsqueeze(1).unsqueeze(1).broadcast_to(full), ALU.is_equal)
                D_()
                dve.tensor_tensor(onehot[:, :, :, :], onehot[:, :, :, :],
                                  topif[:, :, half, :].unsqueeze(2).broadcast_to(full), ALU.mult)
                D_()
                dve.tensor_reduce(sel[:, half, :, :], onehot[:, :, :, :], AX_X, ALU.add)

            def numbers(p, taken):
                D_()
                if taken is not None:
                    dve.wait_ge(win_set, after(win_set, taken))
                dve.scalar_tensor_tensor(
                    idx_all[:, ds(p * 32, 32)], sel[:, 0, :, :].rearrange("p a b -> p (a b)"), float(KEYS),
                    sel[:, 1, :, :].rearrange("p a b -> p (a b)"), ALU.mult, ALU.add).then_inc(pr_idx, 1)

            def dot(us, j, par):
                dve.wait_ge(u_in[j % RING], 16 * (4 * us + j // RING + 1))
                dve.tensor_tensor_reduce(u_ring[j % RING], u_ring[j % RING], h_cur, 1.0, 0.0, ALU.mult, ALU.add,
                                         dots[:, par, j:j + 1]).then_inc(u_used, 1)

            def gelu_arg(x, n):
                D_()
                dve.tensor_tensor(gl[:, 0, 0:n], x, x, ALU.mult)
                D_()
                dve.tensor_scalar(gl[:, 0, 0:n], gl[:, 0, 0:n], 0.044715, 1.0, ALU.mult, ALU.add)
                D_()
                return dve.tensor_tensor(gl[:, 0, 0:n], gl[:, 0, 0:n], x, ALU.mult)

            def gelu_gate(out, x, g, n):
                dve.scalar_tensor_tensor(gl[:, 2, 0:n], gl[:, 1, 0:n], 1.0, x, ALU.add, ALU.mult)
                D_()
                return dve.scalar_tensor_tensor(out, gl[:, 2, 0:n], 0.5, g, ALU.mult, ALU.mult)

            def final_norm(t, rows=P):
                r = slice(0, rows)
                junk = h_cur if isinstance(t, int) and t >= NT - 1 else h_next
                D_()
                hold(dve, "dve", fin_free, t + 1)
                sum_squares(ybuf[r, :], D, ssum[r, 0:1], junk[r, :])
                rsqrt(rows, 1, D)

            def final_gain(t, rows=P):
                r = slice(0, rows)
                dve.scalar_tensor_tensor(ybuf[r, :], ybuf[r, :], nw_y[r, 0:1], fgain[r, :], ALU.mult, ALU.mult)\
                    .then_inc(fin_y, 1)

            def section(t, p, par):
                tg, tp, ta = tiles_of(t)
                h = place(p, par)
                s = 8 * t + 2 * p + par
                b = s + 6
                rank = exists(t, p, par, 2)
                out = t + 2 if h == 7 and has_next(t) else None
                dots_next = tg is not None or (isinstance(t, int) and t == -1 and h == 7)
                if isinstance(t, int) and t == NT - 1 and h == 7:
                    dots_next = False
                if tg is not None:
                    gelu_arg(dots[:, par, :], TOPK).then_inc(gl_in, 1)
                if h == 7 and dots_next:
                    dve.tensor_copy(h_cur, h_next)
                    D_()
                for j in range(TOPK):
                    if dots_next:
                        dot(s + 1, j, 1 - par)
                    if tg is not None and j == 0:
                        dve.wait_ge(gl_th, after(gl_th, s + 1))
                        gelu_gate(wv[:, par, :], dots[:, par, :], gates[:, ds(p * 32 + par * TOPK, TOPK)], TOPK)\
                            .then_inc(w_set, 1)
                    if ta is not None and j == (10 if h == 0 else 1):
                        att_maxima(ta, p, par, isinstance(t, int) and t == -2)
                    if h == 0 and (not isinstance(t, int) or t >= 1):
                        if j == 1:
                            final_norm(t - 1)
                        if j == 2:
                            final_gain(t - 1)
                    if rank and j in (3, 4):
                        rank_half(b, par, j - 3)
                    if rank and j == 5:
                        rank_sums(par)
                    if rank and j == 6:
                        rank_rest(par)
                    if h == 0 and tp is not None and j == 7:
                        residual(tp)
                    if h == 0 and tp is not None and j == 8:
                        norm_h(tp)
                    if rank and j == 9:
                        gate(b, *back(p, par, 2))
                    if ta is not None and j == (15 if h == 0 else 9):
                        att_output(ta, p, par)
                    if out is not None and j == 10:
                        out_squares(out)
                    if out is not None and j == 11:
                        out_norm(out)
                    if out is not None and j == 14:
                        out_gain(out)
                    if rank and par == 1 and j == (12 if h == 7 else 11):
                        numbers_half(0)
                    if rank and par == 1 and j == 13:
                        numbers_half(1)
                        numbers(back(p, par, 2)[0], s - 1 if begun(t) else None)

            iterations(dve, section)
            section(NT, 0, 0)
            section(NT, 0, 1)
            D_()
            dve.tensor_copy(S[0:8, 0:P], idx_all[0:8, :]).then_inc(gs_in, 1)
            dve.wait_ge(gs_t, after(gs_t, 1))
            dve.tensor_copy(gateT[:, :], pA[:, 8:16])
            dve.tensor_copy(idxT[:, :], pA[:, 0:8]).then_inc(gs_idx, 1)
            for r in range(NS):
                dve.wait_ge(u_in[r % RING], 16 * (4 * 8 * NT + r // RING + 1))
                dve.wait_ge(gs_h, after(gs_h, r + 1))
                dve.tensor_tensor_reduce(u_ring[r % RING], u_ring[r % RING], (pS, pT)[r % 2][:, :], 1.0, 0.0,
                                         ALU.mult, ALU.add, dotsT[:, r:r + 1]).then_inc(u_used, 1)
            gelu_arg(dotsT[:, :], NS).then_inc(gs_in, 1)
            dve.wait_ge(gs_th, after(gs_th, 1))
            gelu_gate(gl[:, 0, NS:2 * NS], dotsT[:, :], gateT[:, :], NS)
            D_()
            dve.tensor_tensor(wz[:, :, :], gl[:, 0, NS:2 * NS].unsqueeze(2).broadcast_to([P, NS, 8]),
                              e8[:, :, :], ALU.mult).then_inc(gs_w, 1)
            final_norm(NT, NS)
            final_gain(NT, NS)


def tables(np):
    pos = np.concatenate([np.arange(NT * P), np.full(P, NT * P)]).astype(np.float32)
    inv = (np.float32(500000.0) ** (-np.arange(0, 16, 2, dtype=np.float32) / np.float32(16))).astype(np.float32)
    ang = (pos[:, None] * inv[None, :]).astype(np.float32)
    rope_cs = np.concatenate([np.cos(ang), np.sin(ang)], axis=1).astype(np.float32)

    def log_count(dist, branches):
        c = sum(((dist >= 0) & (dist <= w) & (dist % d == 0)).astype(np.int64) for w, d in branches)
        return np.where(c > 0, 8 * np.log(np.maximum(c, 1)), -1e30).astype(np.float32)

    dil = ((128, 1), (512, 4), (2048, 16))
    win = ((128, 1),)
    q = np.arange(P)[:, None]
    mask_b = log_count(q + (NT - 1) * P - np.arange((2 * NT - 1) * P)[None, :], dil)
    both = log_count(q + P - np.arange(2 * P)[None, :], win)
    own = np.where(np.arange(2 * P)[None, :] < P, np.float32(-1e30), both)
    mask_a = np.stack([own, both], axis=1).astype(np.float32)
    rows = np.concatenate([np.arange(896, 1024), np.arange(512, 896, 4), np.arange(0, 512, 16)])
    new = np.repeat(np.where(np.eye(NS) > 0, 8 * np.log(3.0), -1e30), HEADS, axis=0)
    mask_sb = np.concatenate([np.repeat(log_count(1024 - rows[None, :], dil), 64, axis=0), new], axis=1)
    new = np.repeat(np.where(np.eye(NS) > 0, 0.0, -1e30), HEADS, axis=0)
    mask_sa = np.concatenate([np.zeros((64, P)), new], axis=1)
    return {
        "ident": np.eye(P, dtype=np.float32), "rope_cs": rope_cs, "mask_b": mask_b, "mask_a": mask_a,
        "mask_sb": mask_sb.astype(np.float32), "mask_sa": mask_sa.astype(np.float32),
        "iota16": np.tile(np.arange(16, dtype=np.float32), (P, 1)),
        "eye8": np.tile(np.eye(8, dtype=np.float32)[None], (P, 1, 1)),
        "head_mask": np.repeat(np.eye(8, dtype=np.float32), HD, axis=1),
    }


_INS = ("x_all", "cache_swa", "cache_dil", "w_in", "sinks", "w_out", "w_q", "keys", "peer_u", "peer_v", "ident",
        "gain_cols", "gain_rows", "final_gain", "rope_cs", "mask_b", "mask_a", "mask_sb", "mask_sa", "iota16", "eye8",
        "head_mask")
_OUTS = (("y_p", (1024, 1024)), ("y_s", (8, 1024)), ("swa_p", (128, 256)), ("dil_p", (1024, 1024)),
         ("swa_s", (8, 128 * 256)), ("dil_s", (8, 1024, 1024)))


def kernel(x_prompt, x_sample, cache_swa_kv, cache_dil_kv, attn_norm, w_in, sinks, out_norm_a, out_norm_b,
           w_out, ffn_norm, peer_w_q, peer_sub_keys, peer_u, peer_v, final_norm):
    import numpy as np
    import concourse.bacc as bacc
    from concourse.bass_utils import run_bass_kernel_spmd

    def cols(g):
        return np.asarray(g).reshape(KD, P).T

    x_all = np.concatenate([np.asarray(x_prompt).reshape(NT * P, D), np.asarray(x_sample).reshape(NS, D),
                            np.zeros((P - NS, D), np.float32)])
    out_gain = np.concatenate([np.asarray(out_norm_a)[0], np.asarray(out_norm_b)[0]])
    arrays = {
        "x_all": x_all,
        "cache_swa": np.asarray(cache_swa_kv).reshape(NS, 128 * 256),
        "cache_dil": np.asarray(cache_dil_kv).reshape(NS, 1024, 1024),
        "w_in": np.asarray(w_in)[0], "sinks": np.asarray(sinks).reshape(1, HEADS), "w_out": np.asarray(w_out)[0],
        "w_q": np.asarray(peer_w_q)[0], "keys": np.asarray(peer_sub_keys).reshape(2 * HEADS, KEYS, P),
        "peer_u": np.asarray(peer_u)[0], "peer_v": np.asarray(peer_v)[0],
        "gain_cols": np.stack([cols(np.asarray(attn_norm)[0]), cols(out_gain)], axis=1),
        "gain_rows": np.asarray(ffn_norm)[0].reshape(KD, P), "final_gain": np.asarray(final_norm).reshape(1, D),
        **tables(np),
    }
    nc = bacc.Bacc("TRN2", target_bir_lowering=False, num_devices=1)
    feeds, args = {}, []
    for name in _INS:
        a = np.ascontiguousarray(arrays[name])
        feeds[f"in_{name}"] = a
        args.append(nc.dram_tensor(f"in_{name}", a.shape, mybir.dt.from_np(a.dtype), kind="ExternalInput").ap())
    for name, shape in _OUTS:
        args.append(nc.dram_tensor(f"out_{name}", shape, F32, kind="ExternalOutput").ap())
    build(nc, *args)
    r = run_bass_kernel_spmd(nc, [feeds], core_ids=[0]).results[0]
    got = [np.asarray(r[f"out_{name}"]) for name, _ in _OUTS]
    return (got[0].reshape(1, 1024, 1024), got[1].reshape(8, 1, 1024), got[2].reshape(1, 1, 128, 2, 2, 64),
            got[3].reshape(1, 1, 1024, 2, 8, 64), got[4].reshape(1, 8, 128, 2, 2, 64),
            got[5].reshape(1, 8, 1024, 2, 8, 64))
```

```python
from contextlib import ExitStack

import concourse.bass as bass
from concourse import mybir

F32 = mybir.dt.float32
U32 = mybir.dt.uint32
I32 = mybir.dt.int32
ALU = mybir.AluOpType
ACT = mybir.ActivationFunctionType
AX_X = mybir.AxisListType.X

P = 128
D = 1024
NT = 8
ROWS = (NT + 1) * P
NS = 8
KD = D // P
HD = 64
D_IN = 2304
HEADS = 8
KEYS = 128
TOPK = 16
EPS = 1e-6
NEG = -3.0e38
GELU_C = 0.7978845608028654
QA, KVA, QB, KB, VB_, END = 0, 512, 768, 1280, 1792, 2304
CHUNKS = ((QA, 512), (KVA, 256), (QB, 512), (KB, 512), (VB_, 512))
RING = 4
WO_SLOTS = 2
MAGIC = float(0x5F3759DF)


def build(nc, x_all, cache_swa, cache_dil, w_in, sinks, w_out, w_q, keys, peer_u, peer_v,
          ident, gain_cols, gain_rows, final_gain, rope_cs, mask_b, mask_a, mask_sb, mask_sa, iota16, eye8, eye_tok, head_mask,
          y_p, y_s, swa_p, dil_p, swa_s, dil_s):
    ds = bass.ds
    with ExitStack() as ctx:
        def sb(name, shape, dt=F32):
            return ctx.enter_context(nc.sbuf_tensor(name, shape, dt))

        def pb(name, shape):
            return ctx.enter_context(nc.psum_tensor(name, shape, F32))

        producers, starts, names, kept = {}, {}, {}, []

        def sem(name, producer=None, start=1):
            s = ctx.enter_context(nc.semaphore(name))
            if producer:
                producers.setdefault(producer, []).append((s, start))
                starts[name] = start
                names[id(s)] = name
                kept.append(s)
            return s

        def after(s, n):
            return n + starts.get(names.get(id(s)), 0)

        def scratch(name, shape):
            return nc.dram_tensor(name, shape, F32, kind="Internal").ap()

        qT_scr = scratch("qT_scr", (8, P, ROWS))
        kTA_scr = scratch("kTA_scr", (P, ROWS))
        kvA_scr = scratch("kvA_scr", (ROWS, 256))
        zS_scr = scratch("zS_scr", (NS, D_IN))

        wbuf = sb("wbuf", [P, KD * D_IN])
        w_in_sb = wbuf[:, :].rearrange("p (k n) -> p k n", k=KD)
        wq_sb = wbuf[:, 0:KD * 2048].rearrange("p (k n) -> p k n", k=KD)
        keysT = wbuf[:, KD * 2048:].rearrange("p (h k) -> p h k", h=2 * HEADS)
        KTB = sb("KTB", [P, 4, D])
        VB = sb("VB", [P, NT, 512])
        ring = sb("ring", [P, 2 * RING, D])
        u_ring = [ring[:, i, :] for i in range(RING)]
        v_ring = [ring[:, RING + i, :] for i in range(RING)]
        hpair = sb("hpair", [P, 2, D])
        h_cur, h_next = hpair[:, 0, :], hpair[:, 1, :]
        x2 = sb("x2", [P, D])
        o_all = sb("o_all", [P, D])
        TT = sb("TT", [P, KD, P])
        S = sb("S", [P, D + 256])
        S_B, S_A = S[:, 0:D], S[:, D:D + 256]
        PT = sb("PT", [P, 10, P])
        maskB = sb("maskB", [P, D])
        maskA = sb("maskA", [P, 2, 256])
        wo_sb = sb("wo_sb", [P, WO_SLOTS, D])
        ybuf = sb("ybuf", [P, D])
        fgain = sb("fgain", [P, D])
        idn = sb("idn", [P, P])
        diag = sb("diag", [P, 4, P])
        qpad = sb("qpad", [P, 2, 2, P])
        kTA = sb("kTA", [P, 256])
        vA = sb("vA", [P, 2, P])
        gcol = sb("gcol", [P, 2, KD])
        grow = sb("grow", [KD, P])
        rcs = sb("rcs", [P, NT + 1, 16])
        sink = sb("sink", [P, HEADS])
        iota = sb("iota", [P, TOPK])
        e8 = sb("e8", [P, 8, 8])
        tok8 = sb("tok8", [64, 8])
        pq = sb("pq", [P, 256])
        pqT = sb("pqT", [P, 2, P])
        sc = sb("sc", [P, 2, P])
        topv = sb("topv", [P, 2, 2, TOPK])
        topi = sb("topi", [P, 2, 2, TOPK], U32)
        topif = sb("topif", [P, 2, 2, TOPK])
        cand = sb("cand", [P, TOPK, TOPK])
        candv = sb("candv", [P, 2, TOPK])
        candp = sb("candp", [P, 2, TOPK], U32)
        candh = sb("candh", [P, 2, TOPK], U32)
        candf = sb("candf", [P, 2, TOPK])
        onehot = sb("onehot", [P, 2, TOPK, TOPK])
        sel = sb("sel", [P, 2, 2, TOPK])
        gexp = sb("gexp", [P, TOPK])
        idx_all = sb("idx_all", [P, P], U32)
        gates = sb("gates", [P, P])
        win_u = sb("win_u", [P, 2, TOPK], U32)
        win_v = sb("win_v", [P, 2, TOPK], U32)
        dots = sb("dots", [P, 2, TOPK])
        gl = sb("gl", [P, 3, TOPK])
        wv = sb("wv", [P, 2, TOPK])
        nw_x = sb("nw_x", [P, 2])
        nw_i = sb("nw_i", [P, 2], I32)
        nw_a = sb("nw_a", [P, 2])
        nw_b = sb("nw_b", [P, 2])
        nw_y = sb("nw_y", [P, 2])
        ssum = sb("ssum", [P, 2])
        amax = sb("amax", [P, 2])
        anm = sb("anm", [P, 2])
        aden = sb("aden", [P, 3])
        arden = sb("arden", [P, 2])
        gsm = sb("gsm", [P, 4])
        idxT = sb("idxT", [P, NS], U32)
        gateT = sb("gateT", [P, NS])
        dotsT = sb("dotsT", [P, NS])
        wz = sb("wz", [P, NS, 8])

        xin = ring[:, 0, :]
        xs = ring[:, 1, :]
        z = ring[:, 2:5, :].rearrange("p a n -> p (a n)")[:, 0:D_IN]
        rtmp = ring[:, 5, :]
        qTe = ring[:, 6, :].rearrange("p (b n) -> p b n", b=8)
        kTAe = ring[:, 7, 0:P]
        s_k = [KTB[:, i, :].rearrange("p (s n) -> p s n", s=2) for i in range(2)]
        s_q = [KTB[:, 2 + i, :] for i in range(2)]
        s_v = [VB[:, 2 * i:2 * i + 2, :] for i in range(2)]
        s_prod = VB[:, 4:6, :].rearrange("p a n -> p (a n)")
        s_newB = VB[0:8, 6:8, :]
        s_newA = maskA[0:8, 0, :]
        s_newq = VB[0:8, 2:4, :]
        s_kA = [kTA[:, i * P:(i + 1) * P] for i in range(2)]
        s_vA = [vA[:, i, :] for i in range(2)]
        s_sc = S[:, 0:192].rearrange("p (s n) -> p s n", s=3)
        s_scn = S[:, 192:320].rearrange("p (s n) -> p s n", s=2)
        s_pB, s_pA = S[:, 320:584], S[:, 584:720]
        s_own = S[0:8, 720:736].rearrange("p (s n) -> p s n", s=2)
        s_pTn = S[:, 736:864].rearrange("p (s n) -> p s n", s=2)
        s_pT = KTB[:, 0:2, :].rearrange("p a n -> p (a n)")[:, 0:3 * 576].rearrange("p (s n) -> p s n", s=3)
        s_mB, s_mA = maskB[0:64, 0:264], maskB[0:64, 264:400]
        s_hm = maskB[0:64, 512:1024]
        s_sink = gsm[0:64, 3:4]
        s_od = KTB[0:64, 2, :]
        s_o = o_all[0:8, :]

        acc = pb("acc", [P, D])
        pS = pb("pS", [P, D])
        pA = pb("pA", [P, 512])
        pT = pb("pT", [P, D])
        pM = pb("pM", [P, 512])
        zbank = (pS[:, 0:512], pS[:, 512:768], pA[:, :], pT[:, 0:512], pT[:, 512:1024])

        c_in = sem("c_in")
        win_in = [sem(f"win_in{i}") for i in range(5)]
        x_in = sem("x_in")
        z_out = sem("z_out", "sp")
        q_out = sem("q_out", "sp")
        cache_out = sem("cache_out")
        wq_in = sem("wq_in")
        keys_in = sem("keys_in")
        snew_in = sem("snew_in")
        sconst_in = sem("sconst_in")
        sk_in = [sem(f"sk_in{i}") for i in range(2)]
        sv_in = [sem(f"sv_in{i}") for i in range(2)]
        newrow_out = sem("newrow_out")
        att_in = sem("att_in")
        qT_in = [sem(f"qT_in{i}") for i in range(2)]
        mx_in = sem("mx_in")
        wo_in = [sem(f"wo_in{i}") for i in range(WO_SLOTS)]
        y_out = sem("y_out", "sp")
        u_in = [sem(f"u_in{i}") for i in range(RING)]
        v_in = [sem(f"v_in{i}") for i in range(RING)]
        swa_out = sem("swa_out")

        a_xs = sem("a_xs", "dve")
        a_xT = sem("a_xT", "dve")
        a_rope = sem("a_rope", "dve")
        a_xt = sem("a_xt", "pe")
        a_z = sem("a_z", "pe")
        a_rt = sem("a_rt", "pe")
        a_ze = sem("a_ze", "act")
        a_te = sem("a_te", "act")
        a_vb = sem("a_vb", "pool")
        pads = sem("pads", "dve")
        k_t = sem("k_t", "pe")
        k_te = sem("k_te", "act")
        s_mul = sem("s_mul", "dve", 2)
        s_sT = sem("s_sT", "pe")
        s_max = sem("s_max", "dve")
        s_exp = sem("s_exp", "act")
        s_prob = sem("s_prob", "dve")
        s_bT = sem("s_bT", "pe")
        s_bTe = sem("s_bTe", "act")
        s_pv = sem("s_pv", "pe", 2)
        s_dg = sem("s_dg", "dve")
        s_fold = sem("s_fold", "pe")
        s_own_set = sem("s_own_set", "dve")
        s_zero = sem("s_zero", "dve")
        att_s = sem("att_s", "pe", 2)
        att_max = sem("att_max", "dve")
        att_exp = sem("att_exp", "act")
        att_t = sem("att_t", "pe")
        att_te = sem("att_te", "act")
        att_pv = sem("att_pv", "pe")
        att_o = sem("att_o", "dve")
        mx_on = sem("mx_on", "dve")
        mx_t = sem("mx_t", "pe")
        mx_onT = sem("mx_onT", "dve")
        wo_used = sem("wo_used", "pe", WO_SLOTS)
        mx_mm = sem("mx_mm", "pe")
        mx_x2 = sem("mx_x2", "dve")
        mx_h = sem("mx_h", "dve")
        mx_ht = sem("mx_ht", "pe")
        mx_hT = sem("mx_hT", "act")
        pr_q = sem("pr_q", "pe")
        pr_qe = sem("pr_qe", "act")
        pr_t = sem("pr_t", "pe")
        pr_te = sem("pr_te", "act")
        pr_s = sem("pr_s", "pe")
        pr_se = sem("pr_se", "act")
        pr_read = sem("pr_read", "dve")
        pr_top = sem("pr_top", "dve")
        pr_exp = sem("pr_exp", "act")
        pr_idx = sem("pr_idx", "dve")
        win_set = sem("win_set", "pool")
        win_cp = sem("win_cp", "pool")
        gl_in = sem("gl_in", "dve")
        gl_th = sem("gl_th", "act")
        w_set = sem("w_set", "dve")
        diag_set = sem("diag_set", "act")
        u_used = sem("u_used", "dve", RING)
        v_used = sem("v_used", "pe", RING)
        acc_init = sem("acc_init", "pe")
        fin_y = sem("fin_y", "dve")
        fin_free = sem("fin_free", "act")
        gs_t = sem("gs_t", "pe")
        gs_idx = sem("gs_idx", "dve")
        gs_h = sem("gs_h", "pe")
        gs_in = sem("gs_in", "dve")
        gs_th = sem("gs_th", "act")
        gs_w = sem("gs_w", "dve")

        steps = {who: ctx.enter_context(nc.semaphore(f"{who}_step")) for who in ("sp", "pool", "dve")}

        def hold(eng, who, s, n):
            eng.wait_ge(s, after(s, n))
            eng.sem_inc(steps[who], 1)

        def set_starts(eng, who):
            for s, start in producers[who]:
                eng.sem_inc(s, start)

        def repeat(eng, start, end):
            return eng.Fori(start, end)

        def tiles_of(t):
            if not isinstance(t, int):
                return t, t + 1, t + 2
            return (t if 0 <= t < NT else None, t + 1 if 0 <= t + 1 <= NT else None,
                    t + 2 if t + 2 < NT else None)

        def blocks_of(t):
            return t + 1 if isinstance(t, int) else NT

        def halves_of(blocks):
            return [(b, min(b + 4, blocks)) for b in range(0, blocks, 4)]

        def place(p, par):
            return 2 * p + par if isinstance(p, int) else None

        def back(p, par, n):
            half = (par - n) % 2
            pair = p + (par - n - half) // 2
            return (pair % 4 if isinstance(p, int) else pair), half

        def has_next(t):
            return not isinstance(t, int) or t + 2 <= NT

        def begun(t):
            return not isinstance(t, int) or t >= 0

        def is_last(t, p, par):
            return isinstance(t, int) and t == NT - 1 and place(p, par) == 7

        def exists(t, p, par, n):
            if not isinstance(t, int) or t >= -1 and not isinstance(p, int):
                return True
            return t >= -1 and 0 <= 8 * (t + 1) + 2 * p + par - n < 8 * (NT + 1)

        def iteration(eng, section, t):
            section(t, 0, 0)
            section(t, 0, 1)
            if isinstance(t, int) and t in (-1, NT - 2):
                for p in (1, 2):
                    section(t, p, 0)
                    section(t, p, 1)
            else:
                with repeat(eng, 1, 3) as p:
                    section(t, p, 0)
                    section(t, p, 1)
            section(t, 3, 0)
            section(t, 3, 1)

        def iterations(eng, section):
            iteration(eng, section, -2)
            iteration(eng, section, -1)
            iteration(eng, section, 0)
            with repeat(eng, 1, NT - 2) as t:
                iteration(eng, section, t)
            iteration(eng, section, NT - 2)
            iteration(eng, section, NT - 1)

        block = ctx.enter_context(nc.Block())

        @block.sync
        def _(sp):
            set_starts(sp, "sp")
            sp.dma_start(xin, x_all[0:P, :]).then_inc(x_in, 16)
            consts = [(idn[:, :], ident), (gcol[:, :, :], gain_cols), (grow[:, :], gain_rows), (fgain[:, :], final_gain.broadcast_to([P, D])),
                      (rcs[:, :, :], rope_cs.rearrange("(t p) c -> p t c", p=P)), (maskA[:, :, :], mask_a),
                      (sink[:, :], sinks.broadcast_to([P, HEADS])), (iota[:, :], iota16), (e8[:, :, :], eye8), (tok8[:, :], eye_tok)]
            for dst, src in consts:
                sp.dma_start(dst, src).then_inc(c_in, 16)
            for r in range(NS):
                sp.dma_start(gsm[r * 8:r * 8 + 8, 3:4], sinks.rearrange("a h -> h a")).then_inc(sconst_in, 16)
            w_in_v = w_in.rearrange("(k p) n -> p k n", p=P)
            for n, (c0, w) in enumerate(CHUNKS):
                sp.dma_start(w_in_sb[:, :, c0:c0 + w], w_in_v[:, :, c0:c0 + w]).then_inc(win_in[n], 16)
            sp.dma_start(hpair[:, :, :].rearrange("p a n -> p (a n)").rearrange("p (h d) -> p h d", d=P),
                         keys.rearrange("h k d -> k h d")).then_inc(keys_in, 16)

            def cache_copy(r):
                n = 1023 * D
                src = cache_dil[ds(r, 1)].rearrange("r s n -> r (s n)")[:, D:D + n]
                dst = dil_s[ds(r, 1)].rearrange("r s n -> r (s n)")[:, 0:n]
                sp.dma_start(dst.rearrange("r (a b) -> (r a) b", a=176),
                             src.rearrange("r (a b) -> (r a) b", a=176)).then_inc(cache_out, 16)

            with repeat(sp, 0, NT) as t:
                hold(sp, "sp", a_xs, t + 1)
                sp.dma_start(xin, x_all[ds((t + 1) * P, P), :]).then_inc(x_in, 16)
                cache_copy(t)
                hold(sp, "sp", a_ze, 5 * t + 5)
                hold(sp, "sp", a_rope, 2 * t + 2)
                sp.dma_start(dil_p[ds(t * P, P), :], z[:, KB:END]).then_inc(z_out, 16)
                sp.dma_start(kvA_scr[ds(t * P, P), :], z[:, KVA:QB]).then_inc(z_out, 16)
                hold(sp, "sp", a_te, 4 * t + 4)
                sp.dma_start(qT_scr[:, :, ds(t * P, P)].rearrange("b p n -> p b n"), qTe).then_inc(q_out, 16)
                sp.dma_start(kTA_scr[:, ds(t * P, P)], kTAe).then_inc(q_out, 16)
            sp.dma_start(swa_s[:, 0:127 * 256].rearrange("r (a b) -> r a b", a=16),
                         cache_swa[:, 256:].rearrange("r (a b) -> r a b", a=16)).then_inc(cache_out, 16)
            hold(sp, "sp", a_ze, 5 * NT + 5)
            hold(sp, "sp", a_rope, 2 * NT + 2)
            sp.dma_start(zS_scr, z[0:NS, :]).then_inc(z_out, 16)
            sp.dma_start(dil_s[:, 1023, :], z[0:NS, KB:END]).then_inc(newrow_out, 16)
            sp.dma_start(swa_s[:, 127 * 256:], z[0:NS, KVA:QB]).then_inc(newrow_out, 16)
            hold(sp, "sp", a_z, 5 * NT + 5)
            hold(sp, "sp", a_vb, NT)
            hold(sp, "sp", z_out, 32 * NT + 16)
            hold(sp, "sp", q_out, 32 * NT)
            sp.wait_ge(newrow_out, 32)

            def cache_rows(dst, r, k_or_v):
                c = cache_dil[ds(r, 1), :, k_or_v * 512:k_or_v * 512 + 512].rearrange("r s n -> (r s) n")
                yield dst[:, 0, :], c[896:1024, :]
                yield dst[0:96, 1, :], c[512:896:4, :]
                yield dst[96:128, 1, :], c[0:512:16, :]

            def sample_loads():
                hold(sp, "sp", att_pv, 8 * NT)
                hold(sp, "sp", att_max, 8 * NT)
                for dst, src in ((s_mB, mask_sb), (s_mA, mask_sa), (s_hm, head_mask)):
                    sp.dma_start(dst, src).then_inc(sconst_in, 16)
                sp.dma_start(s_newA, zS_scr[:, KVA:QB]).then_inc(snew_in, 16)
                sp.dma_start(s_newB.rearrange("p a n -> p (a n)"), zS_scr[:, KB:END]).then_inc(snew_in, 16)
                sp.dma_start(s_newq[:, 0, :], zS_scr[:, QA:KVA]).then_inc(snew_in, 16)
                sp.dma_start(s_newq[:, 1, :], zS_scr[:, QB:KB]).then_inc(snew_in, 16)
                with repeat(sp, 0, NS // 2) as i:
                    for b in range(2):
                        r = 2 * i + b
                        hold(sp, "sp", s_mul, r - 1)
                        for dst, src in cache_rows(s_k[b], r, 0):
                            sp.dma_start(dst, src).then_inc(sk_in[b], 16)
                        sp.dma_start(s_kA[b], cache_swa[ds(r, 1), :].rearrange(
                            "r (s n) -> (r s) n", n=256)[:, 0:P]).then_inc(sk_in[b], 16)
                        sp.dma_start(s_q[b][:, 0:512], zS_scr[ds(r, 1), QA:KVA].broadcast_to([P, 512]))\
                          .then_inc(sk_in[b], 16)
                        sp.dma_start(s_q[b][:, 512:1024], zS_scr[ds(r, 1), QB:KB].broadcast_to([P, 512]))\
                          .then_inc(sk_in[b], 16)
                hold(sp, "sp", s_own_set, 1)
                with repeat(sp, 0, NS // 2) as i:
                    for b in range(2):
                        r = 2 * i + b
                        hold(sp, "sp", s_pv, r - 1)
                        for dst, src in cache_rows(s_v[b], r, 1):
                            sp.dma_start(dst, src).then_inc(sv_in[b], 16)
                        sp.dma_start(s_vA[b], cache_swa[ds(r, 1), :].rearrange(
                            "r (s n) -> (r s) n", n=256)[:, P:256]).then_inc(sv_in[b], 16)

            def att_tile(t):
                first = isinstance(t, int) and t == 0
                if not first:
                    hold(sp, "sp", att_s, 8 * t)
                    hold(sp, "sp", att_max, 8 * t)
                    hold(sp, "sp", att_pv, 8 * t)
                sp.dma_start(maskB[:, :], mask_b[:, ds((NT - 1 - t) * P, D)]).then_inc(att_in, 16)
                if first:
                    sp.dma_start(kTA[:, P:256], kTA_scr[:, 0:P]).then_inc(att_in, 16)
                    sp.dma_start(vA[:, 1, :], kvA_scr[0:P, P:256]).then_inc(att_in, 16)
                else:
                    sp.dma_start(kTA[:, :], kTA_scr[:, ds((t - 1) * P, 256)]).then_inc(att_in, 16)
                    sp.dma_start(vA[:, :, :], kvA_scr[ds((t - 1) * P, 256), P:256].rearrange(
                        "(b p) n -> p b n", p=P)).then_inc(att_in, 16)

            def att_q(t, p, par):
                hold(sp, "sp", att_s, 8 * t + 2 * p + par - 1)
                rows = slice(64 * par, 64 * par + 64)
                src = qT_scr.rearrange("(m b) r n -> b r m n", m=2)[ds(p, 1), rows, :, ds(t * P, P)]
                sp.dma_start(qpad[rows, par, :, :], src.rearrange("b r m n -> (b r) m n")).then_inc(qT_in[par], 16)

            wo_v = w_out.rearrange("(k p) n -> k p n", p=P)

            def w_out_chunks(t, chunks):
                for k in chunks:
                    hold(sp, "sp", wo_used, KD * t + k + 1 - WO_SLOTS)
                    sp.dma_start(wo_sb[:, k % WO_SLOTS, :], wo_v[k]).then_inc(wo_in[k % WO_SLOTS], 16)

            def loads(t):
                _, tp, ta = tiles_of(t)
                if ta is not None:
                    att_tile(ta)
                    att_q(ta, 0, 0)
                    att_q(ta, 0, 1)
                if tp is not None:
                    if begun(t):
                        hold(sp, "sp", acc_init, tp)
                    sp.dma_start(x2[:, :], x_all[ds(tp * P, P), :]).then_inc(mx_in, 16)
                    w_out_chunks(tp, range(WO_SLOTS, KD))
                if not (isinstance(t, int) and t == NT - 1):
                    w_out_chunks(t + 2, range(WO_SLOTS))
                if not isinstance(t, int) or t >= 1:
                    store_y(t - 1)
                if ta is not None:
                    with repeat(sp, 1, 4) as p:
                        att_q(ta, p, 0)
                        att_q(ta, p, 1)

            def store_y(t):
                hold(sp, "sp", fin_y, t + 1)
                sp.dma_start(y_p[ds(t * P, P), :], ybuf[:, :]).then_inc(y_out, 16)

            hold(sp, "sp", pads, 1)
            loads(-2)
            sp.dma_start(wq_sb[:, :, :], w_q.rearrange("(k p) n -> p k n", p=P)).then_inc(wq_in, 16)
            sp.dma_start(swa_p, kvA_scr[(NT - 1) * P:NT * P, :]).then_inc(swa_out, 16)
            loads(-1)
            loads(0)
            with repeat(sp, 1, NT - 2) as t:
                loads(t)
            loads(NT - 2)
            sample_loads()
            loads(NT - 1)
            store_y(NT - 1)
            hold(sp, "sp", fin_y, NT + 1)
            sp.dma_start(y_s, ybuf[0:NS, :]).then_inc(y_out, 16)
            hold(sp, "sp", y_out, 16 * (NT + 1))
            sp.wait_ge(cache_out, 16 * (NT + 1))
            sp.wait_ge(swa_out, 16)

        @block.gpsimd
        def _(pool):
            set_starts(pool, "pool")
            with repeat(pool, 0, NT) as t:
                hold(pool, "pool", a_ze, 5 * t + 5)
                pool.tensor_copy(VB[:, ds(t, 1), :].rearrange("p t n -> p (t n)"), z[:, VB_:END]).then_inc(a_vb, 1)

            def fetch(buf, table, win, landed):
                pool.indirect_dma_start(buf, None, table, bass.IndirectOffsetOnAxis(win, 0)).then_inc(landed, 16)

            def section(t, p, par, last=False):
                head = 2 * p + par
                s = 8 * t + head
                nxt = s + 1
                pool.tensor_copy(win_v[:, par, :], win_u[:, par, :]).then_inc(win_cp, 1)
                if not last:
                    hold(pool, "pool", pr_idx, 4 * t + p + 1 + par)
                    col = 0 if isinstance(p, int) and p == 3 and par == 1 else (head + 1) * TOPK
                    pool.tensor_copy(win_u[:, 1 - par, :], idx_all[:, ds(col, TOPK)]).then_inc(win_set, 1)
                    hold(pool, "pool", win_set, nxt + 1)
                hold(pool, "pool", win_cp, s + 1)
                for j in range(TOPK):
                    if not last:
                        hold(pool, "pool", u_used, TOPK * nxt + j - RING + 1)
                        fetch(u_ring[j % RING], peer_u, win_u[:, 1 - par, j:j + 1], u_in[j % RING])
                    hold(pool, "pool", v_used, TOPK * s + j - RING + 1)
                    fetch(v_ring[j % RING], peer_v, win_v[:, par, j:j + 1], v_in[j % RING])

            hold(pool, "pool", pr_idx, 1)
            pool.tensor_copy(win_u[:, 0, :], idx_all[:, 0:TOPK]).then_inc(win_set, 1)
            hold(pool, "pool", win_set, 1)
            for j in range(TOPK):
                hold(pool, "pool", u_used, j - RING + 1)
                fetch(u_ring[j % RING], peer_u, win_u[:, 0, j:j + 1], u_in[j % RING])
            with repeat(pool, 0, NT - 1) as t:
                with repeat(pool, 0, 3) as p:
                    section(t, p, 0)
                    section(t, p, 1)
                section(t, 3, 0)
                section(t, 3, 1)
            with repeat(pool, 0, 3) as p:
                section(NT - 1, p, 0)
                section(NT - 1, p, 1)
            section(NT - 1, 3, 0)
            section(NT - 1, 3, 1, last=True)
            hold(pool, "pool", gs_idx, 1)
            for r in range(NS):
                n = TOPK * HEADS * NT + r
                hold(pool, "pool", u_used, n - RING + 1)
                fetch(u_ring[r % RING], peer_u, idxT[:, r:r + 1], u_in[r % RING])
            for r in range(NS):
                n = TOPK * HEADS * NT + r
                hold(pool, "pool", v_used, n - RING + 1)
                fetch(v_ring[r % RING], peer_v, idxT[:, r:r + 1], v_in[r % RING])

        @block.tensor
        def _(pe):
            set_starts(pe, "pe")

            def x_transposes(t):
                pe.wait_ge(a_xs, after(a_xs, t + 1))
                for k in range(KD):
                    m = pe.transpose(acc[:, k * P:(k + 1) * P], xs[:, k * P:(k + 1) * P], idn[:, :])
                m.then_inc(a_xt, 1)

            def z_chunk(t, c, first=False):
                c0, w = CHUNKS[c]
                if first:
                    pe.wait_ge(win_in[c], 16)
                if c == 0:
                    pe.wait_ge(a_xT, after(a_xT, t + 1))
                    pe.wait_ge(a_ze, after(a_ze, 5 * t))
                if c == 1:
                    pe.wait_ge(a_te, after(a_te, 4 * t))
                for k in range(KD):
                    m = pe.matmul(zbank[c][:, 0:w], TT[:, k, :], w_in_sb[:, k, c0:c0 + w],
                                  start=(k == 0), stop=(k == KD - 1))
                m.then_inc(a_z, 1)

            def qk_transposes(t):
                pe.wait_ge(a_rope, after(a_rope, 2 * t + 2))
                pe.wait_ge(a_ze, after(a_ze, 5 * t + 4))
                for b in range(4):
                    m = pe.transpose(pS[:, 512 + b * P:512 + (b + 1) * P], z[:, b * P:(b + 1) * P], idn[:, :])
                m.then_inc(a_rt, 1)
                for b in range(4):
                    m = pe.transpose(pA[:, b * P:(b + 1) * P], z[:, QB + b * P:QB + (b + 1) * P], idn[:, :])
                m.then_inc(a_rt, 1)
                for b in range(4):
                    m = pe.transpose(pM[:, b * P:(b + 1) * P], z[:, KB + b * P:KB + (b + 1) * P], idn[:, :])
                m.then_inc(a_rt, 1)
                pe.transpose(pT[:, 0:P], z[:, KVA:KVA + P], idn[:, :]).then_inc(a_rt, 1)

            def project(t, first=False, last=False):
                z_chunk(t, 0, first)
                z_chunk(t, 1, first)
                if not last:
                    x_transposes(t + 1)
                for c in (2, 3, 4):
                    z_chunk(t, c, first)
                if not last:
                    qk_transposes(t)

            pe.wait_ge(c_in, 16 * 10)
            x_transposes(0)
            project(0, first=True)
            with repeat(pe, 1, NT) as t:
                project(t)
            project(NT, last=True)

            pe.wait_ge(keys_in, 16)
            pe.wait_ge(a_ze, after(a_ze, 5 * NT + 5))
            pe.wait_ge(a_te, after(a_te, 4 * NT))
            for b in range(2):
                if b:
                    pe.wait_ge(k_te, after(k_te, 1))
                for k in range(8):
                    m = pe.transpose(pT[:, k * P:(k + 1) * P], hpair[:, b, k * P:(k + 1) * P], idn[:, :])
                m.then_inc(k_t, 1)

            pe.wait_ge(k_te, after(k_te, 2))

            def sample_scores():
                pe.wait_ge(s_mul, after(s_mul, NS))
                pe.transpose(pS[0:64, 0:P], s_sc[:, 0, :], idn[:, :])
                pe.transpose(pS[0:64, P:2 * P], s_sc[:, 1, :], idn[:, :])
                pe.transpose(pS[0:64, 256:264], s_scn[0:8, 0, :], idn[0:8, 0:8])
                pe.transpose(pS[0:64, 512:640], s_sc[:, 2, :], idn[:, :])
                pe.transpose(pS[0:64, 640:648], s_scn[0:8, 1, :], idn[0:8, 0:8]).then_inc(s_sT, 1)

            def sample_probs():
                pe.wait_ge(s_prob, after(s_prob, 1))
                i64 = idn[0:64, 0:64]
                pe.transpose(pT[:, 0:64], s_pB[0:64, 0:P], i64)
                pe.transpose(pT[:, 64:128], s_pB[0:64, P:2 * P], i64)
                pe.transpose(pT[:, 128:192], s_pA[0:64, 0:P], i64)
                pe.transpose(pT[0:8, 192:256], s_pB[0:64, 256:264], i64)
                pe.transpose(pT[0:8, 256:320], s_pA[0:64, P:136], i64).then_inc(s_bT, 1)

            def sample_pv(r):
                b = r % 2
                c = slice(64 * r, 64 * r + 64)
                last = r == NS - 1
                if r == 0:
                    pe.wait_ge(s_bTe, after(s_bTe, 1))
                    pe.matmul(pS[0:64, 0:512], s_pTn[0:8, 0, :], s_newB[:, 1, :], start=True, stop=False)
                    pe.matmul(pS[0:64, 512:640], s_pTn[0:8, 1, :], s_newA[:, P:256], start=True, stop=False)
                pe.wait_ge(sv_in[b], 64 * (r // 2 + 1))
                pe.matmul(pS[0:64, 0:512], s_pT[:, 0, c], s_v[b][:, 0, :], start=False, stop=False)
                pe.matmul(pS[0:64, 0:512], s_pT[:, 1, c], s_v[b][:, 1, :], start=False, stop=last)
                pe.matmul(pS[0:64, 512:640], s_pT[:, 2, c], s_vA[b], start=False, stop=last).then_inc(s_pv, 1)

            def sample_fold():
                pe.wait_ge(s_dg, after(s_dg, 1))
                for half in range(2):
                    m = pe.matmul(pT[0:8, half * 512:(half + 1) * 512], tok8[:, :],
                                  s_od[:, half * 512:(half + 1) * 512], start=True, stop=True)
                m.then_inc(s_fold, 1)

            def att_scores(t, p, par):
                a = 8 * t + 2 * p + par
                if place(p, par) == 0:
                    pe.wait_ge(att_in, 48 * (t + 1))
                    if begun(t - 1):
                        pe.wait_ge(mx_x2, after(mx_x2, t))
                pe.wait_ge(qT_in[par], 16 * (4 * t + p + 1))
                pe.wait_ge(att_max, after(att_max, a))
                pe.wait_ge(att_te, after(att_te, 3 * a))
                for b0, b1 in halves_of(blocks_of(t)):
                    pe.matmul(pS[:, b0 * P:b1 * P], qpad[:, par, 1, :], KTB[:, ds(p, 1), b0 * P:b1 * P],
                              start=True, stop=True)
                pe.matmul(pA[:, 0:256], qpad[:, par, 0, :], kTA[:, :], start=True, stop=True).then_inc(att_s, 1)

            def att_transposes(t, p, par):
                a = 8 * t + 2 * p + par
                pe.wait_ge(att_exp, after(att_exp, a + 1))
                if place(p, par) == 0 and begun(t - 1):
                    pe.wait_ge(mx_hT, after(mx_hT, t))
                halves = halves_of(blocks_of(t))
                for b0, b1 in halves:
                    for k in range(b0, b1):
                        m = pe.transpose(pT[:, k * P:(k + 1) * P], S_B[:, k * P:(k + 1) * P], idn[:, :])
                    m.then_inc(att_t, 2 // len(halves))
                for k in range(2):
                    m = pe.transpose(pA[:, 256 + k * P:256 + (k + 1) * P], S_A[:, k * P:(k + 1) * P], idn[:, :])
                m.then_inc(att_t, 1)

            def att_values(t, p, par):
                a = 8 * t + 2 * p + par
                pe.wait_ge(att_te, after(att_te, 3 * a + 3))
                if place(p, par) == 0:
                    if exists(t - 2, p, par, 1):
                        pe.wait_ge(pr_se, after(pr_se, 8 * (t - 1)))
                elif exists(t - 2, p, par, 1):
                    pe.wait_ge(pr_qe, after(pr_qe, a - 8))
                for k in range(blocks_of(t)):
                    pe.matmul(pM[:, 256:320], PT[:, k, :], VB[:, k, ds(p * P + par * HD, HD)],
                              start=(k == 0), stop=(k == blocks_of(t) - 1))
                for k in range(2):
                    m = pe.matmul(pM[:, 320:384], PT[:, 8 + k, :], vA[:, k, par * HD:(par + 1) * HD],
                                  start=(k == 0), stop=(k == 1))
                m.then_inc(att_pv, 1)

            def out_transposes(t):
                pe.wait_ge(mx_on, after(mx_on, t + 1))
                for k in range(KD):
                    m = pe.transpose(pT[:, k * P:(k + 1) * P], S[:, k * P:(k + 1) * P], idn[:, :])
                m.then_inc(mx_t, 1)

            def out_projection(t, k):
                if k == 0:
                    pe.wait_ge(mx_onT, after(mx_onT, t + 1))
                pe.wait_ge(wo_in[k % WO_SLOTS], 16 * ((KD // WO_SLOTS) * t + k // WO_SLOTS + 1))
                for half in range(2):
                    m = pe.matmul(pS[:, half * 512:(half + 1) * 512], PT[:, k, :],
                                  wo_sb[:, k % WO_SLOTS, half * 512:(half + 1) * 512],
                                  start=(k == 0), stop=(k == KD - 1))
                m.then_inc(wo_used, 1)

            def h_gain():
                for k in range(KD):
                    m = pe.matmul(pT[:, k * P:(k + 1) * P], idn[0:KD, k:k + 1].broadcast_to([KD, P]),
                                  grow[0:KD, :], start=True, stop=True)
                m.then_inc(mx_mm, 1)

            def h_transposes(t):
                pe.wait_ge(mx_h, after(mx_h, t + 1))
                for k in range(KD):
                    m = pe.transpose(pT[:, k * P:(k + 1) * P], h_next[:, k * P:(k + 1) * P], idn[:, :])
                m.then_inc(mx_ht, 1)

            def peer_query(t, b, p, par, att):
                if isinstance(b, int) and b == 0:
                    pe.wait_ge(wq_in, 16)
                pe.wait_ge(mx_hT, after(mx_hT, t + 1))
                pe.wait_ge(pr_se, after(pr_se, b))
                pe.wait_ge(att_o, after(att_o, att))
                for k in range(KD):
                    m = pe.matmul(pM[:, 0:256], TT[:, k, :], wq_sb[:, k, ds(p * 512 + par * 256, 256)],
                                  start=(k == 0), stop=(k == KD - 1))
                m.then_inc(pr_q, 1)

            def peer_transposes(b, att):
                pe.wait_ge(pr_qe, after(pr_qe, b + 1))
                pe.wait_ge(att_te, after(att_te, 3 * att))
                for k in range(2):
                    m = pe.transpose(pA[:, k * P:(k + 1) * P], pq[:, k * P:(k + 1) * P], idn[:, :])
                m.then_inc(pr_t, 1)

            def peer_scores(b, p, par, att):
                pe.wait_ge(pr_te, after(pr_te, b + 1))
                pe.wait_ge(att_o, after(att_o, att))
                for k in range(2):
                    m = pe.matmul(pM[:, k * P:(k + 1) * P], pqT[:, k, :],
                                  keysT[:, ds(4 * p + 2 * par + k, 1), :], start=True, stop=True)
                m.then_inc(pr_s, 1)

            def weigh(s, j):
                n = TOPK * s + j
                pe.wait_ge(diag_set, after(diag_set, n + 1))
                pe.wait_ge(v_in[j % RING], 16 * (4 * s + j // RING + 1))
                for half in range(2):
                    m = pe.matmul(acc[:, half * 512:(half + 1) * 512], diag[:, j % 4, :],
                                  v_ring[j % RING][:, half * 512:(half + 1) * 512],
                                  start=False, stop=False, skip_group_check=True)
                m.then_inc(v_used, 1)

            def acc_start(t, rows=P):
                pe.wait_ge(mx_h, after(mx_h, t + 1))
                if not (isinstance(t, int) and t == 0):
                    pe.wait_ge(fin_free, after(fin_free, t))
                for half in range(2):
                    m = pe.matmul(acc[0:rows, half * 512:(half + 1) * 512], idn[:, 0:rows],
                                  x2[:, half * 512:(half + 1) * 512], start=True, stop=False,
                                  skip_group_check=True)
                m.then_inc(acc_init, 1)

            def section(t, p, par):
                tg, tp, ta = tiles_of(t)
                h = place(p, par)
                b = 8 * (t + 1) + 2 * p + par - 1
                peer = exists(t, p, par, 1)
                of_peer = t if h == 0 else t + 1
                before = NT * 8 if ta is None else 8 * ta + 2 * p + par
                att = before if ta is None or h == 0 else before + 1
                out = t + 2 if h == 7 and has_next(t) else None
                s_, t_, v_ = (9, 13, 15) if h == 0 else (0, 5, 8)
                last = is_last(t, p, par)
                q_, qt_, qs_ = (0, 3, 5) if h == 0 or last else (2, 9, 12)
                if h == 0 and tg is not None:
                    acc_start(tg)
                for j in range(TOPK):
                    if peer and j == q_:
                        peer_query(of_peer, b, *back(p, par, 1), before)
                    if ta is not None and j == s_:
                        att_scores(ta, p, par)
                    if ta is not None and j == t_:
                        att_transposes(ta, p, par)
                    if ta is not None and j == v_:
                        att_values(ta, p, par)
                    if peer and j == qt_:
                        peer_transposes(b, att)
                    if peer and j == qs_:
                        peer_scores(b, *back(p, par, 1), att)
                    if last and j == 8:
                        peer_query(NT, b + 1, p, par, before)
                    if last and j == 10:
                        peer_transposes(b + 1, att)
                    if last and j == 12:
                        peer_scores(b + 1, p, par, att)
                    if out is not None and j == 13:
                        out_transposes(out)
                    if out is not None and j >= 14:
                        out_projection(out, j - 14)
                    if h == 0 and tp is not None:
                        if 1 <= j <= 6:
                            out_projection(tp, j + 1)
                        if j == 6:
                            h_gain()
                        if j == 10:
                            h_transposes(tp)
                    if sample_step(t, p, par, j) == "scores":
                        sample_scores()
                    if sample_step(t, p, par, j) == "probs":
                        sample_probs()
                    if isinstance(sample_step(t, p, par, j), int):
                        sample_pv(sample_step(t, p, par, j))
                    if sample_step(t, p, par, j) == "fold":
                        sample_fold()
                    if tg is not None:
                        weigh(8 * tg + 2 * p + par, j)

            def sample_step(t, p, par, j):
                if not isinstance(t, int) or t != NT - 2:
                    return None
                return {(5, 0): "scores", (5, 8): "probs", (5, 11): 0, (5, 14): 1, (6, 1): 2, (6, 4): 3, (6, 6): 4,
                        (6, 8): 5, (6, 11): 6, (6, 14): 7, (7, 5): "fold"}.get((2 * p + par, j))

            iterations(pe, section)
            pe.wait_ge(gs_in, after(gs_in, 1))
            pe.transpose(pA[:, 0:8], S[0:8, 0:P], idn[0:8, 0:8])
            pe.transpose(pA[:, 8:16], gates[0:8, :], idn[0:8, 0:8]).then_inc(gs_t, 1)
            acc_start(NT, NS)
            for r in range(NS):
                bank = (pS, pT)[r % 2]
                if r >= 2:
                    pe.wait_ge(u_used, after(u_used, TOPK * 8 * NT + r - 1))
                for half in range(2):
                    m = pe.matmul(bank[:, half * 512:(half + 1) * 512], idn[:, r:r + 1].broadcast_to([P, P]),
                                  h_next[:, half * 512:(half + 1) * 512], start=True, stop=True)
                m.then_inc(gs_h, 1)
            pe.wait_ge(gs_w, after(gs_w, 1))
            for r in range(NS):
                pe.wait_ge(v_in[r % RING], 16 * (4 * 8 * NT + r // RING + 1))
                for half in range(2):
                    m = pe.matmul(acc[0:NS, half * 512:(half + 1) * 512], wz[:, r, :],
                                  v_ring[r % RING][:, half * 512:(half + 1) * 512],
                                  start=False, stop=False, skip_group_check=True)
                m.then_inc(v_used, 1)

        @block.scalar
        def _(act):
            set_starts(act, "act")

            def copy(out, in_):
                return act.activation(out, in_, ACT.Copy)

            def z_copies(t):
                for c, (c0, w) in enumerate(CHUNKS):
                    act.wait_ge(a_z, after(a_z, 5 * t + c + 1))
                    if c == 0:
                        act.wait_ge(z_out, after(z_out, 32 * t))
                        act.wait_ge(a_vb, after(a_vb, t))
                        act.wait_ge(a_rt, after(a_rt, 4 * t))
                    if c == 0:
                        copy(z[:, 0:512].rearrange("p (b a d) -> p a b d", a=2, b=4),
                             zbank[0].rearrange("p (a b d) -> p a b d", a=2, b=4)).then_inc(a_ze, 1)
                    else:
                        copy(z[:, c0:c0 + w], zbank[c][:, 0:w]).then_inc(a_ze, 1)

            with repeat(act, 0, NT) as t:
                z_copies(t)
                act.wait_ge(q_out, after(q_out, 32 * t))
                act.wait_ge(a_rt, after(a_rt, 4 * t + 1))
                copy(qTe[:, 0:4, :], pS[:, 512:1024].rearrange("p (b n) -> p b n", b=4)).then_inc(a_te, 1)
                act.wait_ge(a_rt, after(a_rt, 4 * t + 2))
                copy(qTe[:, 4:8, :], pA[:, :].rearrange("p (b n) -> p b n", b=4)).then_inc(a_te, 1)
                act.wait_ge(a_rt, after(a_rt, 4 * t + 3))
                copy(KTB[:, :, ds(t * P, P)], pM[:, :].rearrange("p (b n) -> p b n", b=4)).then_inc(a_te, 1)
                act.wait_ge(a_rt, after(a_rt, 4 * t + 4))
                copy(kTAe, pT[:, 0:P]).then_inc(a_te, 1)
            z_copies(NT)
            for b in range(2):
                act.wait_ge(k_t, after(k_t, b + 1))
                copy(keysT[:, 8 * b:8 * b + 8, :], pT[:, :].rearrange("p (h k) -> p h k", h=8)).then_inc(k_te, 1)

            def sample_exp():
                act.wait_ge(s_max, after(s_max, 1))
                act.activation(s_pB[0:64, :], s_pB[0:64, :], ACT.Exp, bias=anm[0:64, 0:1], accum_out=aden[0:64, 0:1])
                act.activation(s_pA[0:64, :], s_pA[0:64, :], ACT.Exp, bias=anm[0:64, 1:2], accum_out=aden[0:64, 1:2])
                act.activation(aden[0:64, 2:3], s_sink, ACT.Exp, bias=anm[0:64, 1:2]).then_inc(s_exp, 1)

            def sample_pT():
                act.wait_ge(s_bT, after(s_bT, 1))
                act.wait_ge(s_zero, after(s_zero, 1))
                for k in range(3):
                    copy(s_pT[:, k, :].rearrange("p (r x) -> p r x", x=72)[:, :, 0:8],
                         pT[:, 64 * k:64 * k + 64].rearrange("p (r x) -> p r x", x=8))
                copy(s_pTn[0:8, :, :], pT[0:8, 192:320].rearrange("p (s n) -> p s n", s=2)).then_inc(s_bTe, 1)

            def att_softmax(t, p, par):
                a = 8 * t + 2 * p + par
                act.wait_ge(att_max, after(att_max, a + 1))
                B = S_B[:, 0:blocks_of(t) * P]
                act.activation(B, B, ACT.Exp, bias=anm[:, 0:1], accum_out=aden[:, 0:1])
                act.activation(S_A, S_A, ACT.Exp, bias=anm[:, 1:2], accum_out=aden[:, 1:2])
                act.activation(aden[:, 2:3], sink[:, ds(p + 4 * par, 1)], ACT.Exp,
                               bias=anm[:, 1:2]).then_inc(att_exp, 1)

            def att_copies(t, p, par):
                a = 8 * t + 2 * p + par
                act.wait_ge(att_pv, after(att_pv, a))
                if place(p, par) == 0 and begun(t - 1):
                    act.wait_ge(mx_mm, after(mx_mm, t))
                halves = halves_of(blocks_of(t))
                for k, (b0, b1) in enumerate(halves):
                    act.wait_ge(att_t, after(att_t, 3 * a + (k + 1) * (2 // len(halves))))
                    copy(PT[:, b0:b1, :], pT[:, b0 * P:b1 * P].rearrange("p (b n) -> p b n", b=b1 - b0))\
                        .then_inc(att_te, 2 // len(halves))
                act.wait_ge(att_t, after(att_t, 3 * a + 3))
                copy(PT[:, 8:10, :], pA[:, 256:512].rearrange("p (b n) -> p b n", b=2)).then_inc(att_te, 1)

            def h_copies(t):
                act.wait_ge(mx_ht, after(mx_ht, t + 1))
                copy(TT[:, 0:4, :], pT[:, 0:512].rearrange("p (b n) -> p b n", b=4))
                copy(TT[:, 4:8, :], pT[:, 512:1024].rearrange("p (b n) -> p b n", b=4)).then_inc(mx_hT, 1)

            def tanh(s, par):
                act.wait_ge(gl_in, after(gl_in, s + 1))
                act.activation(gl[:, 1, :], gl[:, 0, :], ACT.Tanh, scale=GELU_C).then_inc(gl_th, 1)

            def peer_query(b):
                act.wait_ge(pr_q, after(pr_q, b + 1))
                act.wait_ge(pr_t, after(pr_t, b))
                copy(pq[:, :], pM[:, 0:256]).then_inc(pr_qe, 1)

            def peer_queryT(b):
                act.wait_ge(pr_t, after(pr_t, b + 1))
                copy(pqT[:, :, :], pA[:, 0:256].rearrange("p (b n) -> p b n", b=2)).then_inc(pr_te, 1)

            def peer_scores(b):
                act.wait_ge(pr_s, after(pr_s, b + 1))
                act.wait_ge(pr_read, after(pr_read, b))
                copy(sc[:, :, :], pM[:, 0:256].rearrange("p (b n) -> p b n", b=2)).then_inc(pr_se, 1)

            def peer_exp(b, par):
                act.wait_ge(pr_top, after(pr_top, b + 1))
                act.activation(gexp[:, :], candv[:, par, :], ACT.Exp, bias=gsm[:, 0:1],
                               accum_out=gsm[:, 1:2]).then_inc(pr_exp, 1)

            def take_tile(t, rows=P):
                act.wait_ge(v_used, after(v_used, TOPK * 8 * (t + 1) if rows == P else TOPK * 8 * NT + NS))
                act.wait_ge(y_out, after(y_out, 16 * t))
                copy(ybuf[0:rows, :], acc[0:rows, :]).then_inc(fin_free, 1)

            def section(t, p, par):
                tg, tp, ta = tiles_of(t)
                h = place(p, par)
                b = 8 * (t + 1) + 2 * p + par - 1
                peer = exists(t, p, par, 1)
                rank = exists(t, p, par, 2)
                last = is_last(t, p, par)
                soon = h == 0 or last
                if h == 0 and (not isinstance(t, int) or t >= 1):
                    take_tile(t - 1)
                if tg is not None:
                    s = 8 * tg + 2 * p + par
                    tanh(s, par)
                    act.wait_ge(w_set, after(w_set, s + 1))
                for j in range(TOPK):
                    if tg is not None:
                        n = TOPK * s + j
                        act.wait_ge(v_used, after(v_used, n - 3))
                        act.activation(diag[:, j % 4, :], idn[:, :], ACT.Copy,
                                       scale=wv[:, par, j:j + 1]).then_inc(diag_set, 1)
                    if ta is not None and j == (12 if h == 0 else 3):
                        att_softmax(ta, p, par)
                    if peer and j == (1 if soon else 4):
                        peer_query(b)
                    if ta is not None and j == (14 if h == 0 else 7):
                        att_copies(ta, p, par)
                    if peer and j == (4 if soon else 10):
                        peer_queryT(b)
                    if peer and j == (6 if soon else 13):
                        peer_scores(b)
                    if rank and j == (7 if last else 14):
                        peer_exp(b - 1, par)
                    if last and j == 9:
                        peer_query(b + 1)
                    if last and j == 11:
                        peer_queryT(b + 1)
                    if last and j == 13:
                        peer_scores(b + 1)
                    if last and j == 15:
                        peer_exp(b, 1 - par)
                    if h == 0 and tp is not None and j == 11:
                        h_copies(tp)
                    if isinstance(t, int) and t == NT - 2 and h == 5:
                        if j == 2:
                            sample_exp()
                        if j == 9:
                            sample_pT()

            iterations(act, section)
            peer_exp(8 * (NT + 1) - 1, 1)
            take_tile(NT - 1)
            act.wait_ge(gs_in, after(gs_in, 2))
            act.activation(gl[:, 1, 0:NS], gl[:, 0, 0:NS], ACT.Tanh, scale=GELU_C).then_inc(gs_th, 1)
            take_tile(NT, NS)

        @block.vector
        def _(dve):
            set_starts(dve, "dve")
            D_ = dve.drain

            dve.memset(qpad[:, :, :, :], 0.0)
            dve.memset(kTA[:, 0:P], 0.0)
            dve.memset(vA[:, 0, :], 0.0).then_inc(pads, 1)

            def sum_squares(x, n, out, junk, rows=P):
                dve.tensor_tensor_reduce(junk, x, x, 1.0, 0.0, ALU.mult, ALU.add, out)

            def rsqrt(rows, cols, count):
                r, c = slice(0, rows), slice(0, cols)
                D_()
                dve.tensor_scalar(nw_x[r, c], ssum[r, c], 1.0 / count, EPS, ALU.mult, ALU.add)
                D_()
                dve.tensor_scalar(nw_i[r, c], nw_x[r, c].bitcast(I32), 1, None, ALU.arith_shift_right)
                D_()
                dve.tensor_scalar(nw_i[r, c], nw_i[r, c], -1.0, MAGIC, ALU.mult, ALU.add)
                y = nw_i[r, c].bitcast(F32)
                for _ in range(3):
                    D_()
                    dve.tensor_tensor(nw_a[r, c], y, y, ALU.mult)
                    D_()
                    dve.scalar_tensor_tensor(nw_b[r, c], nw_a[r, c], -0.5, nw_x[r, c], ALU.mult, ALU.mult)
                    D_()
                    dve.scalar_tensor_tensor(nw_y[r, c], nw_b[r, c], 1.5, y, ALU.add, ALU.mult)
                    y = nw_y[r, c]
                D_()

            def with_gain(which, out, psum, done):
                for half in range(2):
                    g = gcol[:, which, 4 * half:4 * half + 4].unsqueeze(2).broadcast_to([P, 4, P])
                    i = dve.tensor_tensor(out[:, 4 * half:4 * half + 4, :],
                                          psum[:, 512 * half:512 * half + 512].rearrange("p (b n) -> p b n", b=4),
                                          g, ALU.mult)
                i.then_inc(done, 1)

            def scale_x(t):
                dve.wait_ge(x_in, 16 * (t + 1))
                sum_squares(xin, D, ssum[:, 0:1], xs)
                rsqrt(P, 1, D)
                dve.tensor_scalar(xs, xin, nw_y[:, 0:1], None, ALU.mult).then_inc(a_xs, 1)

            def x_gain(t):
                dve.wait_ge(a_xt, after(a_xt, t + 1))
                dve.wait_ge(a_z, after(a_z, 5 * t))
                with_gain(0, TT, acc, a_xT)

            def rope(t, c0, heads):
                zr = z[:, c0:c0 + heads * HD].rearrange("p (h d) -> p h d", d=HD)[:, :, 0:16]
                lo, hi = zr[:, :, 0:8], zr[:, :, 8:16]
                cos = rcs[:, ds(t, 1), 0:8].broadcast_to([P, heads, 8])
                sin = rcs[:, ds(t, 1), 8:16].broadcast_to([P, heads, 8])
                tmp = rtmp[:, 0:4 * heads * 8].rearrange("p (a h d) -> p a h d", a=4, h=heads)
                dve.tensor_tensor(tmp[:, 0, :, :], lo, cos, ALU.mult)
                dve.tensor_tensor(tmp[:, 1, :, :], hi, sin, ALU.mult)
                dve.tensor_tensor(tmp[:, 2, :, :], hi, cos, ALU.mult)
                dve.tensor_tensor(tmp[:, 3, :, :], lo, sin, ALU.mult)
                D_()
                dve.tensor_tensor(lo, tmp[:, 0, :, :], tmp[:, 1, :, :], ALU.subtract)
                dve.tensor_tensor(hi, tmp[:, 2, :, :], tmp[:, 3, :, :], ALU.add).then_inc(a_rope, 1)

            def rope_tile(t):
                dve.wait_ge(a_ze, after(a_ze, 5 * t + 2))
                rope(t, QA, 10)
                D_()
                dve.wait_ge(a_ze, after(a_ze, 5 * t + 4))
                rope(t, QB, 16)

            dve.wait_ge(c_in, 16 * 10)
            scale_x(0)
            x_gain(0)
            with repeat(dve, 0, NT) as t:
                scale_x(t + 1)
                rope_tile(t)
                x_gain(t + 1)
            rope_tile(NT)

            def dot_heads(out, k, q, n, rows, groups):
                prod = s_prod[0:rows, 0:n]
                D_()
                dve.tensor_tensor(prod.rearrange("p (a b c) -> p a b c", a=groups[0], b=groups[1]), k, q, ALU.mult)
                D_()
                return dve.tensor_reduce(out, prod.rearrange("p (a b d) -> p a b d", d=HD, a=groups[2]),
                                         AX_X, ALU.add)

            def sample_own():
                dve.wait_ge(snew_in, 64)
                dot_heads(s_own[:, 0:1, :], s_newB[:, 0, :].unsqueeze(1).unsqueeze(1),
                          s_newq[:, 1, :].unsqueeze(1).unsqueeze(1), 512, 8, (1, 1, 1))
                dot_heads(s_own[:, 1:2, :], s_newA[:, 0:P].rearrange("p (a d) -> p a d", a=2)
                          .unsqueeze(2).broadcast_to([8, 2, 4, HD]),
                          s_newq[:, 0, :].rearrange("p (b a d) -> p a b d", a=2, b=4), 512, 8, (2, 4, 1))\
                    .then_inc(s_own_set, 1)
                D_()
                for k in range(2):
                    dve.tensor_copy(s_scn[0:8, k, :].rearrange("p (r h) -> p r h", r=NS),
                                    s_own[:, k, :].unsqueeze(1).broadcast_to([8, NS, HEADS]))

            def sample_dilated(r):
                b = r % 2
                dve.wait_ge(sk_in[b], 96 * (r // 2 + 1))
                dot_heads(s_sc[:, 0:2, 8 * r:8 * r + 8], s_k[b].unsqueeze(2),
                          s_q[b][:, 512:1024].unsqueeze(1).unsqueeze(1).broadcast_to([P, 2, 1, 512]),
                          1024, P, (2, 1, 2))

            def sample_window(r):
                b = r % 2
                dot_heads(s_sc[:, 2:3, 8 * r:8 * r + 8], s_kA[b].rearrange("p (a d) -> p a d", a=2)
                          .unsqueeze(2).broadcast_to([P, 2, 4, HD]),
                          s_q[b][:, 0:512].rearrange("p (b a d) -> p a b d", a=2, b=4), 512, P, (2, 4, 1))\
                    .then_inc(s_mul, 1)

            R = slice(0, 64)

            def sample_maxima():
                D_()
                dve.memset(s_pT[:, :, :], 0.0).then_inc(s_zero, 1)
                dve.wait_ge(s_sT, after(s_sT, 1))
                dve.wait_ge(sconst_in, 16 * (3 + NS))
                dve.tensor_tensor_reduce(s_pB[R, :], pS[R, 0:264], s_mB, 0.125, NEG, ALU.add, ALU.max, amax[R, 0:1])
                dve.tensor_tensor_reduce(s_pA[R, :], pS[R, 512:648], s_mA, 0.125, NEG, ALU.add, ALU.max,
                                         amax[R, 1:2])
                D_()
                dve.tensor_tensor(amax[R, 1:2], amax[R, 1:2], s_sink, ALU.max)
                D_()
                dve.tensor_scalar(anm[R, :], amax[R, :], -1.0, None, ALU.mult).then_inc(s_max, 1)

            def sample_divide():
                dve.wait_ge(s_exp, after(s_exp, 1))
                dve.tensor_tensor(aden[R, 1:2], aden[R, 1:2], aden[R, 2:3], ALU.add)
                D_()
                dve.reciprocal(arden[R, :], aden[R, 0:2])
                D_()
                dve.tensor_scalar(s_pB[R, :], s_pB[R, :], arden[R, 0:1], None, ALU.mult)
                dve.tensor_scalar(s_pA[R, :], s_pA[R, :], arden[R, 1:2], None, ALU.mult).then_inc(s_prob, 1)

            def sample_own_columns():
                dve.wait_ge(s_pv, after(s_pv, NS))
                D_()
                dve.tensor_tensor(s_od[:, 0:512].rearrange("p (a b d) -> p a b d", a=2, b=4),
                                  pS[R, 512:640].rearrange("p (a d) -> p a d", a=2).unsqueeze(2)
                                  .broadcast_to([64, 2, 4, HD]),
                                  s_hm.rearrange("p (a b d) -> p a b d", a=2, b=4), ALU.mult)
                dve.tensor_tensor(s_od[:, 512:1024], pS[R, 0:512], s_hm, ALU.mult).then_inc(s_dg, 1)

            def sample_output():
                dve.wait_ge(s_fold, after(s_fold, 1))
                dve.tensor_copy(s_o, pT[0:8, :])

            def sample_step(h, j):
                if h == 1 and j == 0:
                    sample_own()
                if 1 <= h <= 4 and j in (1, 7):
                    sample_dilated(2 * h - 2 + (j == 7))
                if 1 <= h <= 4 and j in (2, 10):
                    sample_window(2 * h - 2 + (j == 10))
                if (h, j) == (5, 1):
                    sample_maxima()
                if (h, j) == (5, 7):
                    sample_divide()
                if (h, j) == (7, 2):
                    sample_own_columns()
                if (h, j) == (7, 7):
                    sample_output()

            def att_maxima(t, p, par, first):
                a = 8 * t + 2 * p + par
                dve.wait_ge(att_s, after(att_s, a + 1))
                hold(dve, "dve", att_t, 3 * a)
                n = blocks_of(t) * P
                dve.tensor_tensor_reduce(S_B[:, 0:n], pS[:, 0:n], maskB[:, 0:n], 0.125, NEG, ALU.add, ALU.max,
                                         amax[:, 0:1])
                dve.tensor_tensor_reduce(S_A, pA[:, 0:256], maskA[:, 0 if first else 1, :], 0.125, NEG,
                                         ALU.add, ALU.max, amax[:, 1:2])
                D_()
                dve.tensor_tensor(amax[:, 1:2], amax[:, 1:2], sink[:, ds(p + 4 * par, 1)], ALU.max)
                D_()
                dve.tensor_scalar(anm[:, :], amax[:, :], -1.0, None, ALU.mult).then_inc(att_max, 1)

            def att_output(t, p, par):
                a = 8 * t + 2 * p + par
                dve.wait_ge(att_exp, after(att_exp, a + 1))
                dve.tensor_tensor(aden[:, 1:2], aden[:, 1:2], aden[:, 2:3], ALU.add)
                D_()
                dve.reciprocal(arden[:, :], aden[:, 0:2])
                D_()
                dve.wait_ge(att_pv, after(att_pv, a + 1))
                dve.tensor_scalar(o_all[:, ds(512 + p * P + par * HD, HD)], pM[:, 256:320], arden[:, 0:1],
                                  None, ALU.mult)
                dve.tensor_scalar(o_all[:, ds(p * HD + par * 256, HD)], pM[:, 320:384], arden[:, 1:2],
                                  None, ALU.mult).then_inc(att_o, 1)

            def out_squares(t):
                D_()
                for half in range(2):
                    c = slice(512 * half, 512 * half + 512)
                    sum_squares(o_all[:, c], 512, ssum[:, half:half + 1], S[:, c])

            def out_norm(t):
                rsqrt(P, 2, 512)
                for half in range(2):
                    c = slice(512 * half, 512 * half + 512)
                    i = dve.tensor_scalar(S[:, c], o_all[:, c], nw_y[:, half:half + 1], None, ALU.mult)
                i.then_inc(mx_on, 1)

            def out_gain(t):
                dve.wait_ge(mx_t, after(mx_t, t + 1))
                with_gain(1, PT, pT, mx_onT)

            def residual(t):
                dve.wait_ge(mx_mm, after(mx_mm, t + 1))
                dve.wait_ge(mx_in, 16 * (t + 1))
                dve.tensor_tensor(x2[:, :], x2[:, :], pS[:, :], ALU.add).then_inc(mx_x2, 1)
                D_()
                sum_squares(x2[:, :], D, ssum[:, 0:1], S_B)

            def norm_h(t):
                rsqrt(P, 1, D)
                dve.scalar_tensor_tensor(h_next, x2[:, :], nw_y[:, 0:1], pT[:, :], ALU.mult,
                                         ALU.mult).then_inc(mx_h, 1)

            def top8(values, places, scores):
                D_()
                dve.max(values, scores)
                D_()
                return dve.max_index(places, values, scores)

            def rank_half(b, par, half):
                if half == 0:
                    hold(dve, "dve", pr_se, b + 1)
                values, places, x = topv[:, par, half, :], topi[:, par, half, :], sc[:, half, :]
                top8(values[:, 0:8], places[:, 0:8], x)
                D_()
                dve.match_replace(x, values[:, 0:8], x, NEG)
                i = top8(values[:, 8:16], places[:, 8:16], x)
                if half == 1:
                    i.then_inc(pr_read, 1)

            sums = cand[:, :, :].rearrange("p a b -> p (a b)")

            def rank_sums(par):
                D_()
                dve.tensor_tensor(cand[:, :, :], topv[:, par, 0, :].unsqueeze(2).broadcast_to([P, TOPK, TOPK]),
                                  topv[:, par, 1, :].unsqueeze(1).broadcast_to([P, TOPK, TOPK]), ALU.add)
                top8(candv[:, par, 0:8], candp[:, par, 0:8], sums)

            def rank_rest(par):
                D_()
                dve.match_replace(sums, candv[:, par, 0:8], sums, NEG)
                top8(candv[:, par, 8:16], candp[:, par, 8:16], sums)
                dve.tensor_scalar(gsm[:, 0:1], candv[:, par, 0:1], -1.0, None, ALU.mult).then_inc(pr_top, 1)

            def gate(b, p, par):
                dve.wait_ge(pr_exp, after(pr_exp, b + 1))
                dve.reciprocal(gsm[:, 2:3], gsm[:, 1:2])
                D_()
                dve.tensor_scalar(gates[:, ds(p * 32 + par * TOPK, TOPK)], gexp[:, :], gsm[:, 2:3], None, ALU.mult)

            def numbers_half(half):
                D_()
                if half == 0:
                    dve.tensor_copy(topif[:, :, :, :], topi[:, :, :, :])
                    dve.tensor_scalar(candh[:, :, :], candp[:, :, :], 4, None, ALU.logical_shift_right)
                else:
                    dve.tensor_scalar(candh[:, :, :], candp[:, :, :], 15, None, ALU.bitwise_and)
                D_()
                dve.tensor_copy(candf[:, :, :], candh[:, :, :])
                D_()
                full = [P, 2, TOPK, TOPK]
                dve.tensor_tensor(onehot[:, :, :, :], candf[:, :, :].unsqueeze(3).broadcast_to(full),
                                  iota[:, :].unsqueeze(1).unsqueeze(1).broadcast_to(full), ALU.is_equal)
                D_()
                dve.tensor_tensor(onehot[:, :, :, :], onehot[:, :, :, :],
                                  topif[:, :, half, :].unsqueeze(2).broadcast_to(full), ALU.mult)
                D_()
                dve.tensor_reduce(sel[:, half, :, :], onehot[:, :, :, :], AX_X, ALU.add)

            def numbers(p, taken):
                D_()
                if taken is not None:
                    dve.wait_ge(win_set, after(win_set, taken))
                dve.scalar_tensor_tensor(
                    idx_all[:, ds(p * 32, 32)], sel[:, 0, :, :].rearrange("p a b -> p (a b)"), float(KEYS),
                    sel[:, 1, :, :].rearrange("p a b -> p (a b)"), ALU.mult, ALU.add).then_inc(pr_idx, 1)

            def dot(us, j, par):
                dve.wait_ge(u_in[j % RING], 16 * (4 * us + j // RING + 1))
                dve.tensor_tensor_reduce(u_ring[j % RING], u_ring[j % RING], h_cur, 1.0, 0.0, ALU.mult, ALU.add,
                                         dots[:, par, j:j + 1]).then_inc(u_used, 1)

            def gelu_arg(x, n):
                D_()
                dve.tensor_tensor(gl[:, 0, 0:n], x, x, ALU.mult)
                D_()
                dve.tensor_scalar(gl[:, 0, 0:n], gl[:, 0, 0:n], 0.044715, 1.0, ALU.mult, ALU.add)
                D_()
                return dve.tensor_tensor(gl[:, 0, 0:n], gl[:, 0, 0:n], x, ALU.mult)

            def gelu_gate(out, x, g, n):
                dve.scalar_tensor_tensor(gl[:, 2, 0:n], gl[:, 1, 0:n], 1.0, x, ALU.add, ALU.mult)
                D_()
                return dve.scalar_tensor_tensor(out, gl[:, 2, 0:n], 0.5, g, ALU.mult, ALU.mult)

            def final_norm(t, rows=P):
                r = slice(0, rows)
                junk = h_cur if isinstance(t, int) and t >= NT - 1 else h_next
                D_()
                hold(dve, "dve", fin_free, t + 1)
                sum_squares(ybuf[r, :], D, ssum[r, 0:1], junk[r, :])
                rsqrt(rows, 1, D)

            def final_gain(t, rows=P):
                r = slice(0, rows)
                dve.scalar_tensor_tensor(ybuf[r, :], ybuf[r, :], nw_y[r, 0:1], fgain[r, :], ALU.mult, ALU.mult)\
                    .then_inc(fin_y, 1)

            def section(t, p, par):
                tg, tp, ta = tiles_of(t)
                h = place(p, par)
                s = 8 * t + 2 * p + par
                b = s + 6
                rank = exists(t, p, par, 2)
                last = is_last(t, p, par)
                out = t + 2 if h == 7 and has_next(t) else None
                dots_next = tg is not None
                if last:
                    dots_next = False
                if tg is not None:
                    gelu_arg(dots[:, par, :], TOPK).then_inc(gl_in, 1)
                early = isinstance(t, int) and t == -1 and h >= 4
                if h == 7 and dots_next or early and h == 4:
                    dve.tensor_copy(h_cur, h_next)
                    D_()
                for j in range(TOPK):
                    if dots_next:
                        dot(s + 1, j, 1 - par)
                    if early and j in (2, 7, 10, 14):
                        dot(0, 4 * (h - 4) + (2, 7, 10, 14).index(j), 0)
                    if tg is not None and j == 0:
                        dve.wait_ge(gl_th, after(gl_th, s + 1))
                        gelu_gate(wv[:, par, :], dots[:, par, :], gates[:, ds(p * 32 + par * TOPK, TOPK)], TOPK)\
                            .then_inc(w_set, 1)
                    if ta is not None and j == (10 if h == 0 else 1):
                        att_maxima(ta, p, par, isinstance(t, int) and t == -2)
                    if h == 0 and (not isinstance(t, int) or t >= 1):
                        if j == 1:
                            final_norm(t - 1)
                        if j == 2:
                            final_gain(t - 1)
                    if rank and j in (3, 4):
                        rank_half(b, par, j - 3)
                    if rank and j == 5:
                        rank_sums(par)
                    if rank and j == 6:
                        rank_rest(par)
                    if h == 0 and tp is not None and j == 7:
                        residual(tp)
                    if h == 0 and tp is not None and j == 8:
                        norm_h(tp)
                    if isinstance(t, int) and t == NT - 2:
                        sample_step(h, j)
                    if rank and j == (7 if last else 15):
                        gate(b, *back(p, par, 2))
                    if ta is not None and j == (15 if h == 0 else 9):
                        att_output(ta, p, par)
                    if out is not None and j == 10:
                        out_squares(out)
                    if out is not None and j == 11:
                        out_norm(out)
                    if out is not None and j == 14:
                        out_gain(out)
                    if rank and par == 1 and j == (8 if last else 12 if h == 7 else 11):
                        numbers_half(0)
                    if rank and par == 1 and j == (8 if last else 13):
                        numbers_half(1)
                        numbers(back(p, par, 2)[0], s - 1 if begun(t) else None)
                    if last and j == 9:
                        for half in range(2):
                            rank_half(b + 1, 1 - par, half)
                        rank_sums(1 - par)
                        rank_rest(1 - par)
                    if last and j == 15:
                        gate(b + 1, *back(p, par, 1))

            iterations(dve, section)
            b = 8 * (NT + 1) - 1
            for half in range(2):
                rank_half(b, 1, half)
            rank_sums(1)
            rank_rest(1)
            numbers_half(0)
            numbers_half(1)
            numbers(3, 8 * NT)
            gate(b, 3, 1)
            D_()
            dve.tensor_copy(S[0:8, 0:P], idx_all[0:8, :]).then_inc(gs_in, 1)
            dve.wait_ge(gs_t, after(gs_t, 1))
            dve.tensor_copy(gateT[:, :], pA[:, 8:16])
            dve.tensor_copy(idxT[:, :], pA[:, 0:8]).then_inc(gs_idx, 1)
            final_norm(NT - 1)
            final_gain(NT - 1)
            for r in range(NS):
                dve.wait_ge(u_in[r % RING], 16 * (4 * 8 * NT + r // RING + 1))
                dve.wait_ge(gs_h, after(gs_h, r + 1))
                dve.tensor_tensor_reduce(u_ring[r % RING], u_ring[r % RING], (pS, pT)[r % 2][:, :], 1.0, 0.0,
                                         ALU.mult, ALU.add, dotsT[:, r:r + 1]).then_inc(u_used, 1)
            gelu_arg(dotsT[:, :], NS).then_inc(gs_in, 1)
            dve.wait_ge(gs_th, after(gs_th, 1))
            gelu_gate(gl[:, 0, NS:2 * NS], dotsT[:, :], gateT[:, :], NS)
            D_()
            dve.tensor_tensor(wz[:, :, :], gl[:, 0, NS:2 * NS].unsqueeze(2).broadcast_to([P, NS, 8]),
                              e8[:, :, :], ALU.mult).then_inc(gs_w, 1)
            final_norm(NT, NS)
            final_gain(NT, NS)


def tables(np):
    pos = np.concatenate([np.arange(NT * P), np.full(P, NT * P)]).astype(np.float32)
    inv = (np.float32(500000.0) ** (-np.arange(0, 16, 2, dtype=np.float32) / np.float32(16))).astype(np.float32)
    ang = (pos[:, None] * inv[None, :]).astype(np.float32)
    rope_cs = np.concatenate([np.cos(ang), np.sin(ang)], axis=1).astype(np.float32)

    def log_count(dist, branches):
        c = sum(((dist >= 0) & (dist <= w) & (dist % d == 0)).astype(np.int64) for w, d in branches)
        return np.where(c > 0, 8 * np.log(np.maximum(c, 1)), -1e30).astype(np.float32)

    dil = ((128, 1), (512, 4), (2048, 16))
    win = ((128, 1),)
    q = np.arange(P)[:, None]
    mask_b = log_count(q + (NT - 1) * P - np.arange((2 * NT - 1) * P)[None, :], dil)
    both = log_count(q + P - np.arange(2 * P)[None, :], win)
    own = np.where(np.arange(2 * P)[None, :] < P, np.float32(-1e30), both)
    mask_a = np.stack([own, both], axis=1).astype(np.float32)
    rows = np.concatenate([np.arange(896, 1024), np.arange(512, 896, 4), np.arange(0, 512, 16)])
    new = np.repeat(np.where(np.eye(NS) > 0, 8 * np.log(3.0), -1e30), HEADS, axis=0)
    mask_sb = np.concatenate([np.repeat(log_count(1024 - rows[None, :], dil), 64, axis=0), new], axis=1)
    new = np.repeat(np.where(np.eye(NS) > 0, 0.0, -1e30), HEADS, axis=0)
    mask_sa = np.concatenate([np.zeros((64, P)), new], axis=1)
    return {
        "ident": np.eye(P, dtype=np.float32), "rope_cs": rope_cs, "mask_b": mask_b, "mask_a": mask_a,
        "mask_sb": mask_sb.astype(np.float32), "mask_sa": mask_sa.astype(np.float32),
        "iota16": np.tile(np.arange(16, dtype=np.float32), (P, 1)),
        "eye8": np.tile(np.eye(8, dtype=np.float32)[None], (P, 1, 1)),
        "eye_tok": np.repeat(np.eye(8, dtype=np.float32), HEADS, axis=0),
        "head_mask": np.tile(np.repeat(np.eye(8, dtype=np.float32), HD, axis=1), (NS, 1)),
    }


_INS = ("x_all", "cache_swa", "cache_dil", "w_in", "sinks", "w_out", "w_q", "keys", "peer_u", "peer_v", "ident",
        "gain_cols", "gain_rows", "final_gain", "rope_cs", "mask_b", "mask_a", "mask_sb", "mask_sa", "iota16", "eye8",
        "eye_tok", "head_mask")
_OUTS = (("y_p", (1024, 1024)), ("y_s", (8, 1024)), ("swa_p", (128, 256)), ("dil_p", (1024, 1024)),
         ("swa_s", (8, 128 * 256)), ("dil_s", (8, 1024, 1024)))


def kernel(x_prompt, x_sample, cache_swa_kv, cache_dil_kv, attn_norm, w_in, sinks, out_norm_a, out_norm_b,
           w_out, ffn_norm, peer_w_q, peer_sub_keys, peer_u, peer_v, final_norm):
    import numpy as np
    import concourse.bacc as bacc
    from concourse.bass_utils import run_bass_kernel_spmd

    def cols(g):
        return np.asarray(g).reshape(KD, P).T

    x_all = np.concatenate([np.asarray(x_prompt).reshape(NT * P, D), np.asarray(x_sample).reshape(NS, D),
                            np.zeros((P - NS, D), np.float32)])
    out_gain = np.concatenate([np.asarray(out_norm_a)[0], np.asarray(out_norm_b)[0]])
    arrays = {
        "x_all": x_all,
        "cache_swa": np.asarray(cache_swa_kv).reshape(NS, 128 * 256),
        "cache_dil": np.asarray(cache_dil_kv).reshape(NS, 1024, 1024),
        "w_in": np.asarray(w_in)[0], "sinks": np.asarray(sinks).reshape(1, HEADS), "w_out": np.asarray(w_out)[0],
        "w_q": np.asarray(peer_w_q)[0], "keys": np.asarray(peer_sub_keys).reshape(2 * HEADS, KEYS, P),
        "peer_u": np.asarray(peer_u)[0], "peer_v": np.asarray(peer_v)[0],
        "gain_cols": np.stack([cols(np.asarray(attn_norm)[0]), cols(out_gain)], axis=1),
        "gain_rows": np.asarray(ffn_norm)[0].reshape(KD, P), "final_gain": np.asarray(final_norm).reshape(1, D),
        **tables(np),
    }
    nc = bacc.Bacc("TRN2", target_bir_lowering=False, num_devices=1)
    feeds, args = {}, []
    for name in _INS:
        a = np.ascontiguousarray(arrays[name])
        feeds[f"in_{name}"] = a
        args.append(nc.dram_tensor(f"in_{name}", a.shape, mybir.dt.from_np(a.dtype), kind="ExternalInput").ap())
    for name, shape in _OUTS:
        args.append(nc.dram_tensor(f"out_{name}", shape, F32, kind="ExternalOutput").ap())
    build(nc, *args)
    r = run_bass_kernel_spmd(nc, [feeds], core_ids=[0]).results[0]
    got = [np.asarray(r[f"out_{name}"]) for name, _ in _OUTS]
    return (got[0].reshape(1, 1024, 1024), got[1].reshape(8, 1, 1024), got[2].reshape(1, 1, 128, 2, 2, 64),
            got[3].reshape(1, 1, 1024, 2, 8, 64), got[4].reshape(1, 8, 128, 2, 2, 64),
            got[5].reshape(1, 8, 1024, 2, 8, 64))
```
